# Optimizing a Trainium2 kernel written in Bass

```python
import jax, jax.numpy as jnp
from jax import lax
import numpy as np
import math

D_MODEL = 1024
BATCH = 1
SEQ = 512
DEPTH = 2

GRID_W = 64
CTX_LEN = 256
HEAD_DIM = 64
ATTN_HEADS = 8
KV_HEADS = 2
Q_PER_KV = ATTN_HEADS // KV_HEADS
ATTN_WIDTH = ATTN_HEADS * HEAD_DIM
KV_WIDTH = KV_HEADS * HEAD_DIM
WINDOW = 128
BLOCK = 128
FOURIER_GROUPS = 4
FOURIER_GROUP_DIM = 64
FOURIER_WIDTH = FOURIER_GROUPS * FOURIER_GROUP_DIM
CONV_GROUPS = 4
CONV_WIDTH = 256
CONV_TAPS = 3
MIX_WIDTH = ATTN_WIDTH + FOURIER_WIDTH + CONV_WIDTH
PROJ_SIZES = (ATTN_WIDTH, KV_WIDTH, KV_WIDTH, ATTN_WIDTH,
              FOURIER_WIDTH, FOURIER_WIDTH,
              CONV_WIDTH, CONV_WIDTH, CONV_WIDTH, CONV_WIDTH)
PROJ_WIDTH = 2 * ATTN_WIDTH + 2 * KV_WIDTH + 2 * FOURIER_WIDTH + 4 * CONV_WIDTH
ROPE_FREQS = HEAD_DIM // 4
ROPE_BASE = 10000.0
NORM_EPS = 1e-6


def rmsnorm(x, g):
    xf = x.astype(jnp.float32)
    y = xf * lax.rsqrt(jnp.mean(xf * xf, axis=-1, keepdims=True) + NORM_EPS)
    return (y * g.astype(jnp.float32)).astype(x.dtype)

def split_cols(p, sizes):
    out = []
    start = 0
    for s in sizes:
        out.append(p[..., start:start + s])
        start += s
    return out

def axial_rope_tables(n):
    rows = n // GRID_W
    row = jnp.repeat(jnp.arange(rows, dtype=jnp.float32), GRID_W)
    col = jnp.tile(jnp.arange(GRID_W, dtype=jnp.float32), rows)
    inv_freq = jnp.power(ROPE_BASE, -jnp.arange(ROPE_FREQS, dtype=jnp.float32) / ROPE_FREQS)
    ang = jnp.concatenate([row[:, None] * inv_freq, col[:, None] * inv_freq], axis=-1)
    return jnp.cos(ang), jnp.sin(ang)

def apply_axial_rope(x, cos, sin):
    b, n, h, d = x.shape
    xr = x.astype(jnp.float32).reshape(b, n, h, 2, 2, ROPE_FREQS)
    x1 = xr[..., 0, :]
    x2 = xr[..., 1, :]
    cs = cos.reshape(n, 1, 2, ROPE_FREQS)
    sn = sin.reshape(n, 1, 2, ROPE_FREQS)
    out = jnp.stack([x1 * cs - x2 * sn, x1 * sn + x2 * cs], axis=-2)
    return out.reshape(b, n, h, d).astype(x.dtype)

def sink_softmax(s, sink_b):
    m = jnp.maximum(jnp.max(s, axis=-1, keepdims=True), sink_b)
    e = jnp.exp(s - m)
    return e / (jnp.sum(e, axis=-1, keepdims=True) + jnp.exp(sink_b - m))

def window_attention(q, k, v, kc, vc, sink_b):
    b, n = q.shape[:2]
    nb = n // BLOCK
    span = BLOCK + 2 * WINDOW
    nc = kc.shape[1]
    qb = (q * (HEAD_DIM ** -0.5)).reshape(b, nb, BLOCK, KV_HEADS, Q_PER_KV, HEAD_DIM).transpose(1, 0, 2, 3, 4, 5)
    pad = ((0, 0), (WINDOW, WINDOW), (0, 0), (0, 0))
    kp = jnp.pad(k, pad)
    vp = jnp.pad(v, pad)
    offs_q = jnp.arange(BLOCK)
    offs_k = jnp.arange(span) - WINDOW

    def one_block(args):
        qi, i = args
        start = i * BLOCK
        ks = lax.dynamic_slice_in_dim(kp, start, span, axis=1)
        vs = lax.dynamic_slice_in_dim(vp, start, span, axis=1)
        qpos = start + offs_q
        kpos = start + offs_k
        valid = (jnp.abs(qpos[:, None] - kpos[None, :]) <= WINDOW) & (kpos >= 0)[None, :] & (kpos < n)[None, :]
        s_loc = jnp.einsum('bqkgd,bnkd->bkgqn', qi, ks).astype(jnp.float32)
        s_loc = jnp.where(valid, s_loc, -jnp.inf)
        s_ctx = jnp.einsum('bqkgd,bnkd->bkgqn', qi, kc).astype(jnp.float32)
        p = sink_softmax(jnp.concatenate([s_ctx, s_loc], axis=-1), sink_b).astype(v.dtype)
        return (jnp.einsum('bkgqn,bnkd->bqkgd', p[..., :nc], vc)
                + jnp.einsum('bkgqn,bnkd->bqkgd', p[..., nc:], vs))

    o = lax.map(one_block, (qb, jnp.arange(nb)))
    return o.transpose(1, 0, 2, 3, 4, 5).reshape(b, n, ATTN_WIDTH)

def context_attention(q, k, v, sink_b):
    b, n = q.shape[:2]
    qg = (q * (HEAD_DIM ** -0.5)).reshape(b, n, KV_HEADS, Q_PER_KV, HEAD_DIM)
    s = jnp.einsum('bqkgd,bnkd->bkgqn', qg, k).astype(jnp.float32)
    p = sink_softmax(s, sink_b).astype(v.dtype)
    return jnp.einsum('bkgqn,bnkd->bqkgd', p, v).reshape(b, n, ATTN_WIDTH)

def fourier_mix(u, w_f):
    b, n, _ = u.shape
    ug = u.reshape(b, n, FOURIER_GROUPS, FOURIER_GROUP_DIM).astype(jnp.float32)
    f = jnp.fft.fft2(ug, axes=(1, 3), norm='ortho').real.astype(u.dtype)
    return jnp.einsum('bngc,gcd->bngd', f, w_f).reshape(b, n, FOURIER_WIDTH)

def short_conv_mix(z, b_gate, c_gate, w, bias):
    t = c_gate * z
    tp = jnp.pad(t, ((0, 0), (1, 1), (0, 0)))
    y = tp[:, :-2] * w[0] + tp[:, 1:-1] * w[1] + tp[:, 2:] * w[2] + bias
    return b_gate * y

def gated_merge(a, ga, f, gf, s, gc, w_out):
    h = jnp.concatenate([a * jax.nn.silu(ga), f * jax.nn.silu(gf), s * jax.nn.silu(gc)], axis=-1)
    return h @ w_out

def layer(x, ctx, c, c_ctx, w_mod, b_mod, g_pre, g_post, w_in, w_out, sink, w_fourier, conv_w, conv_b,
          cos, sin, update_ctx):
    b, n = x.shape[:2]
    nc = ctx.shape[1]
    shift, scale, gate = jnp.split(jax.nn.silu(c) @ w_mod + b_mod, 3, axis=-1)
    shift_c, scale_c, gate_c = jnp.split(jax.nn.silu(c_ctx) @ w_mod + b_mod, 3, axis=-1)
    sink_b = sink.astype(jnp.float32).reshape(1, KV_HEADS, Q_PER_KV, 1, 1)

    hx = rmsnorm(x, g_pre) * (1 + scale[:, None]) + shift[:, None]
    hc = rmsnorm(ctx, g_pre) * (1 + scale_c) + shift_c

    if update_ctx:
        qc, kc, vc, gac, ufc, gfc, zcc, bcc, ccc, gcc = split_cols(hc @ w_in, PROJ_SIZES)
    else:
        kc, vc = split_cols(hc @ w_in[:, ATTN_WIDTH:ATTN_WIDTH + 2 * KV_WIDTH], (KV_WIDTH, KV_WIDTH))
    kc = kc.reshape(b, nc, KV_HEADS, HEAD_DIM)
    vc = vc.reshape(b, nc, KV_HEADS, HEAD_DIM)

    q, k, v, ga, uf, gf, zc, bc, cc, gc = split_cols(hx @ w_in, PROJ_SIZES)
    q = apply_axial_rope(q.reshape(b, n, ATTN_HEADS, HEAD_DIM), cos, sin)
    k = apply_axial_rope(k.reshape(b, n, KV_HEADS, HEAD_DIM), cos, sin)
    v = v.reshape(b, n, KV_HEADS, HEAD_DIM)
    a = window_attention(q, k, v, kc, vc, sink_b)
    f = fourier_mix(uf, w_fourier)
    s = short_conv_mix(zc, bc, cc, conv_w, conv_b)
    y = gated_merge(a, ga, f, gf, s, gc, w_out)
    x_new = x + gate[:, None] * rmsnorm(y, g_post)

    if update_ctx:
        ac = context_attention(qc.reshape(b, nc, ATTN_HEADS, HEAD_DIM), kc, vc, sink_b)
        fc = fourier_mix(ufc, w_fourier)
        sc = short_conv_mix(zcc, bcc, ccc, conv_w, conv_b)
        yc = gated_merge(ac, gac, fc, gfc, sc, gcc, w_out)
        ctx = ctx + gate_c * rmsnorm(yc, g_post)
    return x_new, ctx

def first_inputs(seed: int = 0) -> dict:
    key = jax.random.key(seed)
    ks = jax.random.split(key, 14)
    nrm = jax.random.normal
    x = nrm(ks[0], (BATCH, SEQ, D_MODEL), jnp.float32)
    c = nrm(ks[1], (BATCH, D_MODEL), jnp.float32)
    ctx = nrm(ks[2], (BATCH, CTX_LEN, D_MODEL), jnp.float32)
    c_ctx = nrm(ks[3], (D_MODEL,), jnp.float32)
    w_mod = nrm(ks[4], (DEPTH, D_MODEL, 3 * D_MODEL), jnp.float32) * (0.5 * D_MODEL ** -0.5)
    b_mod = 0.01 * nrm(ks[5], (DEPTH, 3 * D_MODEL), jnp.float32)
    g_pre = 1.0 + 0.05 * nrm(ks[6], (DEPTH, D_MODEL), jnp.float32)
    g_post = 1.0 + 0.05 * nrm(ks[7], (DEPTH, D_MODEL), jnp.float32)
    w_in = nrm(ks[8], (DEPTH, D_MODEL, PROJ_WIDTH), jnp.float32) * (D_MODEL ** -0.5)
    w_out = nrm(ks[9], (DEPTH, MIX_WIDTH, D_MODEL), jnp.float32) * (MIX_WIDTH ** -0.5)
    sink = 0.5 * nrm(ks[10], (DEPTH, ATTN_HEADS), jnp.float32)
    w_fourier = nrm(ks[11], (DEPTH, FOURIER_GROUPS, FOURIER_GROUP_DIM, FOURIER_GROUP_DIM), jnp.float32) * (FOURIER_GROUP_DIM ** -0.5)
    conv_w = nrm(ks[12], (DEPTH, CONV_TAPS, CONV_WIDTH), jnp.float32) * (CONV_TAPS ** -0.5)
    conv_b = 0.01 * nrm(ks[13], (DEPTH, CONV_WIDTH), jnp.float32)
    return {'x': x, 'c': c, 'ctx': ctx, 'c_ctx': c_ctx, 'w_mod': w_mod, 'b_mod': b_mod,
            'g_pre': g_pre, 'g_post': g_post, 'w_in': w_in, 'w_out': w_out, 'sink': sink,
            'w_fourier': w_fourier, 'conv_w': conv_w, 'conv_b': conv_b}

def first_block(x, c, ctx, c_ctx, w_mod, b_mod, g_pre, g_post, w_in, w_out, sink, w_fourier, conv_w, conv_b):
    cos, sin = axial_rope_tables(x.shape[1])
    for l in range(DEPTH):
        x, ctx = layer(x, ctx, c, c_ctx, w_mod[l], b_mod[l], g_pre[l], g_post[l], w_in[l], w_out[l],
                       sink[l], w_fourier[l], conv_w[l], conv_b[l], cos, sin, l < DEPTH - 1)
    return x


A_HEADS = 6
A_PAIRS = ((128, 1), (512, 4), (2048, 16))
B_HEADS = 4
B_QK_DIM = 32
B_V_DIM = 2 * B_QK_DIM
C_HEADS = 6
C_Q_LORA = 256
C_KV_LORA = 128
C_NOPE = 64
C_ROPE = 32
C_V = 64
ROPE_THETA = 10000.0
MIX_WIDTH_2 = (A_HEADS + B_HEADS + C_HEADS) * HEAD_DIM
A_COLS = 3 * A_HEADS * HEAD_DIM
B_COLS = B_HEADS * (2 * 2 * B_QK_DIM + B_V_DIM)
C_COLS = C_Q_LORA + C_KV_LORA + C_ROPE
IN_COLS = A_COLS + B_COLS + C_COLS
NUM_BUCKETS = 32
MAX_DISTANCE = 2048
BIAS_HEADS = A_HEADS + B_HEADS
FF_DIM = -(-8 * D_MODEL // (3 * 256)) * 256
Q_BLOCK = 128
DEEPNORM_ALPHA = (2 * DEPTH) ** 0.25
DEEPNORM_BETA = (8 * DEPTH) ** -0.25
LN_EPS = 1e-5
LATENT_EPS = 1e-6
SUBLN_EPS = 1e-5


def layer_norm(x, g, b):
    xf = x.astype(jnp.float32)
    mu = jnp.mean(xf, axis=-1, keepdims=True)
    var = jnp.mean(jnp.square(xf - mu), axis=-1, keepdims=True)
    return ((xf - mu) * lax.rsqrt(var + LN_EPS) * g + b).astype(x.dtype)

def rms_norm(x, g, eps):
    xf = x.astype(jnp.float32)
    return (xf * lax.rsqrt(jnp.mean(xf * xf, axis=-1, keepdims=True) + eps) * g).astype(x.dtype)

def t5_bucket(dist):
    max_exact = NUM_BUCKETS // 2
    d = jnp.maximum(dist, 0)
    df = jnp.maximum(d, 1).astype(jnp.float32)
    large = max_exact + (jnp.log(df / max_exact) / math.log(MAX_DISTANCE / max_exact)
                         * (NUM_BUCKETS - max_exact)).astype(jnp.int32)
    large = jnp.minimum(large, NUM_BUCKETS - 1)
    return jnp.where(d < max_exact, d, large)

def apply_rope(x):
    S, half = x.shape[1], x.shape[-1] // 2
    inv = ROPE_THETA ** (-jnp.arange(half, dtype=jnp.float32) / half)
    ang = jnp.arange(S, dtype=jnp.float32)[:, None] * inv[None, :]
    cos, sin = jnp.cos(ang)[None, :, None, :], jnp.sin(ang)[None, :, None, :]
    xf = x.astype(jnp.float32)
    x1, x2 = xf[..., :half], xf[..., half:]
    return jnp.concatenate([x1 * cos - x2 * sin, x2 * cos + x1 * sin], axis=-1).astype(x.dtype)

def dilated_pair(q, k, v, bias_tab, window, dil):
    Bn, S, H, Dh = q.shape
    blk = window // dil
    L = S // dil
    nb = -(-L // blk)
    pad = nb * blk - L

    def to_blocks(a):
        a = a.reshape(Bn, L, dil, H, Dh)
        a = jnp.pad(a, ((0, 0), (0, pad), (0, 0), (0, 0), (0, 0)))
        return a.reshape(Bn, nb, blk, dil, H, Dh)

    def with_prev(a):
        prev = jnp.pad(a, ((0, 0), (1, 0), (0, 0), (0, 0), (0, 0), (0, 0)))[:, :nb]
        return jnp.concatenate([prev, a], axis=2)

    qb = to_blocks(q)
    kb = with_prev(to_blocks(k))
    vb = with_prev(to_blocks(v))
    rel = jnp.arange(blk)[:, None] + blk - jnp.arange(2 * blk)[None, :]
    band = (rel >= 0) & (rel <= blk)
    not_first = (jnp.arange(nb)[:, None, None] > 0) | (jnp.arange(2 * blk)[None, None, :] >= blk)
    mask = band[None] & not_first
    bias = bias_tab[t5_bucket(rel * dil)].astype(jnp.float32).transpose(2, 0, 1)
    s = jnp.einsum('bnqrhd,bnkrhd->bnrhqk', qb, kb).astype(jnp.float32) * (Dh ** -0.5) + bias
    s = jnp.where(mask[None, :, None, None], s, -jnp.inf)
    lse = jax.nn.logsumexp(s, axis=-1)
    p = jnp.exp(s - lse[..., None]).astype(v.dtype)
    o = jnp.einsum('bnrhqk,bnkrhd->bnqrhd', p, vb)
    o = o.reshape(Bn, nb * blk, dil, H, Dh)[:, :L].reshape(Bn, S, H, Dh)
    lse = lse.transpose(0, 1, 4, 2, 3).reshape(Bn, nb * blk, dil, H)[:, :L].reshape(Bn, S, H)
    return o, lse

def dilated_mixture(q, k, v, bias_tab):
    outs, lses = [], []
    for window, dil in A_PAIRS:
        o, lse = dilated_pair(q, k, v, bias_tab, window, dil)
        outs.append(o)
        lses.append(lse)
    w = jax.nn.softmax(jnp.stack(lses, axis=0), axis=0)
    o = jnp.sum(w[..., None] * jnp.stack(outs, axis=0).astype(jnp.float32), axis=0)
    return o.astype(q.dtype)

def sweep_query_blocks(block_fn, n_pos):
    o = lax.map(block_fn, jnp.arange(n_pos // Q_BLOCK))
    o = jnp.moveaxis(o, 0, 1)
    return o.reshape((o.shape[0], n_pos) + o.shape[3:])

def diff_attention(q1, q2, k1, k2, v, lam, bias_tab):
    S = q1.shape[1]
    scale = q1.shape[-1] ** -0.5
    kpos = jnp.arange(S)

    def block(i):
        start = i * Q_BLOCK
        sl = lambda a: lax.dynamic_slice_in_dim(a, start, Q_BLOCK, axis=1)
        rel = (start + jnp.arange(Q_BLOCK))[:, None] - kpos[None, :]
        causal = rel >= 0
        bias = bias_tab[t5_bucket(rel)].astype(jnp.float32).transpose(2, 0, 1)

        def probs(q, k):
            s = jnp.einsum('bqhd,bkhd->bhqk', sl(q), k).astype(jnp.float32) * scale + bias
            return jax.nn.softmax(jnp.where(causal, s, -jnp.inf), axis=-1)

        a = probs(q1, k1) - lam * probs(q2, k2)
        return jnp.einsum('bhqk,bkhd->bqhd', a.astype(v.dtype), v)

    return sweep_query_blocks(block, S)

def causal_attention(q, k, v):
    S = q.shape[1]
    scale = q.shape[-1] ** -0.5
    kpos = jnp.arange(S)

    def block(i):
        start = i * Q_BLOCK
        qs = lax.dynamic_slice_in_dim(q, start, Q_BLOCK, axis=1)
        causal = (start + jnp.arange(Q_BLOCK))[:, None] >= kpos[None, :]
        s = jnp.einsum('bqhd,bkhd->bhqk', qs, k).astype(jnp.float32) * scale
        p = jax.nn.softmax(jnp.where(causal, s, -jnp.inf), axis=-1)
        return jnp.einsum('bhqk,bkhd->bqhd', p.astype(v.dtype), v)

    return sweep_query_blocks(block, S)

def hybrid_layer(x, layer_idx, rel_bias, w_in, q_norm_g, kv_norm_g, w_uq, w_ukv,
                 diff_lambda, subln_g, w_o, ln1_g, ln1_b, ln2_g, ln2_b, w_gate, w_up, w_down):
    Bn, S, _ = x.shape
    proj = x @ w_in
    a_in, b_in, c_in = jnp.split(proj, [A_COLS, A_COLS + B_COLS], axis=-1)

    a = a_in.reshape(Bn, S, 3, A_HEADS, HEAD_DIM)
    o_a = dilated_mixture(a[:, :, 0], a[:, :, 1], a[:, :, 2], rel_bias[:, :A_HEADS])

    qk_cols = B_HEADS * 2 * B_QK_DIM
    bq = b_in[..., :qk_cols].reshape(Bn, S, B_HEADS, 2, B_QK_DIM)
    bk = b_in[..., qk_cols:2 * qk_cols].reshape(Bn, S, B_HEADS, 2, B_QK_DIM)
    bv = b_in[..., 2 * qk_cols:].reshape(Bn, S, B_HEADS, B_V_DIM)
    lam_init = 0.8 - 0.6 * math.exp(-0.3 * layer_idx)
    lf = diff_lambda.astype(jnp.float32)
    lam = jnp.exp(jnp.sum(lf[0] * lf[1])) - jnp.exp(jnp.sum(lf[2] * lf[3])) + lam_init
    o_b = diff_attention(bq[..., 0, :], bq[..., 1, :], bk[..., 0, :], bk[..., 1, :], bv, lam,
                         rel_bias[:, A_HEADS:])
    o_b = (rms_norm(o_b, subln_g, SUBLN_EPS) * (1.0 - lam_init)).astype(x.dtype)

    c_q, c_kv, k_r = jnp.split(c_in, [C_Q_LORA, C_Q_LORA + C_KV_LORA], axis=-1)
    q = (rms_norm(c_q, q_norm_g, LATENT_EPS) @ w_uq).reshape(Bn, S, C_HEADS, C_NOPE + C_ROPE)
    kv = (rms_norm(c_kv, kv_norm_g, LATENT_EPS) @ w_ukv).reshape(Bn, S, C_HEADS, C_NOPE + C_V)
    q_c = jnp.concatenate([q[..., :C_NOPE], apply_rope(q[..., C_NOPE:])], axis=-1)
    k_rope = apply_rope(k_r[:, :, None, :])
    k_c = jnp.concatenate([kv[..., :C_NOPE],
                           jnp.broadcast_to(k_rope, (Bn, S, C_HEADS, C_ROPE))], axis=-1)
    o_c = causal_attention(q_c, k_c, kv[..., C_NOPE:])

    heads = jnp.concatenate([o_a.reshape(Bn, S, -1), o_b.reshape(Bn, S, -1),
                             o_c.reshape(Bn, S, -1)], axis=-1)
    h = layer_norm(DEEPNORM_ALPHA * x + heads @ w_o, ln1_g, ln1_b)

    ffn = (jax.nn.silu(h @ w_gate) * (h @ w_up)) @ w_down
    return layer_norm(DEEPNORM_ALPHA * h + ffn, ln2_g, ln2_b)

def second_inputs(seed: int = 0) -> dict:
    key = jax.random.key(seed)
    ks = jax.random.split(key, 20)
    f32 = jnp.float32
    nrm = lambda k, shape, scale: jax.random.normal(k, shape, f32) * scale
    return {
        "x": nrm(ks[0], (BATCH, SEQ, D_MODEL), 1.0),
        "rel_bias": nrm(ks[1], (NUM_BUCKETS, BIAS_HEADS), 0.5),
        "w_in": nrm(ks[2], (DEPTH, D_MODEL, IN_COLS), D_MODEL ** -0.5),
        "q_norm_g": 1.0 + nrm(ks[3], (DEPTH, C_Q_LORA), 0.05),
        "kv_norm_g": 1.0 + nrm(ks[4], (DEPTH, C_KV_LORA), 0.05),
        "w_uq": nrm(ks[5], (DEPTH, C_Q_LORA, C_HEADS * (C_NOPE + C_ROPE)), C_Q_LORA ** -0.5),
        "w_ukv": nrm(ks[6], (DEPTH, C_KV_LORA, C_HEADS * (C_NOPE + C_V)), C_KV_LORA ** -0.5),
        "diff_lambda": nrm(ks[7], (DEPTH, 4, B_QK_DIM), 0.1),
        "subln_g": 1.0 + nrm(ks[8], (DEPTH, B_V_DIM), 0.05),
        "w_o": nrm(ks[9], (DEPTH, MIX_WIDTH_2, D_MODEL), MIX_WIDTH_2 ** -0.5 * DEEPNORM_BETA),
        "ln1_g": 1.0 + nrm(ks[10], (DEPTH, D_MODEL), 0.05),
        "ln1_b": nrm(ks[11], (DEPTH, D_MODEL), 0.02),
        "ln2_g": 1.0 + nrm(ks[12], (DEPTH, D_MODEL), 0.05),
        "ln2_b": nrm(ks[13], (DEPTH, D_MODEL), 0.02),
        "w_gate": nrm(ks[14], (DEPTH, D_MODEL, FF_DIM), D_MODEL ** -0.5),
        "w_up": nrm(ks[15], (DEPTH, D_MODEL, FF_DIM), D_MODEL ** -0.5),
        "w_down": nrm(ks[16], (DEPTH, FF_DIM, D_MODEL), FF_DIM ** -0.5 * DEEPNORM_BETA),
    }

def second_block(x, rel_bias, w_in, q_norm_g, kv_norm_g, w_uq, w_ukv, diff_lambda, subln_g, w_o,
              ln1_g, ln1_b, ln2_g, ln2_b, w_gate, w_up, w_down):
    for l in range(DEPTH):
        x = hybrid_layer(x, l, rel_bias, w_in[l], q_norm_g[l], kv_norm_g[l], w_uq[l], w_ukv[l],
                         diff_lambda[l], subln_g[l], w_o[l], ln1_g[l], ln1_b[l], ln2_g[l], ln2_b[l],
                         w_gate[l], w_up[l], w_down[l])
    return x


def setup_inputs(seed=0):
    out = dict(first_inputs(seed))
    for name, value in second_inputs(seed + 1).items():
        if name != "x":
            out[name + "_2"] = value
    return out


def reference(
    x, c, ctx, c_ctx, w_mod, b_mod, g_pre, g_post, w_in, w_out, sink, w_fourier, conv_w, conv_b,
    rel_bias_2, w_in_2, q_norm_g_2, kv_norm_g_2, w_uq_2, w_ukv_2, diff_lambda_2, subln_g_2,
    w_o_2, ln1_g_2, ln1_b_2, ln2_g_2, ln2_b_2, w_gate_2, w_up_2, w_down_2,
):
    x = first_block(
        x, c, ctx, c_ctx, w_mod, b_mod, g_pre, g_post, w_in, w_out, sink, w_fourier, conv_w,
        conv_b,
    )
    return second_block(
        x, rel_bias_2, w_in_2, q_norm_g_2, kv_norm_g_2, w_uq_2, w_ukv_2, diff_lambda_2,
        subln_g_2, w_o_2, ln1_g_2, ln1_b_2, ln2_g_2, ln2_b_2, w_gate_2, w_up_2, w_down_2,
    )


_drawn_inputs = setup_inputs


def setup_inputs(seed=0):
    import zlib

    import numpy as np

    out = dict(_drawn_inputs(seed))
    spreads = {}
    factors = {'b_mod': 2.918,
     'sink': 8.0,
     'conv_b': 8.0,
     'q_norm_g_2': 8.0,
     'kv_norm_g_2': 8.0,
     'diff_lambda_2': 7.142,
     'subln_g_2': 6.466}
    for name, (base, spread) in spreads.items():
        noise = np.random.default_rng([zlib.crc32(name.encode()), seed]).standard_normal(out[name].shape)
        drawn = base * np.exp(spread * noise) if base else spread * noise
        out[name] = __import__('jax').numpy.asarray(drawn.astype(out[name].dtype))
    for name, factor in factors.items():
        out[name] = (out[name] * factor).astype(out[name].dtype)
    return out
```

```python
from contextlib import ExitStack

import numpy as np

import concourse.bass as bass
from concourse import mybir

F32 = mybir.dt.float32
F32R = mybir.dt.float32r
ALU = mybir.AluOpType
ACT = mybir.ActivationFunctionType
AX_X = mybir.AxisListType.X

P = 128
D = 1024
KD = D // P
SEQ, CTX, DEPTH = 512, 256, 2
XT, CT = SEQ // P, CTX // P
TOK = SEQ + CTX
NT = XT + CT
HD = 64
EPS = 1e-6
HEADS, KVH = 8, 2
FF = 2816
FC = FF // P
A_HEADS, B_HEADS, C_HEADS = 6, 4, 6
BUCKETS = 32
ALPHA = (2 * DEPTH) ** 0.25
LN_EPS = 1e-5
NEG = -1.0e30
RAW, SPLIT = 3, 2
TILE = 2048
ROPE = 32
QC = HD + ROPE


class Signal:

    def __init__(self, nc, ctx, seen, name):
        self.sem = ctx.enter_context(nc.semaphore(name))
        self.seen = seen.setdefault(name, {})
        self.count = 0

    def nth(self, key, by=1):
        self.count += by
        self.seen[key] = self.count
        return by

    def name_latest(self, key):
        self.seen[key] = self.count

    def at(self, key):
        return self.seen.get(key, 1)

    def after(self, key):
        return self.sem, self.at(key)


def _constants():
    f = np.float32
    c = {}
    c["ident"] = np.eye(P, dtype=f)
    pos = np.arange(SEQ)
    inv = np.power(f(10000.0), -np.arange(16, dtype=f) / f(16)).astype(f)
    ang = np.stack([(pos // 64).astype(f)[:, None] * inv, (pos % 64).astype(f)[:, None] * inv], 1)
    rows = np.arange(P)
    axis, freq = (rows % 64) // 32, rows % 16
    c["cos1"] = np.ascontiguousarray(np.cos(ang)[:, axis, freq].T.astype(f))
    c["sin1"] = np.ascontiguousarray(np.sin(ang)[:, axis, freq].T.astype(f))

    def rotation(n, half):
        r = np.zeros((n, n), f)
        for i in range(n):
            first = (i % (2 * half)) < half
            r[i + half if first else i - half, i] = -1.0 if first else 1.0
        return r

    c["rot1"] = rotation(P, 16)
    inv2 = np.power(f(10000.0), -np.arange(16, dtype=f) / f(16)).astype(f)
    ang2 = pos.astype(f)[:, None] * inv2
    c["cos2"] = np.ascontiguousarray(np.tile(np.cos(ang2).T, (2, 1)).astype(f))
    c["sin2"] = np.ascontiguousarray(np.tile(np.sin(ang2).T, (2, 1)).astype(f))
    rot2 = np.zeros((ROPE, QC), f)
    rot2[:, HD:] = rotation(ROPE, 16)
    c["rot2"] = rot2
    q, k = np.arange(P)[:, None], np.arange(3 * P)[None, :] - P
    band = np.where(np.abs(q - k) <= P, 0.0, NEG).astype(f)
    c["band_mid"] = np.concatenate([band, np.zeros((P, CTX), f)], 1)
    c["band_last"] = np.concatenate([band[:, :2 * P], np.zeros((P, CTX), f)], 1)
    for n in (SEQ, CTX):
        t = np.outer(np.arange(n), np.arange(n)) % n * (2 * np.pi / n)
        c[f"dft_cos{n}"] = (np.cos(t) / np.sqrt(n)).astype(f)
        c[f"dft_sin{n}"] = (np.sin(t) / np.sqrt(n)).astype(f)
    t = np.outer(np.arange(HD), np.arange(HD)) % HD * (2 * np.pi / HD)
    two = np.eye(2)
    c["dft_ccos"] = np.kron(two, np.cos(t) / 8.0).astype(f)
    c["dft_csin"] = np.kron(two, -np.sin(t) / 8.0).astype(f)
    dist = SEQ - 1 - np.arange(SEQ + P)
    df = np.maximum(dist, 1).astype(f)
    large = 16 + (np.log(df / f(16)) / f(np.log(2048 / 16)) * f(16)).astype(np.int32)
    bucket = np.where(dist < 16, np.maximum(dist, 0), np.minimum(large, BUCKETS - 1))
    hot = np.zeros((BUCKETS + 2, SEQ + P), f)
    hot[bucket, np.arange(SEQ + P)] = (dist >= 0)
    times = (dist <= P).astype(int) + (dist % 4 == 0) + (dist % 16 == 0)
    ok = dist >= 0
    hot[BUCKETS] = np.where(ok & (times > 0), np.log(np.maximum(times, 1)), NEG)
    hot[BUCKETS + 1] = np.where(ok, 0.0, NEG)
    c["hot"] = hot
    pick = np.zeros((2, A_HEADS + B_HEADS), f)
    pick[0, :A_HEADS] = 1.0
    pick[1, A_HEADS:] = 1.0
    c["pick"] = pick
    d2 = 384 + np.arange(P)[:, None] - np.arange(SEQ)[None, :]
    c["causal"] = np.where(d2 >= 0, 0.0, NEG).astype(f)
    init = [0.8 - 0.6 * np.exp(-0.3 * l) for l in range(DEPTH)]
    c["lam_init"] = np.array([[-i, 1.0 - i] for i in init], f)
    return c


def _program(nc, I, out, seen):
    ctx = ExitStack()
    with ctx:
        base = -(-nc.sbuf_base // 64) * 64
        names = {}

        def at(name, shape, off, dt=F32):
            n = 4 * int(np.prod(shape[1:]))
            assert base + off + n <= nc.sbuf_usable_end, (name, off, n)
            names[name] = (off, n)
            return nc.alloc_sbuf_tensor_at(name, shape, dt, offset=base + off)

        off = 0

        def put(name, shape, dt=F32):
            nonlocal off
            t = at(name, shape, off, dt)
            off += -(-4 * int(np.prod(shape[1:])) // 32) * 32
            return t

        raw = put("raw", [P, RAW, TILE])
        w_hi = put("w_hi", [P, SPLIT, TILE], F32R)
        w_lo = put("w_lo", [P, SPLIT, TILE], F32R)
        ident = put("ident", [P, P])
        ones = put("ones", [P, P])
        rot1 = put("rot1", [P, P])
        rot2 = put("rot2", [P, QC])
        vec = put("vec", [P, P])
        vec_t = put("vec_t", [P, P])
        cond = put("cond", [P, KD, 2])
        mod = put("mod", [P, 2, 24])
        mod_a = put("mod_a", [P, 2, KD])
        mod_g = put("mod_g", [P, 2, KD])
        ssq = put("ssq", [P, 16])
        rstd = put("rstd", [P, 16])
        mean_var = put("mean_var", [P, XT, 2])
        bn = put("bn", [P, XT, 2, 6])
        small = put("small", [P, 5, 4])
        sinks = put("sinks", [P, DEPTH * HEADS])
        lam_c = put("lam_c", [P, 2])
        lam = put("lam", [P, 8])
        table = put("table", [BUCKETS + 2, A_HEADS + B_HEADS])
        res = put("res", [P, XT, D])
        res_c_at = off
        res_c = put("res_c", [P, CT, D])
        ph = off
        h_hi = put("h_hi", [P, KD, TOK], F32R)
        h_lo = put("h_lo", [P, KD, TOK], F32R)
        mix_at = off
        q1 = put("q1", [P, 4, TOK])
        k1 = put("k1", [P, TOK])
        ga = put("ga", [P, 4, TOK])
        gf = put("gf", [P, 2, TOK])
        cz = put("cz", [P, 2, TOK])
        cb = put("cb", [P, 2, TOK])
        v1 = put("v1", [P, NT, P])
        uf_at = off
        uf_hi = put("uf_hi", [P, NT, 256], F32R)
        uf_lo = put("uf_lo", [P, NT, 256], F32R)
        cos1 = put("cos1", [P, SEQ])
        sin1 = put("sin1", [P, SEQ])
        band_mid = put("band_mid", [P, 5 * P])
        band_last = put("band_last", [P, 4 * P])
        dft_ccos = put("dft_ccos", [P, P])
        dft_csin = put("dft_csin", [P, P])
        wf = put("wf", [P, DEPTH, 2, P])
        wf_m = put("wf_m", [P, 2, 2, P])
        xn = at("xn", [P, NT, D], mix_at)
        tmp_n = at("tmp_n", [P, 2, TOK], names["cz"][0])
        tmp_p = at("tmp_p", [P, 2, TOK], names["ga"][0])
        four = at("four", [P, 2, 2, TOK], names["h_lo"][0])
        conv_y = at("conv_y", [P, 2, TOK], names["h_lo"][0] + 4 * 4 * TOK)
        sc = at("sc", [P, 2, 5 * P], names["h_hi"][0])
        pr = at("pr", [P, 2, 5 * P], names["h_hi"][0] + 8 * 5 * P)
        pt = at("pt", [P, 2, 5 * P], names["h_hi"][0] + 16 * 5 * P)
        ao1 = at("ao1", [P, NT, 512], uf_at)
        tmp_m = at("tmp_m", [P, 2, 512], names["q1"][0])
        y1 = at("y1", [P, NT, D], mix_at)
        gate_b = at("gate_b", [P, 2, D], names["gf"][0])
        diag = at("diag", [P, 2, KD, P], names["gf"][0] + 8 * D)
        assert names["ga"][0] + names["ga"][1] - mix_at >= 4 * NT * D
        assert names["cb"][0] + names["cb"][1] - names["gf"][0] >= 16 * D
        off = res_c_at
        g_hi = put("g_hi", [P, KD, SEQ], F32R)
        g_lo = put("g_lo", [P, KD, SEQ], F32R)
        ao2 = put("ao2", [P, XT, D])
        att_at = off
        qa = put("qa", [P, 3, SEQ])
        ka = put("ka", [P, 3, SEQ])
        va = put("va", [P, XT, 384])
        qb = put("qb", [P, 2, SEQ])
        kb = put("kb", [P, 2, SEQ])
        vb = put("vb", [P, XT, 256])
        qc = put("qc", [P, C_HEADS, SEQ])
        kc = put("kc", [P, C_HEADS, SEQ])
        vc = put("vc", [P, XT, 384])
        strip_at = off
        strips = put("strips", [P, 11, SEQ])
        off = strip_at
        c_in = put("c_in", [P, XT, 416])
        cq_hi = put("cq_hi", [P, 2, SEQ], F32R)
        cq_lo = put("cq_lo", [P, 2, SEQ], F32R)
        ckv_hi = put("ckv_hi", [P, SEQ], F32R)
        ckv_lo = put("ckv_lo", [P, SEQ], F32R)
        cos2 = put("cos2", [P, SEQ])
        sin2 = put("sin2", [P, SEQ])
        subln = put("subln", [P, HD])
        dlam = put("dlam", [P, 4 * 32])
        tmp_c = at("tmp_c", [P, 2, SEQ], names["ao2"][0])
        sc2 = at("sc2", [P, 2, SEQ], names["g_hi"][0])
        pr2 = at("pr2", [P, 2, SEQ], names["g_hi"][0] + 8 * SEQ)
        pt2 = at("pt2", [P, 2, SEQ], names["g_hi"][0] + 16 * SEQ)
        sq_b = at("sq_b", [P, 16, HD], names["g_lo"][0])
        ln1 = at("ln1", [P, 2, D], att_at)
        ln2 = at("ln2", [P, 2, D], names["g_lo"][0])
        off = names["ao2"][0] + 4 * 4 * SEQ
        hid_hi = put("hid_hi", [P, FC, SEQ], F32R)
        hid_lo = put("hid_lo", [P, FC, SEQ], F32R)
        tmp_f = at("tmp_f", [P, 4, SEQ], names["ao2"][0])
        rr = at("rr", [A_HEADS + B_HEADS, SEQ + P], uf_at)
        hot = at("hot", [BUCKETS + 2, SEQ + P], uf_at + 4 * (SEQ + P))
        junk = at("junk", [P, D], uf_at)

        ps = ctx.enter_context(nc.psum_tensor("ps", [P, 8, 512], F32))
        ps_flat = ps[:].rearrange("p b n -> p (b n)")
        scratch = nc.dram_tensor("bias_rows", [A_HEADS + B_HEADS, P * (SEQ + P)], F32).ap()

        s_aot = Signal(nc, ctx, seen, "aot")
        s_bias_rows = Signal(nc, ctx, seen, "bias_rows")
        s_cond = Signal(nc, ctx, seen, "cond")
        s_consts = Signal(nc, ctx, seen, "consts")
        s_conv_gate = Signal(nc, ctx, seen, "conv_gate")
        s_conv_t = Signal(nc, ctx, seen, "conv_t")
        s_diag = Signal(nc, ctx, seen, "diag")
        s_dve_step = Signal(nc, ctx, seen, "dve_step")
        s_fmix = Signal(nc, ctx, seen, "fmix")
        s_four_out = Signal(nc, ctx, seen, "four_out")
        s_gate_b = Signal(nc, ctx, seen, "gate_b")
        s_gate_mm = Signal(nc, ctx, seen, "gate_mm")
        s_gated = Signal(nc, ctx, seen, "gated")
        s_glu = Signal(nc, ctx, seen, "glu")
        s_hi = Signal(nc, ctx, seen, "hi")
        s_ht = Signal(nc, ctx, seen, "ht")
        s_kr_all = Signal(nc, ctx, seen, "kr_all")
        s_kr_raw = Signal(nc, ctx, seen, "kr_raw")
        s_kr_rot = Signal(nc, ctx, seen, "kr_rot")
        s_lam_exp = Signal(nc, ctx, seen, "lam_exp")
        s_lam_sums = Signal(nc, ctx, seen, "lam_sums")
        s_lat = Signal(nc, ctx, seen, "lat")
        s_lat_t = Signal(nc, ctx, seen, "lat_t")
        s_latn = Signal(nc, ctx, seen, "latn")
        s_layer_consts = Signal(nc, ctx, seen, "layer_consts")
        s_ln = Signal(nc, ctx, seen, "ln")
        s_lo = Signal(nc, ctx, seen, "lo")
        s_mixed = Signal(nc, ctx, seen, "mixed")
        s_mm = Signal(nc, ctx, seen, "mm")
        s_mod = Signal(nc, ctx, seen, "mod")
        s_mod_out = Signal(nc, ctx, seen, "mod_out")
        s_mod_x = Signal(nc, ctx, seen, "mod_x")
        s_negm = Signal(nc, ctx, seen, "negm")
        s_normed = Signal(nc, ctx, seen, "normed")
        s_nt = Signal(nc, ctx, seen, "nt")
        s_o_out = Signal(nc, ctx, seen, "o_out")
        s_ones = Signal(nc, ctx, seen, "ones")
        s_probs = Signal(nc, ctx, seen, "probs")
        s_proj = Signal(nc, ctx, seen, "proj")
        s_pt_act = Signal(nc, ctx, seen, "pt_act")
        s_pt_dve = Signal(nc, ctx, seen, "pt_dve")
        s_q_rot = Signal(nc, ctx, seen, "q_rot")
        s_resid = Signal(nc, ctx, seen, "resid")
        s_root = Signal(nc, ctx, seen, "root")
        s_roped = Signal(nc, ctx, seen, "roped")
        s_rot = Signal(nc, ctx, seen, "rot")
        s_rr = Signal(nc, ctx, seen, "rr")
        s_rr_mm = Signal(nc, ctx, seen, "rr_mm")
        s_scores = Signal(nc, ctx, seen, "scores")
        s_side = Signal(nc, ctx, seen, "side")
        s_silu = Signal(nc, ctx, seen, "silu")
        s_sink_exp = Signal(nc, ctx, seen, "sink_exp")
        s_ssq = Signal(nc, ctx, seen, "ssq")
        s_stored = Signal(nc, ctx, seen, "stored")
        s_strips = Signal(nc, ctx, seen, "strips")
        s_sub = Signal(nc, ctx, seen, "sub")
        s_tile_hi = Signal(nc, ctx, seen, "tile_hi")
        s_tile_lo = Signal(nc, ctx, seen, "tile_lo")
        s_turned = Signal(nc, ctx, seen, "turned")
        s_uf_hi = Signal(nc, ctx, seen, "uf_hi")
        s_uf_lo = Signal(nc, ctx, seen, "uf_lo")
        s_var = Signal(nc, ctx, seen, "var")
        s_vec_mm = Signal(nc, ctx, seen, "vec_mm")
        s_vec_t = Signal(nc, ctx, seen, "vec_t")
        s_wf_landed = Signal(nc, ctx, seen, "wf_landed")
        s_wf_m = Signal(nc, ctx, seen, "wf_m")
        s_wf_mm = Signal(nc, ctx, seen, "wf_mm")
        s_wf_zero = Signal(nc, ctx, seen, "wf_zero")
        s_x_final = Signal(nc, ctx, seen, "x_final")
        s_x_landed = Signal(nc, ctx, seen, "x_landed")
        s_xn = Signal(nc, ctx, seen, "xn")
        s_xt = Signal(nc, ctx, seen, "xt")
        s_y = Signal(nc, ctx, seen, "y")

        def cols(w, a, b):
            return w[:, a:b].rearrange("(k p) c -> p k c", p=P)

        def mod_tile(l, j):
            return ((l, "mod", j), [(lambda r: r.rearrange("p (k c) -> p k c", k=KD),
                                     cols(I["w_mod"][l], 256 * j, 256 * j + 256))], False)

        def mix_tiles(l):
            t = []

            def proj(what, parts):
                t.append(((l, *what), [(lambda r, o=o, n=n: r.rearrange("p (k c) -> p k c", k=KD)[:, :, o:o + n],
                                        cols(I["w_in"][l], a, a + n)) for o, a, n in parts], True))

            for j in range(2):
                proj(("q", j), [(HD * i, HD * h, HD) for i, h in enumerate((2 * j, 2 * j + 4, 2 * j + 1, 2 * j + 5))])
            proj(("kv",), [(0, 512, 256)])
            for what, a in (("uf", 1280), ("gf", 1536), ("zc", 1792), ("bc", 2048), ("cc", 2304), ("gc", 2560)):
                proj((what,), [(0, a, 256)])
            for j in range(2):
                proj(("ga", j), [(0, 768 + 256 * j, 256)])
            for part in ("cos", "sin"):
                t.append(((l, "dft", part), [(lambda r: r.rearrange("p (k c) -> p k c", k=XT),
                                              I[f"dft_{part}{SEQ}"].rearrange("(k p) c -> p k c", p=P))], True))
            if l < DEPTH - 1:
                t.append(((l, "dft", "ctx"), [
                    (lambda r, i=i: r[:, 512 * i:512 * i + 512].rearrange("p (k c) -> p k c", k=CT),
                     I[f"dft_{part}{CTX}"].rearrange("(k p) c -> p k c", p=P))
                    for i, part in enumerate(("cos", "sin"))], True))
            return t

        def square(w, ch, kh):
            return (lambda r: r.rearrange("p (k c) -> p k c", k=4),
                    w[512 * kh:512 * kh + 512, 512 * ch:512 * ch + 512].rearrange("(k p) c -> p k c", p=P))

        SECOND = ([("a", j, 256 * j, 256) for j in range(3)] + [("av", 0, 768, 256), ("av", 1, 1024, 128)]
                  + [("bq", 0, 1152, 256), ("bk", 0, 1408, 256), ("bv", 0, 1664, 256), ("c", 0, 1920, 256), ("c", 1, 2176, 160)])

        def second_tiles(l):
            y = DEPTH + l
            t = []
            for what, j, a, n in SECOND:
                t.append(((y, what, j), [(lambda r, n=n: r[:, 0:KD * n].rearrange("p (k c) -> p k c", k=KD),
                                       cols(I["w_in_2"][l], a, a + n))], True))
            t.append(((y, "up"), [
                (lambda r: r[:, 0:2 * 576].rearrange("p (k c) -> p k c", k=2),
                 I["w_uq_2"][l].rearrange("(k p) c -> p k c", p=P)),
                (lambda r: r[:, 1152:1152 + 768], I["w_ukv_2"][l])], True))
            for ch in range(2):
                for kh in range(2):
                    t.append(((y, "o", ch, kh), [square(I["w_o_2"][l], ch, kh)], True))
            for j in range(FC):
                t.append(((y, "ff", j), [
                    (lambda r, i=i: r.rearrange("p (k c) -> p k c", k=KD)[:, :, P * i:P * i + P],
                     cols(I[w][l], P * j, P * j + P)) for i, w in enumerate(("w_gate_2", "w_up_2"))], True))
            for j in range(FC // 2):
                t.append(((y, "down", j), [(lambda r: r.rearrange("p (k c) -> p k c", k=2),
                                         I["w_down_2"][l][256 * j:256 * j + 256, :].rearrange("(k p) c -> p k c", p=P))], True))
            return t

        stream = []
        mods_in_attention = {0: [(0, j) for j in range(8, 12)] + [(1, j) for j in range(8)],
                             1: [(1, j) for j in range(8, 12)]}
        for j in range(8):
            stream.append(mod_tile(0, j))
        for l in range(DEPTH):
            outs = [((l, "out", ch, kh), [square(I["w_out"][l], ch, kh)], True) for ch in range(2) for kh in range(2)]
            stream += mix_tiles(l) + outs[:2] + [mod_tile(*m) for m in mods_in_attention[l]] + outs[2:]
        for l in range(DEPTH):
            stream += second_tiles(l)
        place = {what: n for n, (what, _, _) in enumerate(stream)}
        splits = [what for what, _, is_split in stream if is_split]
        split_at = {what: i for i, what in enumerate(splits)}
        landed, counts = [], [0] * RAW
        for n, (_, loads, _) in enumerate(stream):
            counts[n % RAW] += 16 * len(loads)
            landed.append(counts[n % RAW])
        landed_sems = [ctx.enter_context(nc.semaphore(f"tile_landed{r}")) for r in range(RAW)]

        def raw_of(what):
            return raw[:, place[what] % RAW, :]

        def wait_landed(eng, what):
            n = place[what]
            eng.wait_ge(landed_sems[n % RAW], landed[n])

        consts = [(ident[:], I["ident"]), (rot1[:], I["rot1"]), (rot2[HD:QC, :], I["rot2"]),
                  (cos1[:], I["cos1"]), (sin1[:], I["sin1"]),
                  (band_mid[:], I["band_mid"]), (band_last[:], I["band_last"]),
                  (dft_ccos[:], I["dft_ccos"]), (dft_csin[:], I["dft_csin"]),
                  (sinks[:], I["sink"].rearrange("l h -> (l h)").partition_broadcast(P)),
                  (table[0:BUCKETS, :], I["rel_bias_2"]), (table[BUCKETS:, :], I["pick"]), (hot[:], I["hot"]),
                  (vec[0:8, :], I["c"].rearrange("a (r p) -> (a r) p", p=P)),
                  (vec[8:16, :], I["c_ctx"].rearrange("(r p) -> r p", p=P))]
        VB = []
        for l in range(DEPTH):
            b0 = 16 + 48 * l
            VB.append(dict(b_mod=b0, g_pre=b0 + 24, g_post=b0 + 32, conv_w=b0 + 40, conv_b=b0 + 46))
            consts += [(vec[b0:b0 + 24, :], I["b_mod"][l].rearrange("(r p) -> r p", p=P)),
                       (vec[b0 + 24:b0 + 32, :], I["g_pre"][l].rearrange("(r p) -> r p", p=P)),
                       (vec[b0 + 32:b0 + 40, :], I["g_post"][l].rearrange("(r p) -> r p", p=P)),
                       (vec[b0 + 40:b0 + 46, :], I["conv_w"][l].rearrange("t (r p) -> (t r) p", p=P)),
                       (vec[b0 + 46:b0 + 48, :], I["conv_b"][l].rearrange("(r p) -> r p", p=P))]
        LG = 16 + 48 * DEPTH
        consts += [(vec[LG:LG + 4, :], I["q_norm_g_2"].rearrange("l (r p) -> (l r) p", p=P)), (vec[LG + 4:LG + 6, :], I["kv_norm_g_2"])]
        NV = LG + 6

        def units1(l):
            u = []
            for h in range(HEADS):
                b = HD * (h // 4)
                for i in range(XT + (CT if l < DEPTH - 1 else 0)):
                    ctx_v = [v1[:, XT + j, b:b + HD] for j in range(CT)]
                    ctx_k = [k1[b:b + HD, SEQ + P * j:SEQ + P * j + P] for j in range(CT)]
                    if i < XT:
                        lo, hi = max(0, i - 1), min(XT - 1, i + 1)
                        n = hi - lo + 1
                        segs = [(0, k1[b:b + HD, P * lo:P * hi + P])] + [(P * (n + j), k) for j, k in enumerate(ctx_k)]
                        vs = [v1[:, j, b:b + HD] for j in range(lo, hi + 1)] + ctx_v
                        mask = band_last[:] if i == XT - 1 else band_mid[:, P if i == 0 else 0:]
                    else:
                        segs, vs, mask = [(0, k1[b:b + HD, SEQ:TOK])], ctx_v, band_mid[:, 3 * P:]
                    u.append(dict(q=q1[b:b + HD, h % 4, P * i:P * i + P], segs=segs, vs=vs, mask=mask, second=False,
                                  out=ao1[:, i, HD * h:HD * h + HD], sink=sinks[:, l * HEADS + h:l * HEADS + h + 1]))
            return u

        def units2():
            u = []

            def add(q, k, v, head, out, second=False):
                for i in range(XT):
                    u.append(dict(q=q(i), segs=[(0, k(P * (i + 1)))], vs=[v(j) for j in range(i + 1)],
                                  mask=strips[:, head, 384 - P * i:SEQ], out=out(i), sink=None, second=second))

            for h in range(B_HEADS):
                for m in range(2):
                    b = HD * (h % 2) + 32 * m
                    add(lambda i: qb[b:b + 32, h // 2, P * i:P * i + P], lambda n: kb[b:b + 32, h // 2, 0:n],
                        lambda j: vb[:, j, HD * h:HD * h + HD], A_HEADS + h,
                        lambda i: ao2[:, i, 384 + HD * h:384 + HD * h + HD], second=m == 1)
            for h in range(A_HEADS):
                b = HD * (h % 2)
                add(lambda i: qa[b:b + HD, h // 2, P * i:P * i + P], lambda n: ka[b:b + HD, h // 2, 0:n],
                    lambda j: va[:, j, HD * h:HD * h + HD], h, lambda i: ao2[:, i, HD * h:HD * h + HD])
            for h in range(C_HEADS):
                add(lambda i: qc[0:QC, h, P * i:P * i + P], lambda n: kc[0:QC, h, 0:n],
                    lambda j: vc[:, j, HD * h:HD * h + HD], A_HEADS + B_HEADS,
                    lambda i: ao2[:, i, 640 + HD * h:640 + HD * h + HD])
            return u

        N_B = 2 * B_HEADS * XT
        BUF = (sc, pr, pt), (sc2, pr2, pt2)

        def halves(u):
            n = len(u["vs"])
            return -(-n // 2), n // 2

        block = ctx.enter_context(nc.Block())

        @block.sync
        def _(sp):
            sp.dma_start(res[:], I["x"][0].rearrange("(t p) d -> p t d", p=P)).then_inc(s_x_landed.sem, 16)
            sp.dma_start(res_c[:], I["ctx"][0].rearrange("(t p) d -> p t d", p=P)).then_inc(s_x_landed.sem, 16)
            for n, (what, loads, _) in enumerate(stream):
                if n >= RAW:
                    before, _, was_split = stream[n - RAW]
                    if was_split:
                        sp.wait_ge(s_tile_lo.sem, s_tile_lo.at(before))
                    else:
                        sp.wait_ge(s_mod.sem, s_mod.at(before))
                for into, src in loads:
                    sp.dma_start(into(raw[:, n % RAW, :]), src).then_inc(landed_sems[n % RAW], 16)
            for t in range(XT):
                sp.wait_ge(s_x_final.sem, s_x_final.at((2 * DEPTH - 1, t)))
                sp.dma_start(out[0, P * t:P * t + P, :], res[:, t, :]).then_inc(s_stored.sem, 16)
            sp.wait_ge(s_stored.sem, 16 * XT)

        @block.gpsimd
        def _(pool):
            for dst, src in consts:
                pool.dma_start(dst, src).then_inc(s_consts.sem, 16)
            pool.memset(ones[:], 1.0).then_inc(s_ones.sem, s_ones.nth(0))
            pool.memset(wf[:], 0.0).then_inc(s_wf_zero.sem, s_wf_zero.nth(0))
            pool.wait_ge(s_wf_zero.sem, s_wf_zero.at(0))
            for l in range(DEPTH):
                for h in range(2):
                    pool.dma_start(wf[HD * h:HD * h + HD, l, :, HD * h:HD * h + HD],
                                   I["w_fourier"][l].rearrange("(c h) a b -> h a c b", h=2)[h]).then_inc(s_wf_landed.sem, 16)
            for i, what in enumerate(splits):
                pool.wait_ge(s_tile_hi.sem, s_tile_hi.at(what))
                pool.tensor_tensor(w_lo[:, i % SPLIT, :], raw_of(what), w_hi[:, i % SPLIT, :].bitcast(F32),
                                         ALU.subtract).then_inc(s_tile_lo.sem, s_tile_lo.nth(what))

        @block.scalar
        def _(act):
            todo = list(splits)

            def split_next():
                if not todo:
                    return
                what = todo.pop(0)
                i = split_at[what]
                if i >= SPLIT:
                    act.wait_ge(s_mm.sem, s_mm.at(("tile", splits[i - SPLIT])))
                wait_landed(act, what)
                act.activation(w_hi[:, i % SPLIT, :], raw_of(what), ACT.Copy).then_inc(s_tile_hi.sem, s_tile_hi.nth(what))

            def root(key, n):
                act.wait_ge(s_var.sem, s_var.at(key))
                act.activation(rstd[:, 0:n], ssq[:, 0:n], ACT.Sqrt).then_inc(s_root.sem, s_root.nth(key))

            def exp_units(y, units, bufs):
                s_, p_, t_ = bufs
                for step in range(len(units) + 2):
                    if step < len(units):
                        u, i = units[step], step
                        n = P * len(u["vs"])
                        act.wait_ge(s_negm.sem, s_negm.at((y, i)))
                        if i >= 2:
                            act.wait_ge(s_turned.sem, s_turned.at((y, i - 2)))
                        act.activation(p_[:, i % 2, 0:n], s_[:, i % 2, 0:n], ACT.Exp, bias=small[:, 1, i % 4:i % 4 + 1],
                                             accum_out=small[:, 2, i % 4:i % 4 + 1]).then_inc(s_probs.sem, s_probs.nth((y, i)))
                        if u["sink"] is not None:
                            act.activation(small[:, 3, i % 4:i % 4 + 1], u["sink"], ACT.Exp,
                                                 bias=small[:, 1, i % 4:i % 4 + 1]).then_inc(s_sink_exp.sem, s_sink_exp.nth((y, i)))
                    i = step - 2
                    if i >= 0:
                        a, _ = halves(units[i])
                        act.wait_ge(s_turned.sem, s_turned.at((y, i)))
                        if i >= 2:
                            act.wait_ge(s_mixed.sem, s_mixed.at((y, i - 2)))
                        act.activation(t_[:, i % 2, 0:P * a], ps[:, 4, 0:P * a], ACT.Copy).then_inc(s_pt_act.sem, s_pt_act.nth((y, i)))
                    if y >= DEPTH and step == N_B + 5:
                        root((y, "sub"), 16)

            act.wait_ge(s_consts.sem, 16 * len(consts))
            act.wait_ge(s_vec_t.sem, s_vec_t.at(0))
            for s in range(2):
                act.activation(cond[:, :, s], vec_t[:, 8 * s:8 * s + 8], ACT.Silu).then_inc(s_cond.sem, s_cond.nth(s))
            act.wait_ge(s_rr.sem, s_rr.at(0))
            for h in range(A_HEADS + B_HEADS):
                act.dma_start(scratch[h].rearrange("(o p n) -> o p n", o=1, n=SEQ + P),
                              rr[h:h + 1, :].unsqueeze(1).broadcast_to((1, P, SEQ + P))).then_inc(s_bias_rows.sem, 16)
            split_next()
            split_next()
            for l in range(DEPTH):
                both = l < DEPTH - 1
                nt, nc_ = (NT, TOK) if both else (XT, SEQ)
                parts = 2 if both else 1
                if l == 0:
                    act.wait_ge(s_x_landed.sem, 32)
                for t in range(NT):
                    if l > 0:
                        act.wait_ge(s_x_final.sem, s_x_final.at((l - 1, t)))
                    src = res[:, t, :] if t < XT else res_c[:, t - XT, :]
                    act.activation(xn[:, t, :], src, ACT.Square, accum_out=ssq[:, t:t + 1]).then_inc(s_ssq.sem, s_ssq.nth((l, "pre", t)))
                root((l, "pre"), NT)
                for k in range(KD):
                    act.wait_ge(s_mod_x.sem, s_mod_x.at((l, k)))
                    act.activation(h_hi[:, k, :], tmp_n[:, k % 2, :], ACT.Copy).then_inc(s_hi.sem, s_hi.nth((l, "n", k)))
                n_fm = 0

                def fm(what, c, func, dst, scale=1.0, n_parts=parts):
                    nonlocal n_fm
                    for part in range(n_parts):
                        act.wait_ge(s_mm.sem, s_mm.at((l, what, c, part)))
                        b, n, a = (n_fm % 4, SEQ, 0) if part == 0 else (4 + n_fm % 2, CTX, SEQ)
                        act.activation(dst[:, a:a + n], ps[:, b, 0:n], func, scale=scale).then_inc(s_proj.sem, s_proj.nth((l, what, c, part)))
                    n_fm += 1

                for j in range(2):
                    for c in range(2):
                        fm(("q", j), c, ACT.Copy, q1[:, 2 * j + c, :], scale=HD ** -0.5)
                    split_next()
                fm(("kv",), 0, ACT.Copy, k1[:], n_parts=2)
                for part, n in ((0, XT), (1, CT)):
                    act.wait_ge(s_mm.sem, s_mm.at((l, ("kv",), 1, part)))
                    act.activation(v1[:, XT * part:XT * part + n, :].rearrange("p t c -> p (t c)"),
                                         ps[:, 6 + part, 0:n * P], ACT.Copy).then_inc(s_proj.sem, s_proj.nth((l, ("kv",), 1, part)))
                split_next()
                if l == 0:
                    act.wait_ge(s_bias_rows.sem, 16 * (A_HEADS + B_HEADS))
                for g in range(nt // 2):
                    act.wait_ge(s_mm.sem, s_mm.at((l, ("uf",), g, 0)))
                    act.activation(uf_hi[:, 2 * g:2 * g + 2, :].rearrange("p t c -> p (t c)"),
                                         ps[:, (6, 7, 5)[g], :], ACT.Copy).then_inc(s_uf_hi.sem, s_uf_hi.nth((l, g)))
                split_next()
                for what, func, dst in (("gf", ACT.Silu, gf), ("zc", ACT.Copy, cz), ("bc", ACT.Copy, cb)):
                    for c in range(2):
                        fm((what,), c, func, dst[:, c, :])
                    split_next()
                n_fm += 2
                split_next()
                act.wait_ge(s_roped.sem, s_roped.at((l, 4)))
                for c in range(2):
                    fm(("gc",), c, ACT.Silu, tmp_p[:, c, :])
                split_next()
                act.wait_ge(s_conv_gate.sem, s_conv_gate.at((l, 1)))
                for j in range(2):
                    for c in range(2):
                        fm(("ga", j), c, ACT.Silu, ga[:, 2 * j + c, :])
                    split_next()
                for i in range(2):
                    for c in range(2):
                        act.wait_ge(s_mm.sem, s_mm.at((l, "four", i, c)))
                        act.activation(four[:, i, c, 0:SEQ], ps[:, 2 * i + c, :], ACT.Copy).then_inc(s_four_out.sem, s_four_out.nth((l, i, c)))
                    split_next()
                if both:
                    for i in range(2):
                        act.wait_ge(s_mm.sem, s_mm.at((l, "four", i, "ctx")))
                        act.activation(four[:, i, :, SEQ:], ps[:, 4 + i, :].rearrange("p (c n) -> p c n", c=2),
                                             ACT.Copy).then_inc(s_four_out.sem, s_four_out.nth((l, i, "ctx")))
                    split_next()
                exp_units(l, units1(l), BUF[0])
                for t in range(nt):
                    act.wait_ge(s_gated.sem, s_gated.at((l, t)))
                    act.activation(h_hi[:, 0:4, P * t:P * t + P],
                                         tmp_m[:, t % 2, :].rearrange("p (c n) -> p c n", c=4), ACT.Copy).then_inc(s_hi.sem, s_hi.nth((l, "m", t)))
                for c in range(4):
                    act.wait_ge(s_side.sem, s_side.at((l, c)))
                    src = gf[:, c, 0:nc_] if c < 2 else cb[:, c - 2, 0:nc_]
                    act.activation(h_hi[:, 4 + c, 0:nc_], src, ACT.Copy).then_inc(s_hi.sem, s_hi.nth((l, "s", c)))
                act.wait_ge(s_lo.sem, s_lo.at((l, "s", 3)))
                for ch in range(2):
                    split_next()
                    for t in range(nt):
                        act.wait_ge(s_mm.sem, s_mm.at((l, "out", ch, t)))
                        act.activation(y1[:, t, 512 * ch:512 * ch + 512], ps[:, t, :], ACT.Copy).then_inc(s_y.sem, s_y.nth((l, ch, t)))
                    if ch < parts:
                        for b in range(2):
                            act.wait_ge(s_gate_mm.sem, s_gate_mm.at((l, ch, b)))
                            act.activation(gate_b[:, ch, 512 * b:512 * b + 512], ps[:, 6 + b, :], ACT.Copy).then_inc(s_gate_b.sem, s_gate_b.nth((l, ch)))
                    if ch == 0:
                        split_next()
                for t in range(nt):
                    act.wait_ge(s_y.sem, s_y.at((l, 1, t)))
                    if t > 0:
                        act.wait_ge(s_ssq.sem, s_ssq.at((l, "post", t - 1)))
                    act.activation(junk[:], y1[:, t, :], ACT.Square, accum_out=ssq[:, t:t + 1]).then_inc(s_ssq.sem, s_ssq.nth((l, "post", t)))
                root((l, "post"), nt)
                split_next()

            for l in range(DEPTH):
                y = DEPTH + l
                for t in range(XT):
                    act.wait_ge(s_x_final.sem, s_x_final.at((y - 1, t)))
                for dst, src in ((cos2[HD:QC, :], I["cos2"]), (sin2[HD:QC, :], I["sin2"]),
                                 (dlam[:], I["diff_lambda_2"][l].rearrange("a b -> (a b)").partition_broadcast(P)),
                                 (lam_c[:], I["lam_init"][l].partition_broadcast(P)),
                                 (subln[:], I["subln_g_2"][l].partition_broadcast(P))):
                    act.dma_start(dst, src).then_inc(s_layer_consts.sem, s_layer_consts.nth(y, 16))
                for k in range(KD):
                    act.wait_ge(s_xt.sem, s_xt.at((y, k)))
                    act.activation(g_hi[:, k, :], ps[:, k % 4, :], ACT.Copy).then_inc(s_hi.sem, s_hi.nth((y, "t", k)))
                act.wait_ge(s_lam_sums.sem, s_lam_sums.at(y))
                act.activation(lam[:, 2:4], lam[:, 0:2], ACT.Exp).then_inc(s_lam_exp.sem, s_lam_exp.nth(y))
                for j in range(3):
                    for c in range(2):
                        i = 2 * j + c
                        act.wait_ge(s_mm.sem, s_mm.at((y, "a", i)))
                        dst, scale = (qa[:, i, :], HD ** -0.5) if i < 3 else (ka[:, i - 3, :], 1.0)
                        act.activation(dst, ps[:, i % 4, :], ACT.Copy, scale=scale).then_inc(s_proj.sem, s_proj.nth((y, "a", i)))
                    split_next()
                for j, n in ((0, 256), (1, 128)):
                    for g in range(2):
                        act.wait_ge(s_mm.sem, s_mm.at((y, "av", j, g)))
                        act.activation(va[:, 2 * g:2 * g + 2, 256 * j:256 * j + n],
                                             ps[:, 4 + 2 * j + g, 0:2 * n].rearrange("p (t c) -> p t c", t=2), ACT.Copy).then_inc(s_proj.sem, s_proj.nth((y, "av", j, g)))
                    split_next()
                for what, dst, b0, scale in (("bq", qb, 0, 32 ** -0.5), ("bk", kb, 2, 1.0)):
                    for c in range(2):
                        act.wait_ge(s_mm.sem, s_mm.at((y, what, c)))
                        act.activation(dst[:, c, :], ps[:, b0 + c, :], ACT.Copy, scale=scale).then_inc(s_proj.sem, s_proj.nth((y, what, c)))
                    split_next()
                for g in range(2):
                    act.wait_ge(s_mm.sem, s_mm.at((y, "bv", 0, g)))
                    act.activation(vb[:, 2 * g:2 * g + 2, :].rearrange("p t c -> p (t c)"), ps[:, 4 + g, :], ACT.Copy).then_inc(s_proj.sem, s_proj.nth((y, "bv", 0, g)))
                split_next()
                for j, n in ((0, 256), (1, 160)):
                    for g in range(2):
                        act.wait_ge(s_mm.sem, s_mm.at((y, "c", j, g)))
                        act.activation(c_in[:, 2 * g:2 * g + 2, 256 * j:256 * j + n],
                                             ps[:, (6, 0)[j] + g, 0:2 * n].rearrange("p (t c) -> p t c", t=2), ACT.Copy).then_inc(s_proj.sem, s_proj.nth((y, "c", j, g)))
                    split_next()
                act.wait_ge(s_proj.sem, s_proj.at((y, "c", 1, 1)))
                for t in range(XT):
                    if t > 0:
                        act.wait_ge(s_ssq.sem, s_ssq.at((y, "c", 3 + t)))
                    act.activation(tmp_c[:, 0, 0:256], c_in[:, t, 0:256], ACT.Square, accum_out=ssq[:, t:t + 1]).then_inc(s_ssq.sem, s_ssq.nth((y, "c", t)))
                    act.activation(tmp_c[:, 1, 0:128], c_in[:, t, 256:384], ACT.Square, accum_out=ssq[:, 4 + t:5 + t]).then_inc(s_ssq.sem, s_ssq.nth((y, "c", 4 + t)))
                root((y, "c"), 8)
                for i in range(3):
                    act.wait_ge(s_lat.sem, s_lat.at((y, i)))
                    act.activation(cq_hi[:, i, :] if i < 2 else ckv_hi[:], tmp_c[:, i % 2, :], ACT.Copy).then_inc(s_hi.sem, s_hi.nth((y, "c", i)))
                for h in range(C_HEADS):
                    act.wait_ge(s_mm.sem, s_mm.at((y, "qc", h)))
                    act.activation(qc[0:QC, h, :], ps[0:QC, h % 2, :], ACT.Copy, scale=QC ** -0.5).then_inc(s_proj.sem, s_proj.nth((y, "qc", h)))
                    act.wait_ge(s_mm.sem, s_mm.at((y, "kc", h)))
                    act.activation(kc[0:HD, h, :], ps[0:HD, 2 + h % 2, :], ACT.Copy).then_inc(s_proj.sem, s_proj.nth((y, "kc", h)))
                for t in range(XT):
                    act.wait_ge(s_mm.sem, s_mm.at((y, "vc", t)))
                    act.activation(vc[:, t, :], ps[:, 4 + t, 0:384], ACT.Copy).then_inc(s_proj.sem, s_proj.nth((y, "vc", t)))
                split_next()
                act.wait_ge(s_roped.sem, s_roped.at((y, C_HEADS - 1)))
                act.wait_ge(s_kr_all.sem, s_kr_all.at(y))
                act.wait_ge(s_bias_rows.sem, 16 * (A_HEADS + B_HEADS))
                for h in range(A_HEADS + B_HEADS):
                    act.dma_start(strips[:, h, :], scratch[h, P - 1:P - 1 + P * (SEQ + P - 1)].rearrange(
                        "(p n) -> p n", n=SEQ + P - 1)[:, 0:SEQ]).then_inc(s_strips.sem, s_strips.nth(y, 16))
                act.dma_start(strips[:, A_HEADS + B_HEADS, :], I["causal"]).then_inc(s_strips.sem, s_strips.nth(y, 16))
                units = units2()
                exp_units(y, units, BUF[1])
                act.wait_ge(s_mixed.sem, s_mixed.at((y, len(units) - 1)))
                for i, w in enumerate(("ln1_g_2", "ln1_b_2")):
                    act.dma_start(ln1[:, i, :], I[w][l].partition_broadcast(P)).then_inc(s_ln.sem, s_ln.nth((y, 1), 16))
                for t in range(XT):
                    for g in range(2):
                        act.wait_ge(s_aot.sem, s_aot.at((y, t, g)))
                        act.activation(g_hi[:, 4 * g:4 * g + 4, P * t:P * t + P],
                                             ps[:, 2 * (t % 2) + g, :].rearrange("p (c n) -> p c n", c=4), ACT.Copy).then_inc(s_hi.sem, s_hi.nth((y, "m", t, g)))
                for _ in range(4):
                    split_next()
                root((y, 1), XT)
                for k in range(KD):
                    act.wait_ge(s_ht.sem, s_ht.at((y, k)))
                    act.activation(g_hi[:, k, :], ps[:, k % 4, :], ACT.Copy).then_inc(s_hi.sem, s_hi.nth((y, "h", k)))
                for j in range(FC):
                    act.wait_ge(s_mm.sem, s_mm.at((y, "gate", j)))
                    act.activation(tmp_f[:, j % 2, :], ps[:, 2 * (j % 3), :], ACT.Silu).then_inc(s_silu.sem, s_silu.nth((y, j)))
                    act.wait_ge(s_glu.sem, s_glu.at((y, j)))
                    act.activation(hid_hi[:, j, :], tmp_f[:, 2 + j % 2, :], ACT.Copy).then_inc(s_hi.sem, s_hi.nth((y, "f", j)))
                    split_next()
                for i, w in enumerate(("ln2_g_2", "ln2_b_2")):
                    act.dma_start(ln2[:, i, :], I[w][l].partition_broadcast(P)).then_inc(s_ln.sem, s_ln.nth((y, 2), 16))
                for j in range(FC // 2):
                    split_next()
                root((y, 2), XT)

        @block.tensor
        def _(pe):
            emptied = {b: (s_consts.sem, 16 * len(consts)) for b in range(8)}

            def begin(what):
                pe.wait_ge(s_tile_lo.sem, s_tile_lo.at(what))
                i = split_at[what] % SPLIT
                return w_hi[:, i, :], w_lo[:, i, :]

            def left(what):
                s_mm.name_latest(("tile", what))

            def mm3(o, lhs, rhs, first, last):
                pe.matmul(o, lhs[1], rhs[0], start=first, stop=False)
                pe.matmul(o, lhs[0], rhs[1], start=False, stop=False)
                return pe.matmul(o, lhs[0], rhs[0], start=False, stop=last)

            def both_parts(pair, f):
                return f(pair[0]), f(pair[1])

            def turn(o, src, key, ident_n=P):
                return pe.transpose(o, src, ident[0:ident_n, 0:ident_n])

            def mod(l, j):
                what = (l, "mod", j)
                wait_landed(pe, what)
                w = raw_of(what).rearrange("p (k c) -> p k c", k=KD)
                for c in range(2):
                    o = 64 * l + 2 * (2 * j + c)
                    for k in range(KD):
                        m = pe.matmul(ps[:, 7, o:o + 2], w[:, k, P * c:P * c + P], cond[:, k, :], start=k == 0, stop=k == KD - 1)
                m.then_inc(s_mod.sem, s_mod.nth(what))

            def attend(y, units, at_step):
                for b in range(8):
                    pe.wait_ge(*emptied[b])
                dve_half = [i for i, u in enumerate(units) if halves(u)[1]]
                s_, p_, t_ = BUF[0 if y < DEPTH else 1]
                for step in range(len(units) + 3):
                    i = step
                    if i < len(units):
                        u = units[i]
                        if i >= 2:
                            pe.wait_ge(s_negm.sem, s_negm.at((y, i - 2)))
                        o0 = 1024 * (i % 2)
                        for col, k in u["segs"]:
                            m = pe.matmul(ps_flat[:, o0 + col:o0 + col + k.shape[1]], u["q"], k, start=True, stop=True)
                        m.then_inc(s_scores.sem, s_scores.nth((y, i)))
                    i = step - 2
                    if 0 <= i < len(units):
                        a, d = halves(units[i])
                        pe.wait_ge(s_probs.sem, s_probs.at((y, i)))
                        if i >= 1:
                            pe.wait_ge(s_pt_act.sem, s_pt_act.at((y, i - 1)))
                        was = [j for j in dve_half if j < i]
                        if d and was:
                            pe.wait_ge(s_pt_dve.sem, s_pt_dve.at((y, was[-1])))
                        for j in range(a + d):
                            o = ps[:, 4, P * j:P * j + P] if j < a else ps[:, 5, P * (j - a):P * (j - a) + P]
                            m = pe.transpose(o, p_[:, i % 2, P * j:P * j + P], ident[:])
                        m.then_inc(s_turned.sem, s_turned.nth((y, i)))
                    i = step - 3
                    if 0 <= i < len(units):
                        u = units[i]
                        n = len(u["vs"])
                        pe.wait_ge(s_pt_act.sem, s_pt_act.at((y, i)))
                        if halves(u)[1]:
                            pe.wait_ge(s_pt_dve.sem, s_pt_dve.at((y, i)))
                        if i >= 1:
                            pe.wait_ge(s_o_out.sem, s_o_out.at((y, i - 1)))
                        for j, v in enumerate(u["vs"]):
                            m = pe.matmul(ps[:, 6, 0:HD], t_[:, i % 2, P * j:P * j + P], v, start=j == 0, stop=j == n - 1)
                        m.then_inc(s_mixed.sem, s_mixed.nth((y, i)))
                    at_step(step)
                n = len(units) - 1
                for b in range(4):
                    emptied[b] = s_negm.after((y, n))
                emptied[4] = s_pt_act.after((y, n))
                emptied[5] = s_pt_dve.after((y, dve_half[-1]))
                emptied[6] = s_o_out.after((y, n))

            pe.wait_ge(s_consts.sem, 16 * len(consts))
            pe.wait_ge(*emptied[7])
            emptied[7] = s_vec_t.after(0)
            pe.transpose(ps[:, 7, 0:NV], vec[0:NV, :], ident[0:NV, 0:NV]).then_inc(s_vec_mm.sem, s_vec_mm.nth(0))
            pe.wait_ge(*emptied[0])
            emptied[0] = s_rr.after(0)
            pe.wait_ge(*emptied[1])
            emptied[1] = s_rr.after(0)
            pe.matmul(ps[0:A_HEADS + B_HEADS, 0, :], table[:], hot[:, 0:SEQ], start=True, stop=True)
            pe.matmul(ps[0:A_HEADS + B_HEADS, 1, 0:P], table[:], hot[:, SEQ:SEQ + P], start=True, stop=True).then_inc(s_rr_mm.sem, s_rr_mm.nth(0))
            pe.wait_ge(*emptied[7])
            emptied[7] = s_mod_out.after((0, 0))
            for s in range(2):
                pe.wait_ge(s_cond.sem, s_cond.at(s))
            for j in range(8):
                mod(0, j)

            for l in range(DEPTH):
                both = l < DEPTH - 1
                nt, nc_ = (NT, TOK) if both else (XT, SEQ)
                parts = 2 if both else 1
                if l == 0:
                    pe.wait_ge(s_wf_landed.sem, 16 * 2 * DEPTH)
                pe.wait_ge(*emptied[6])
                emptied[6] = s_wf_m.after(l)
                for i, m_ in enumerate((dft_ccos, dft_csin)):
                    m = pe.matmul(ps[:, 6, 256 * i:256 * i + 256], m_[:], wf[:, l, :, :], start=True, stop=True)
                m.then_inc(s_wf_mm.sem, s_wf_mm.nth(l))
                for k in range(KD):
                    pe.wait_ge(*emptied[k % 4])
                    emptied[k % 4] = s_mod_x.after((l, k))
                    pe.wait_ge(*emptied[4 + k % 2])
                    emptied[4 + k % 2] = s_mod_x.after((l, k))
                    for t in range(NT):
                        if k == 0:
                            pe.wait_ge(s_xn.sem, s_xn.at((l, t)))
                        o = ps[:, k % 4, P * t:P * t + P] if t < XT else ps[:, 4 + k % 2, P * (t - XT):P * (t - XT) + P]
                        m = pe.transpose(o, xn[:, t, P * k:P * k + P], ident[:])
                    m.then_inc(s_nt.sem, s_nt.nth((l, k)))
                n_fm = 0
                H = (h_hi, h_lo)
                lo_seen = set()

                def rows_ready(k):
                    if k not in lo_seen:
                        lo_seen.add(k)
                        pe.wait_ge(s_lo.sem, s_lo.at((l, "n", k)))

                def fm(what, c, w, until, n_parts=parts):
                    nonlocal n_fm
                    w = both_parts(w, lambda r: r.rearrange("p (k c) -> p k c", k=KD))
                    for part in range(n_parts):
                        b, n, a = (n_fm % 4, SEQ, 0) if part == 0 else (4 + n_fm % 2, CTX, SEQ)
                        pe.wait_ge(*emptied[b])
                        emptied[b] = until.after((l, what, c, part))
                        for k in range(KD):
                            rows_ready(k)
                            m = mm3(ps[:, b, 0:n], both_parts(w, lambda r: r[:, k, P * c:P * c + P]),
                                    both_parts(H, lambda r: r[:, k, a:a + n]), k == 0, k == KD - 1)
                        m.then_inc(s_mm.sem, s_mm.nth((l, what, c, part)))
                    n_fm += 1

                def tm(o, t, w, c0, n):
                    w = both_parts(w, lambda r: r.rearrange("p (k c) -> p k c", k=KD))
                    for k in range(KD):
                        m = mm3(o, both_parts(H, lambda r: r[:, k, P * t:P * t + P]),
                                both_parts(w, lambda r: r[:, k, c0:c0 + n]), k == 0, k == KD - 1)
                    return m

                for j in range(2):
                    w = begin((l, "q", j))
                    for c in range(2):
                        fm(("q", j), c, w, s_proj)
                    left((l, "q", j))
                w = begin((l, "kv"))
                fm(("kv",), 0, w, s_proj, 2)
                for part, t0, n in ((0, 0, XT), (1, XT, CT)):
                    pe.wait_ge(*emptied[6 + part])
                    emptied[6 + part] = s_proj.after((l, ("kv",), 1, part))
                    for t in range(n):
                        m = tm(ps[:, 6 + part, P * t:P * t + P], t0 + t, w, P, P)
                    m.then_inc(s_mm.sem, s_mm.nth((l, ("kv",), 1, part)))
                left((l, "kv"))
                w = begin((l, "uf"))
                for g in range(nt // 2):
                    b = (6, 7, 5)[g]
                    pe.wait_ge(*emptied[b])
                    emptied[b] = s_uf_lo.after((l, g))
                    for t in range(2):
                        m = tm(ps[:, b, 256 * t:256 * t + 256], 2 * g + t, w, 0, 256)
                    m.then_inc(s_mm.sem, s_mm.nth((l, ("uf",), g, 0)))
                left((l, "uf"))
                for what in ("gf", "zc", "bc", "cc", "gc"):
                    w = begin((l, what))
                    for c in range(2):
                        fm((what,), c, w, s_conv_t if what == "cc" else s_proj)
                    left((l, what))
                    if what == "gf":
                        for i in range(5):
                            b = 6 + i % 2
                            pe.wait_ge(*emptied[b])
                            emptied[b] = s_roped.after((l, i))
                            pe.wait_ge(s_proj.sem, s_proj.at((l, ("q", i // 2), i % 2, 0) if i < 4 else (l, ("kv",), 0, 0)))
                            src = q1[:, i, 0:SEQ] if i < 4 else k1[:, 0:SEQ]
                            pe.matmul(ps[:, b, :], rot1[:], src, start=True, stop=True).then_inc(s_rot.sem, s_rot.nth((l, i)))
                for j in range(2):
                    w = begin((l, "ga", j))
                    for c in range(2):
                        fm(("ga", j), c, w, s_proj)
                    left((l, "ga", j))
                U = (uf_hi, uf_lo)
                pe.wait_ge(s_uf_lo.sem, s_uf_lo.at((l, nt // 2 - 1)))
                for i, part in enumerate(("cos", "sin")):
                    w = both_parts(begin((l, "dft", part)), lambda r: r.rearrange("p (k c) -> p k c", k=XT))
                    for c in range(2):
                        pe.wait_ge(*emptied[2 * i + c])
                        emptied[2 * i + c] = s_four_out.after((l, i, c))
                        for k in range(XT):
                            m = mm3(ps[:, 2 * i + c, :], both_parts(U, lambda r: r[:, k, P * c:P * c + P]),
                                    both_parts(w, lambda r: r[:, k, :]), k == 0, k == XT - 1)
                        m.then_inc(s_mm.sem, s_mm.nth((l, "four", i, c)))
                    left((l, "dft", part))
                if both:
                    w = both_parts(begin((l, "dft", "ctx")), lambda r: r[:, 0:1024].rearrange("p (i k c) -> p i k c", i=2, k=CT))
                    for i in range(2):
                        pe.wait_ge(*emptied[4 + i])
                        emptied[4 + i] = s_four_out.after((l, i, "ctx"))
                        for c in range(2):
                            for k in range(CT):
                                m = mm3(ps[:, 4 + i, CTX * c:CTX * c + CTX], both_parts(U, lambda r: r[:, XT + k, P * c:P * c + P]),
                                        both_parts(w, lambda r: r[:, i, k, :]), k == 0, k == CT - 1)
                        m.then_inc(s_mm.sem, s_mm.nth((l, "four", i, "ctx")))
                    left((l, "dft", "ctx"))
                pe.wait_ge(s_wf_m.sem, s_wf_m.at(l))
                for c in range(2):
                    for part in range(parts):
                        b, n, a = (6 + c, SEQ, 0) if part == 0 else (4 + c, CTX, SEQ)
                        pe.wait_ge(s_four_out.sem, s_four_out.at((l, 1, c if part == 0 else "ctx")))
                        pe.wait_ge(*emptied[b])
                        emptied[b] = s_side.after((l, c))
                        for i in range(2):
                            m = pe.matmul(ps[:, b, 0:n], wf_m[:, i, c, :], four[:, i, c, a:a + n], start=i == 0, stop=i == 1)
                        m.then_inc(s_fmix.sem, s_fmix.nth((l, c, part)))
                pe.wait_ge(s_roped.sem, s_roped.at((l, 4)))
                pe.wait_ge(s_proj.sem, s_proj.at((l, ("kv",), 1, 1)))
                units = units1(l)
                mods = list(mods_in_attention[l])

                def between(step):
                    if step >= 3 and step % 2 == 0 and mods:
                        mod(*mods.pop(0))

                attend(l, units, between)
                while mods:
                    mod(*mods.pop(0))
                emptied[7] = s_mod_out.after((l, 1))
                for t in range(nt):
                    pe.wait_ge(*emptied[t % 4])
                    emptied[t % 4] = s_gated.after((l, t))
                    pe.wait_ge(s_o_out.sem, s_o_out.at((l, len(units) - 1)))
                    for c in range(4):
                        m = pe.transpose(ps[:, t % 4, P * c:P * c + P], ao1[:, t, P * c:P * c + P], ident[:])
                    m.then_inc(s_aot.sem, s_aot.nth((l, t)))
                pe.wait_ge(s_lo.sem, s_lo.at((l, "s", 3)))
                for ch in range(2):
                    for kh in range(2):
                        w = both_parts(begin((l, "out", ch, kh)), lambda r: r.rearrange("p (k c) -> p k c", k=4))
                        for t in range(nt):
                            if kh == 0:
                                pe.wait_ge(*emptied[t])
                                emptied[t] = s_y.after((l, ch, t))
                            for k in range(4):
                                m = mm3(ps[:, t, :], both_parts(H, lambda r: r[:, 4 * kh + k, P * t:P * t + P]),
                                        both_parts(w, lambda r: r[:, k, :]), kh == 0 and k == 0, kh == 1 and k == 3)
                            m.then_inc(s_mm.sem, s_mm.nth((l, "out", ch, t) if kh else (l, "out half", ch, t)))
                        left((l, "out", ch, kh))
                    if ch < parts:
                        pe.wait_ge(s_ones.sem, s_ones.at(0))
                        pe.wait_ge(s_diag.sem, s_diag.at((l, ch)))
                        for b in range(2):
                            pe.wait_ge(*emptied[6 + b])
                            emptied[6 + b] = s_gate_b.after((l, ch))
                            pe.matmul(ps[:, 6 + b, :], ones[:], diag[:, ch, 4 * b:4 * b + 4, :], start=True, stop=True).then_inc(s_gate_mm.sem, s_gate_mm.nth((l, ch, b)))

            G = (g_hi, g_lo)
            for l in range(DEPTH):
                y = DEPTH + l

                def rows_fm(turned, ready, before, what):
                    for k in range(KD):
                        pe.wait_ge(*emptied[k % 4])
                        emptied[k % 4] = s_lo.after((y, what, k))
                        for t in range(XT):
                            if k == 0:
                                pe.wait_ge(ready.sem, ready.at((before, t)))
                            m = pe.transpose(ps[:, k % 4, P * t:P * t + P], res[:, t, P * k:P * k + P], ident[:])
                        m.then_inc(turned.sem, turned.nth((y, k)))

                rows_fm(s_xt, s_x_final, y - 1, "t")
                pe.wait_ge(s_lo.sem, s_lo.at((y, "t", KD - 1)))

                def fm(b, w, c, until, key):
                    pe.wait_ge(*emptied[b])
                    emptied[b] = until
                    w = both_parts(w, lambda r: r.rearrange("p (k c) -> p k c", k=KD))
                    for k in range(KD):
                        m = mm3(ps[:, b, :], both_parts(w, lambda r: r[:, k, P * c:P * c + P]),
                                both_parts(G, lambda r: r[:, k, :]), k == 0, k == KD - 1)
                    m.then_inc(s_mm.sem, s_mm.nth(key))

                def tm(b0, w, n, what):
                    w = both_parts(w, lambda r: r[:, 0:KD * n].rearrange("p (k c) -> p k c", k=KD))
                    for g in range(2):
                        pe.wait_ge(*emptied[b0 + g])
                        emptied[b0 + g] = s_proj.after((y, *what, g))
                        for t in range(2):
                            for k in range(KD):
                                m = mm3(ps[:, b0 + g, n * t:n * t + n],
                                        both_parts(G, lambda r: r[:, k, P * (2 * g + t):P * (2 * g + t) + P]),
                                        both_parts(w, lambda r: r[:, k, :]), k == 0, k == KD - 1)
                        m.then_inc(s_mm.sem, s_mm.nth((y, *what, g)))

                for j in range(3):
                    w = begin((y, "a", j))
                    for c in range(2):
                        i = 2 * j + c
                        fm(i % 4, w, c, s_proj.after((y, "a", i)), (y, "a", i))
                    left((y, "a", j))
                for j, n in ((0, 256), (1, 128)):
                    tm(4 + 2 * j, begin((y, "av", j)), n, ("av", j))
                    left((y, "av", j))
                for what, b0 in (("bq", 0), ("bk", 2)):
                    w = begin((y, what, 0))
                    for c in range(2):
                        fm(b0 + c, w, c, s_proj.after((y, what, c)), (y, what, c))
                    left((y, what, 0))
                tm(4, begin((y, "bv", 0)), 256, ("bv", 0))
                left((y, "bv", 0))
                for j, n in ((0, 256), (1, 160)):
                    tm((6, 0)[j], begin((y, "c", j)), n, ("c", j))
                    left((y, "c", j))
                for i in range(4):
                    pe.wait_ge(*emptied[i])
                    emptied[i] = s_lo.after((y, "c", i)) if i < 3 else s_kr_raw.after(y)
                    for t in range(XT):
                        if i == 0:
                            pe.wait_ge(s_latn.sem, s_latn.at((y, t)))
                        if i < 3:
                            m = pe.transpose(ps[:, i, P * t:P * t + P], c_in[:, t, P * i:P * i + P], ident[:])
                        else:
                            m = pe.transpose(ps[0:QC, 3, P * t:P * t + P], c_in[:, t, 416 - QC:416], ident[:])
                    m.then_inc(s_lat_t.sem, s_lat_t.nth((y, i)))
                w = begin((y, "up"))
                uq = both_parts(w, lambda r: r[:, 0:2 * C_HEADS * QC].rearrange("p (k c) -> p k c", k=2))
                ukv = both_parts(w, lambda r: r[:, 2 * C_HEADS * QC:2 * C_HEADS * QC + 2 * C_HEADS * HD])

                def q_rot(h):
                    pe.wait_ge(*emptied[6 + h % 2])
                    emptied[6 + h % 2] = s_roped.after((y, h))
                    pe.wait_ge(s_proj.sem, s_proj.at((y, "qc", h)))
                    pe.matmul(ps[0:QC, 6 + h % 2, :], rot2[HD:QC, :], qc[HD:QC, h, :], start=True, stop=True).then_inc(s_q_rot.sem, s_q_rot.nth((y, h)))

                pe.wait_ge(s_lo.sem, s_lo.at((y, "c", 2)))
                for h in range(C_HEADS):
                    pe.wait_ge(*emptied[h % 2])
                    emptied[h % 2] = s_proj.after((y, "qc", h))
                    for k in range(2):
                        m = mm3(ps[0:QC, h % 2, :], both_parts(uq, lambda r: r[:, k, QC * h:QC * h + QC]),
                                both_parts((cq_hi, cq_lo), lambda r: r[:, k, :]), k == 0, k == 1)
                    m.then_inc(s_mm.sem, s_mm.nth((y, "qc", h)))
                    pe.wait_ge(*emptied[2 + h % 2])
                    emptied[2 + h % 2] = s_proj.after((y, "kc", h))
                    m = mm3(ps[:, 2 + h % 2, :], both_parts(ukv, lambda r: r[:, P * h:P * h + P]),
                            both_parts((ckv_hi, ckv_lo), lambda r: r[:]), True, True)
                    m.then_inc(s_mm.sem, s_mm.nth((y, "kc", h)))
                    if h == 0:
                        pe.wait_ge(*emptied[5])
                        emptied[5] = s_kr_all.after(y)
                        pe.wait_ge(s_kr_raw.sem, s_kr_raw.at(y))
                        pe.matmul(ps[0:QC, 5, :], rot2[HD:QC, :], kc[HD:QC, 0, :], start=True, stop=True).then_inc(s_kr_rot.sem, s_kr_rot.nth(y))
                    else:
                        q_rot(h - 1)
                q_rot(C_HEADS - 1)
                for t in range(XT):
                    pe.wait_ge(*emptied[4 + t])
                    emptied[4 + t] = s_proj.after((y, "vc", t))
                    m = mm3(ps[:, 4 + t, 0:C_HEADS * HD], both_parts((ckv_hi, ckv_lo), lambda r: r[:, P * t:P * t + P]),
                            both_parts(ukv, lambda r: r.rearrange("p (h c) -> p h c", h=C_HEADS)[:, :, HD:2 * HD]), True, True)
                    m.then_inc(s_mm.sem, s_mm.nth((y, "vc", t)))
                left((y, "up"))
                pe.wait_ge(s_roped.sem, s_roped.at((y, C_HEADS - 1)))
                pe.wait_ge(s_kr_all.sem, s_kr_all.at(y))
                units = units2()
                attend(y, units, lambda step: None)
                pe.wait_ge(s_sub.sem, s_sub.at(y))
                pe.wait_ge(s_o_out.sem, s_o_out.at((y, len(units) - 1)))
                for t in range(XT):
                    for g in range(2):
                        b = 2 * (t % 2) + g
                        pe.wait_ge(*emptied[b])
                        emptied[b] = s_lo.after((y, "m", t, g))
                        for c in range(4):
                            m = pe.transpose(ps[:, b, P * c:P * c + P], ao2[:, t, P * (4 * g + c):P * (4 * g + c) + P], ident[:])
                        m.then_inc(s_aot.sem, s_aot.nth((y, t, g)))
                pe.wait_ge(s_lo.sem, s_lo.at((y, "m", XT - 1, 1)))
                for ch in range(2):
                    for kh in range(2):
                        w = both_parts(begin((y, "o", ch, kh)), lambda r: r.rearrange("p (k c) -> p k c", k=4))
                        for t in range(XT):
                            b = 4 * ch + t
                            if kh == 0:
                                pe.wait_ge(*emptied[b])
                                emptied[b] = s_resid.after((y, 1, ch, t))
                            for k in range(4):
                                m = mm3(ps[:, b, :], both_parts(G, lambda r: r[:, 4 * kh + k, P * t:P * t + P]),
                                        both_parts(w, lambda r: r[:, k, :]), kh == 0 and k == 0, kh == 1 and k == 3)
                            m.then_inc(s_mm.sem, s_mm.nth((y, "o", ch, t) if kh else (y, "o half", ch, t)))
                        left((y, "o", ch, kh))
                rows_fm(s_ht, s_normed, y, "h")
                pe.wait_ge(s_lo.sem, s_lo.at((y, "h", KD - 1)))
                for j in range(FC):
                    w = begin((y, "ff", j))
                    b = 2 * (j % 3)
                    fm(b, w, 0, s_silu.after((y, j)), (y, "gate", j))
                    fm(b + 1, w, 1, s_glu.after((y, j)), (y, "ffup", j))
                    left((y, "ff", j))
                for j in range(FC // 2):
                    w = both_parts(begin((y, "down", j)), lambda r: r.rearrange("p (k c) -> p k c", k=2))
                    pe.wait_ge(s_lo.sem, s_lo.at((y, "f", 2 * j + 1)))
                    for t in range(XT):
                        for ch in range(2):
                            b = 2 * t + ch
                            if j == 0:
                                pe.wait_ge(*emptied[b])
                                emptied[b] = s_resid.after((y, 2, ch, t))
                            for k in range(2):
                                m = mm3(ps[:, b, :], both_parts((hid_hi, hid_lo), lambda r: r[:, 2 * j + k, P * t:P * t + P]),
                                        both_parts(w, lambda r: r[:, k, 512 * ch:512 * ch + 512]),
                                        j == 0 and k == 0, j == FC // 2 - 1 and k == 1)
                            m.then_inc(s_mm.sem, s_mm.nth((y, "down", j, ch, t)))
                    left((y, "down", j))

        @block.vector
        def _(dve):
            V = nc.vector

            def step(ins):
                ins.then_inc(s_dve_step.sem, s_dve_step.nth("latest"))
                dve.wait_ge(s_dve_step.sem, s_dve_step.count)

            def inverse(key, n):
                dve.wait_ge(s_root.sem, s_root.at(key))
                step(V.reciprocal(rstd[:, 0:n], rstd[:, 0:n]))

            def lo_part(dst, src, hi, key, wait_key):
                dve.wait_ge(s_hi.sem, s_hi.at(wait_key))
                V.tensor_tensor(dst, src, hi.bitcast(F32), ALU.subtract).then_inc(s_lo.sem, s_lo.nth(key))

            def attend(y, units, bufs, second):
                s_, p_, t_ = bufs
                for st in range(len(units) + 3):
                    i = st
                    if i < len(units):
                        u = units[i]
                        n = P * len(u["vs"])
                        dve.wait_ge(s_scores.sem, s_scores.at((y, i)))
                        if i >= 2:
                            dve.wait_ge(s_probs.sem, s_probs.at((y, i - 2)))
                        o0 = 1024 * (i % 2)
                        step(V.tensor_tensor_reduce(s_[:, i % 2, 0:n], ps_flat[:, o0:o0 + n], u["mask"], 1.0,
                                                    -3.0e38 if u["sink"] is None else u["sink"], ALU.add, ALU.max,
                                                    small[:, 0, i % 4:i % 4 + 1]))
                        V.tensor_scalar(small[:, 1, i % 4:i % 4 + 1], small[:, 0, i % 4:i % 4 + 1], -1.0, None, ALU.mult).then_inc(s_negm.sem, s_negm.nth((y, i)))
                    i = st - 2
                    if 0 <= i < len(units):
                        u = units[i]
                        a, d = halves(u)
                        if d:
                            dve.wait_ge(s_turned.sem, s_turned.at((y, i)))
                            if i >= 2:
                                dve.wait_ge(s_mixed.sem, s_mixed.at((y, i - 2)))
                            V.tensor_copy(t_[:, i % 2, P * a:P * (a + d)], ps[:, 5, 0:P * d]).then_inc(s_pt_dve.sem, s_pt_dve.nth((y, i)))
                        total, r = small[:, 2, i % 4:i % 4 + 1], small[:, 4, i % 4:i % 4 + 1]
                        dve.wait_ge(s_probs.sem, s_probs.at((y, i)))
                        if u["sink"] is not None:
                            dve.wait_ge(s_sink_exp.sem, s_sink_exp.at((y, i)))
                            step(V.tensor_tensor(total, total, small[:, 3, i % 4:i % 4 + 1], ALU.add))
                        step(V.reciprocal(r, total))
                        if u["second"]:
                            step(V.tensor_scalar(r, r, lam[:, 4:5], None, ALU.mult))
                    i = st - 3
                    if i >= 0:
                        u = units[i]
                        r = small[:, 4, i % 4:i % 4 + 1]
                        dve.wait_ge(s_mixed.sem, s_mixed.at((y, i)))
                        if u["second"]:
                            dve.wait_ge(s_o_out.sem, s_o_out.at((y, i - XT)))
                            V.scalar_tensor_tensor(u["out"], ps[:, 6, 0:HD], r, u["out"], ALU.mult, ALU.add).then_inc(s_o_out.sem, s_o_out.nth((y, i)))
                        else:
                            V.tensor_scalar(u["out"], ps[:, 6, 0:HD], r, None, ALU.mult).then_inc(s_o_out.sem, s_o_out.nth((y, i)))
                    if second:
                        second(st)

            dve.wait_ge(s_vec_mm.sem, s_vec_mm.at(0))
            V.tensor_copy(vec_t[:, 0:NV], ps[:, 7, 0:NV]).then_inc(s_vec_t.sem, s_vec_t.nth(0))
            dve.wait_ge(s_vec_t.sem, s_vec_t.at(0))
            dve.wait_ge(s_rr_mm.sem, s_rr_mm.at(0))
            V.tensor_copy(rr[:], ps_flat[0:A_HEADS + B_HEADS, 0:SEQ + P]).then_inc(s_rr.sem, s_rr.nth(0))

            def mods_out(l, a, b, key):
                dve.wait_ge(s_mod.sem, s_mod.at((l, "mod", b // 2 - 1)))
                for s in range(2):
                    p_ = ps[:, 7, 64 * l + 2 * a:64 * l + 2 * b].rearrange("p (c s) -> p s c", s=2)[:, s, :]
                    m = V.tensor_tensor(mod[:, s, a:b], p_, vec_t[:, VB[l]["b_mod"] + a:VB[l]["b_mod"] + b], ALU.add)
                    if s == 0:
                        step(m)
                m.then_inc(s_mod_out.sem, s_mod_out.nth(key))
                dve.wait_ge(s_mod_out.sem, s_mod_out.at(key))

            def scale_and_shift(l):
                g = vec_t[:, VB[l]["g_pre"]:VB[l]["g_pre"] + KD]
                for s in range(2):
                    step(V.scalar_tensor_tensor(mod_a[:, s, :], mod[:, s, KD:2 * KD], 1.0, g, ALU.add, ALU.mult))

            mods_out(0, 0, 16, (0, 0))
            scale_and_shift(0)
            for l in range(DEPTH):
                both = l < DEPTH - 1
                nt, nc_ = (NT, TOK) if both else (XT, SEQ)
                parts = 2 if both else 1
                dve.wait_ge(s_wf_mm.sem, s_wf_mm.at(l))
                V.tensor_copy(wf_m[:].rearrange("p i c n -> p (i c n)"), ps[:, 6, :]).then_inc(s_wf_m.sem, s_wf_m.nth(l))
                dve.wait_ge(s_ssq.sem, s_ssq.at((l, "pre", NT - 1)))
                V.tensor_scalar(ssq[:, 0:NT], ssq[:, 0:NT], 1.0 / D, EPS, ALU.mult, ALU.add).then_inc(s_var.sem, s_var.nth((l, "pre")))
                inverse((l, "pre"), NT)
                for t in range(NT):
                    src = res[:, t, :] if t < XT else res_c[:, t - XT, :]
                    V.tensor_scalar(xn[:, t, :], src, rstd[:, t:t + 1], None, ALU.mult).then_inc(s_xn.sem, s_xn.nth((l, t)))
                for k in range(KD + 1):
                    if k < KD:
                        dve.wait_ge(s_nt.sem, s_nt.at((l, k)))
                        if k >= 2:
                            dve.wait_ge(s_lo.sem, s_lo.at((l, "n", k - 2)))
                        step(V.tensor_scalar(tmp_n[:, k % 2, 0:SEQ], ps[:, k % 4, :], mod_a[:, 0, k:k + 1], mod[:, 0, k:k + 1], ALU.mult, ALU.add))
                        V.tensor_scalar(tmp_n[:, k % 2, SEQ:], ps[:, 4 + k % 2, 0:CTX], mod_a[:, 1, k:k + 1], mod[:, 1, k:k + 1],
                                              ALU.mult, ALU.add).then_inc(s_mod_x.sem, s_mod_x.nth((l, k)))
                    if k > 0:
                        lo_part(h_lo[:, k - 1, :], tmp_n[:, (k - 1) % 2, :], h_hi[:, k - 1, :], (l, "n", k - 1), (l, "n", k - 1))
                for g in range(nt // 2):
                    dve.wait_ge(s_uf_hi.sem, s_uf_hi.at((l, g)))
                    V.tensor_tensor(uf_lo[:, 2 * g:2 * g + 2, :].rearrange("p t c -> p (t c)"), ps[:, (6, 7, 5)[g], :],
                                          uf_hi[:, 2 * g:2 * g + 2, :].rearrange("p t c -> p (t c)").bitcast(F32), ALU.subtract).then_inc(s_uf_lo.sem, s_uf_lo.nth((l, g)))
                for i in range(5):
                    x_ = q1[:, i, 0:SEQ] if i < 4 else k1[:, 0:SEQ]
                    dve.wait_ge(s_rot.sem, s_rot.at((l, i)))
                    step(V.tensor_tensor(tmp_p[:, i % 2, 0:SEQ], ps[:, 6 + i % 2, :], sin1[:], ALU.mult))
                    step(V.tensor_tensor(x_, x_, cos1[:], ALU.mult))
                    V.tensor_tensor(x_, x_, tmp_p[:, i % 2, 0:SEQ], ALU.add).then_inc(s_roped.sem, s_roped.nth((l, i)))
                n_fm = 5 + 6
                for c in range(2):
                    for part in range(parts):
                        b, n, a = (n_fm % 4, SEQ, 0) if part == 0 else (4 + n_fm % 2, CTX, SEQ)
                        dve.wait_ge(s_mm.sem, s_mm.at((l, ("cc",), c, part)))
                        dve.wait_ge(s_proj.sem, s_proj.at((l, ("zc",), c, part)))
                        V.tensor_tensor(cz[:, c, a:a + n], ps[:, b, 0:n], cz[:, c, a:a + n], ALU.mult).then_inc(s_conv_t.sem, s_conv_t.nth((l, ("cc",), c, part)))
                    n_fm += 1
                for c in range(2):
                    dve.wait_ge(s_proj.sem, s_proj.at((l, ("gc",), c, parts - 1)))
                    V.tensor_tensor(cb[:, c, 0:nc_], cb[:, c, 0:nc_], tmp_p[:, c, 0:nc_], ALU.mult).then_inc(s_conv_gate.sem, s_conv_gate.nth((l, c)))
                dve.wait_ge(s_conv_gate.sem, s_conv_gate.at((l, 1)))
                dve.wait_ge(s_mm.sem, s_mm.at((l, ("ga", 1), 1, parts - 1)))
                cw, bias = VB[l]["conv_w"], VB[l]["conv_b"]
                for c in range(2):
                    tap = [vec_t[:, cw + 2 * j + c:cw + 2 * j + c + 1] for j in range(3)]
                    for part in range(parts):
                        a, n = (0, SEQ) if part == 0 else (SEQ, CTX)
                        z, o = cz[:, c, a:a + n], conv_y[:, c, a:a + n]
                        step(V.tensor_scalar(o, z, tap[1], vec_t[:, bias + c:bias + c + 1], ALU.mult, ALU.add))
                        step(V.scalar_tensor_tensor(o[:, 1:n], z[:, 0:n - 1], tap[0], o[:, 1:n], ALU.mult, ALU.add))
                        step(V.scalar_tensor_tensor(o[:, 0:n - 1], z[:, 1:n], tap[2], o[:, 0:n - 1], ALU.mult, ALU.add))
                    V.tensor_tensor(cb[:, c, 0:nc_], cb[:, c, 0:nc_], conv_y[:, c, 0:nc_], ALU.mult).then_inc(s_side.sem, s_side.nth((l, 2 + c)))
                for c in range(2):
                    for part in range(parts):
                        b, n, a = (6 + c, SEQ, 0) if part == 0 else (4 + c, CTX, SEQ)
                        dve.wait_ge(s_fmix.sem, s_fmix.at((l, c, part)))
                        V.tensor_tensor(gf[:, c, a:a + n], ps[:, b, 0:n], gf[:, c, a:a + n], ALU.mult).then_inc(s_side.sem, s_side.nth((l, c)))
                attend(l, units1(l), BUF[0], None)
                for t in range(nt + 1):
                    if t < nt:
                        dve.wait_ge(s_aot.sem, s_aot.at((l, t)))
                        if t >= 2:
                            dve.wait_ge(s_lo.sem, s_lo.at((l, "m", t - 2)))
                        V.tensor_tensor(tmp_m[:, t % 2, :].rearrange("p (c n) -> p c n", c=4),
                                              ps[:, t % 4, :].rearrange("p (c n) -> p c n", c=4), ga[:, :, P * t:P * t + P], ALU.mult).then_inc(s_gated.sem, s_gated.nth((l, t)))
                    if t > 0:
                        lo_part(h_lo[:, 0:4, P * (t - 1):P * t], tmp_m[:, (t - 1) % 2, :].rearrange("p (c n) -> p c n", c=4),
                                h_hi[:, 0:4, P * (t - 1):P * t], (l, "m", t - 1), (l, "m", t - 1))
                for c in range(4):
                    src = gf[:, c, 0:nc_] if c < 2 else cb[:, c - 2, 0:nc_]
                    lo_part(h_lo[:, 4 + c, 0:nc_], src, h_hi[:, 4 + c, 0:nc_], (l, "s", c), (l, "s", c))
                if l + 1 < DEPTH:
                    mods_out(l + 1, 0, 16, (l + 1, 0))
                    scale_and_shift(l + 1)
                mods_out(l, 16, 24, (l, 1))
                dve.wait_ge(s_lo.sem, s_lo.at((l, "s", 3)))
                for s in range(parts):
                    step(V.tensor_tensor(mod_g[:, s, :], mod[:, s, 16:24], vec_t[:, VB[l]["g_post"]:VB[l]["g_post"] + KD], ALU.mult))
                    for c in range(KD):
                        m = V.tensor_scalar(diag[:, s, c, :], ident[:], mod_g[:, s, c:c + 1], None, ALU.mult).then_inc(s_diag.sem, s_diag.nth((l, s)))
                dve.wait_ge(s_ssq.sem, s_ssq.at((l, "post", nt - 1)))
                V.tensor_scalar(ssq[:, 0:nt], ssq[:, 0:nt], 1.0 / D, EPS, ALU.mult, ALU.add).then_inc(s_var.sem, s_var.nth((l, "post")))
                inverse((l, "post"), nt)
                for t in range(nt):
                    s = 0 if t < XT else 1
                    x_ = res[:, t, :] if t < XT else res_c[:, t - XT, :]
                    dve.wait_ge(s_gate_b.sem, s_gate_b.at((l, s)))
                    step(V.scalar_tensor_tensor(y1[:, t, :], y1[:, t, :], rstd[:, t:t + 1], gate_b[:, s, :], ALU.mult, ALU.mult))
                    V.tensor_tensor(x_, x_, y1[:, t, :], ALU.add).then_inc(s_x_final.sem, s_x_final.nth((l, t)))

            for l in range(DEPTH):
                y = DEPTH + l
                for k in range(KD):
                    lo_part(g_lo[:, k, :], ps[:, k % 4, :], g_hi[:, k, :], (y, "t", k), (y, "t", k))
                dve.wait_ge(s_layer_consts.sem, s_layer_consts.at(y))
                for i in range(2):
                    m = V.tensor_tensor_reduce(dlam[:, 64 * i:64 * i + 32], dlam[:, 64 * i:64 * i + 32], dlam[:, 64 * i + 32:64 * i + 64],
                                               1.0, 0.0, ALU.mult, ALU.add, lam[:, i:i + 1])
                    if i == 0:
                        step(m)
                m.then_inc(s_lam_sums.sem, s_lam_sums.nth(y))
                dve.wait_ge(s_lam_exp.sem, s_lam_exp.at(y))
                step(V.scalar_tensor_tensor(lam[:, 4:5], lam[:, 3:4], lam[:, 2:3], lam_c[:, 0:1], ALU.subtract, ALU.add))
                dve.wait_ge(s_ssq.sem, s_ssq.at((y, "c", 7)))
                step(V.tensor_scalar(ssq[:, 0:4], ssq[:, 0:4], 1.0 / 256, EPS, ALU.mult, ALU.add))
                V.tensor_scalar(ssq[:, 4:8], ssq[:, 4:8], 1.0 / 128, EPS, ALU.mult, ALU.add).then_inc(s_var.sem, s_var.nth((y, "c")))
                inverse((y, "c"), 8)
                for t in range(XT):
                    step(V.tensor_scalar(c_in[:, t, 0:256], c_in[:, t, 0:256], rstd[:, t:t + 1], None, ALU.mult))
                    V.tensor_scalar(c_in[:, t, 256:384], c_in[:, t, 256:384], rstd[:, 4 + t:5 + t], None, ALU.mult).then_inc(s_latn.sem, s_latn.nth((y, t)))
                for i in range(3):
                    dve.wait_ge(s_lat_t.sem, s_lat_t.at((y, i)))
                    gain = LG + 2 * l + i if i < 2 else LG + 4 + l
                    V.tensor_scalar(tmp_c[:, i % 2, :], ps[:, i, :], vec_t[:, gain:gain + 1], None, ALU.mult).then_inc(s_lat.sem, s_lat.nth((y, i)))
                    dve.wait_ge(s_lat.sem, s_lat.at((y, i)))
                    hi, lo = (cq_hi[:, i, :], cq_lo[:, i, :]) if i < 2 else (ckv_hi[:], ckv_lo[:])
                    lo_part(lo, tmp_c[:, i % 2, :], hi, (y, "c", i), (y, "c", i))
                dve.wait_ge(s_lo.sem, s_lo.at((y, "c", 2)))
                R = slice(HD, QC)

                def rope(x_, bank, slot):
                    step(V.tensor_tensor(tmp_c[R, slot, :], ps[R, bank, :], sin2[R, :], ALU.mult))
                    step(V.tensor_tensor(x_, x_, cos2[R, :], ALU.mult))
                    return V.tensor_tensor(x_, x_, tmp_c[R, slot, :], ALU.add)

                dve.wait_ge(s_lat_t.sem, s_lat_t.at((y, 3)))
                V.tensor_copy(kc[R, 0, :], ps[R, 3, :]).then_inc(s_kr_raw.sem, s_kr_raw.nth(y))
                dve.wait_ge(s_kr_rot.sem, s_kr_rot.at(y))
                step(rope(kc[R, 0, :], 5, 0))
                for h in range(1, C_HEADS):
                    m = V.tensor_copy(kc[R, h, :], kc[R, 0, :]).then_inc(s_kr_all.sem, s_kr_all.nth(y))
                for h in range(C_HEADS):
                    dve.wait_ge(s_q_rot.sem, s_q_rot.at((y, h)))
                    rope(qc[R, h, :], 6 + h % 2, h % 2).then_inc(s_roped.sem, s_roped.nth((y, h)))
                dve.wait_ge(s_strips.sem, s_strips.at(y))

                def sub_norm(st):
                    o = ao2[:, :, 384:640].rearrange("p t (h d) -> p t h d", d=HD)
                    sq = sq_b[:].rearrange("p (t h) d -> p t h d", t=XT)
                    if st == N_B + 2:
                        dve.wait_ge(s_o_out.sem, s_o_out.at((y, N_B - 1)))
                        step(V.tensor_tensor(sq, o, o, ALU.mult))
                        step(V.tensor_reduce(ssq[:, 0:16], sq_b[:], AX_X, ALU.add))
                        V.tensor_scalar(ssq[:, 0:16], ssq[:, 0:16], 1.0 / HD, 1e-5, ALU.mult, ALU.add).then_inc(s_var.sem, s_var.nth((y, "sub")))
                    if st == N_B + 8:
                        inverse((y, "sub"), 16)
                        step(V.tensor_scalar(rstd[:, 0:16], rstd[:, 0:16], lam_c[:, 1:2], None, ALU.mult))
                        r = rstd[:, 0:16].rearrange("p (t h) -> p t h", t=XT).unsqueeze(3).broadcast_to((P, XT, B_HEADS, HD))
                        g = subln[:].unsqueeze(1).unsqueeze(1).broadcast_to((P, XT, B_HEADS, HD))
                        step(V.tensor_tensor(o, o, r, ALU.mult))
                        V.tensor_tensor(o, o, g, ALU.mult).then_inc(s_sub.sem, s_sub.nth(y))

                attend(y, units2(), BUF[1], sub_norm)
                for t in range(XT):
                    for g in range(2):
                        lo_part(g_lo[:, 4 * g:4 * g + 4, P * t:P * t + P], ps[:, 2 * (t % 2) + g, :].rearrange("p (c n) -> p c n", c=4),
                                g_hi[:, 4 * g:4 * g + 4, P * t:P * t + P], (y, "m", t, g), (y, "m", t, g))

                def residual(n, ch, t, key, bank):
                    dve.wait_ge(s_mm.sem, s_mm.at(key))
                    x_ = res[:, t, 512 * ch:512 * ch + 512]
                    V.scalar_tensor_tensor(x_, x_, ALPHA, ps[:, bank, :], ALU.mult, ALU.add).then_inc(s_resid.sem, s_resid.nth((y, n, ch, t)))
                    dve.wait_ge(s_resid.sem, s_resid.at((y, n, ch, t)))
                    step(V.bn_stats(bn[:, t, ch, :], x_))

                def norm(n, w, done):
                    for t in range(XT):
                        step(V.bn_aggr(mean_var[:, t, :], bn[:, t, :, :].rearrange("p c s -> p (c s)")))
                    V.tensor_scalar(ssq[:, 0:XT], mean_var[:, :, 1], LN_EPS, None, ALU.add).then_inc(s_var.sem, s_var.nth((y, n)))
                    inverse((y, n), XT)
                    dve.wait_ge(s_ln.sem, s_ln.at((y, n)))
                    for t in range(XT):
                        step(V.tensor_scalar(res[:, t, :], res[:, t, :], mean_var[:, t, 0:1], rstd[:, t:t + 1], ALU.subtract, ALU.mult))
                        step(V.tensor_tensor(res[:, t, :], res[:, t, :], w[:, 0, :], ALU.mult))
                        V.tensor_tensor(res[:, t, :], res[:, t, :], w[:, 1, :], ALU.add).then_inc(done.sem, done.nth((y, t)))

                for ch in range(2):
                    for t in range(XT):
                        residual(1, ch, t, (y, "o", ch, t), 4 * ch + t)
                norm(1, ln1, s_normed)
                for k in range(KD):
                    lo_part(g_lo[:, k, :], ps[:, k % 4, :], g_hi[:, k, :], (y, "h", k), (y, "h", k))
                for j in range(FC):
                    dve.wait_ge(s_silu.sem, s_silu.at((y, j)))
                    dve.wait_ge(s_mm.sem, s_mm.at((y, "ffup", j)))
                    V.tensor_tensor(tmp_f[:, 2 + j % 2, :], ps[:, 2 * (j % 3) + 1, :], tmp_f[:, j % 2, :], ALU.mult).then_inc(s_glu.sem, s_glu.nth((y, j)))
                    dve.wait_ge(s_glu.sem, s_glu.at((y, j)))
                    lo_part(hid_lo[:, j, :], tmp_f[:, 2 + j % 2, :], hid_hi[:, j, :], (y, "f", j), (y, "f", j))
                for t in range(XT):
                    for ch in range(2):
                        residual(2, ch, t, (y, "down", FC // 2 - 1, ch, t), 2 * t + ch)
                norm(2, ln2, s_x_final)


_INS = ["x", "c", "ctx", "c_ctx", "w_mod", "b_mod", "g_pre", "g_post", "w_in", "w_out", "sink", "w_fourier",
        "conv_w", "conv_b", "rel_bias_2", "w_in_2", "q_norm_g_2", "kv_norm_g_2", "w_uq_2", "w_ukv_2",
        "diff_lambda_2", "subln_g_2", "w_o_2", "ln1_g_2", "ln1_b_2", "ln2_g_2", "ln2_b_2", "w_gate_2", "w_up_2", "w_down_2"]


def kernel(**inputs):
    import concourse.bacc as bacc
    from concourse.bass_utils import run_bass_kernel_spmd

    arrays = {f"in_{n}": np.ascontiguousarray(inputs[n]) for n in _INS}
    arrays.update({f"in_{n}": np.ascontiguousarray(a) for n, a in _constants().items()})
    seen = {}
    for _ in range(2):
        nc = bacc.Bacc("TRN2", target_bir_lowering=False, num_devices=1)
        aps = {n[3:]: nc.dram_tensor(n, a.shape, F32, kind="ExternalInput").ap() for n, a in arrays.items()}
        y = nc.dram_tensor("y", (1, SEQ, D), F32, kind="ExternalOutput").ap()
        _program(nc, aps, y, seen)
    return run_bass_kernel_spmd(nc, [arrays], core_ids=[0]).results[0]["y"]
```

```python
from contextlib import ExitStack

import numpy as np

import concourse.bass as bass
from concourse import mybir

F32 = mybir.dt.float32
F32R = mybir.dt.float32r
ALU = mybir.AluOpType
ACT = mybir.ActivationFunctionType
AX_X = mybir.AxisListType.X

P = 128
D = 1024
KD = D // P
SEQ, CTX, DEPTH = 512, 256, 2
XT, CT = SEQ // P, CTX // P
TOK = SEQ + CTX
NT = XT + CT
HD = 64
EPS = 1e-6
HEADS, KVH = 8, 2
FF = 2816
FC = FF // P
A_HEADS, B_HEADS, C_HEADS = 6, 4, 6
BUCKETS = 32
ALPHA = (2 * DEPTH) ** 0.25
LN_EPS = 1e-5
FAR = 1.0e30
RAW, SPLIT = 3, 2
TILE = 2048
ROPE = 32
QC = HD + ROPE


class Signal:

    def __init__(self, nc, ctx, seen, name):
        self.sem = ctx.enter_context(nc.semaphore(name))
        self.seen = seen.setdefault(name, {})
        self.count = 0

    def nth(self, key, by=1):
        self.count += by
        self.seen[key] = self.count
        return by

    def name_latest(self, key):
        self.seen[key] = self.count

    def at(self, key):
        return self.seen.get(key, 1)

    def after(self, key):
        return self.sem, self.at(key)


def _constants():
    f = np.float32
    c = {}
    c["ident"] = np.eye(P, dtype=f)
    pos = np.arange(SEQ)
    inv = np.power(f(10000.0), -np.arange(16, dtype=f) / f(16)).astype(f)
    ang = np.stack([(pos // 64).astype(f)[:, None] * inv, (pos % 64).astype(f)[:, None] * inv], 1)
    rows = np.arange(P)
    axis, freq = (rows % 64) // 32, rows % 16
    c["cos1"] = np.ascontiguousarray(np.cos(ang)[:, axis, freq].T.astype(f))
    c["sin1"] = np.ascontiguousarray(np.sin(ang)[:, axis, freq].T.astype(f))

    def rotation(n, half):
        r = np.zeros((n, n), f)
        for i in range(n):
            first = (i % (2 * half)) < half
            r[i + half if first else i - half, i] = -1.0 if first else 1.0
        return r

    c["rot1"] = rotation(P, 16)
    inv2 = np.power(f(10000.0), -np.arange(16, dtype=f) / f(16)).astype(f)
    ang2 = pos.astype(f)[:, None] * inv2
    c["cos2"] = np.ascontiguousarray(np.tile(np.cos(ang2).T, (2, 1)).astype(f))
    c["sin2"] = np.ascontiguousarray(np.tile(np.sin(ang2).T, (2, 1)).astype(f))
    rot2 = np.zeros((ROPE, QC), f)
    rot2[:, HD:] = rotation(ROPE, 16)
    c["rot2"] = rot2
    q, k = np.arange(P)[:, None], np.arange(3 * P)[None, :] - P
    band = np.where(np.abs(q - k) <= P, 0.0, FAR).astype(f)
    c["band_mid"] = np.concatenate([band, np.zeros((P, CTX), f)], 1)
    c["band_last"] = np.concatenate([band[:, :2 * P], np.zeros((P, CTX), f)], 1)
    for n in (SEQ, CTX):
        t = np.outer(np.arange(n), np.arange(n)) % n * (2 * np.pi / n)
        c[f"dft_cos{n}"] = (np.cos(t) / np.sqrt(n)).astype(f)
        c[f"dft_sin{n}"] = (np.sin(t) / np.sqrt(n)).astype(f)
    t = np.outer(np.arange(HD), np.arange(HD)) % HD * (2 * np.pi / HD)
    two = np.eye(2)
    c["dft_ccos"] = np.kron(two, np.cos(t) / 8.0).astype(f)
    c["dft_csin"] = np.kron(two, -np.sin(t) / 8.0).astype(f)
    dist = SEQ - 1 - np.arange(SEQ + P)
    df = np.maximum(dist, 1).astype(f)
    large = 16 + (np.log(df / f(16)) / f(np.log(2048 / 16)) * f(16)).astype(np.int32)
    bucket = np.where(dist < 16, np.maximum(dist, 0), np.minimum(large, BUCKETS - 1))
    hot = np.zeros((BUCKETS + 2, SEQ + P), f)
    hot[bucket, np.arange(SEQ + P)] = (dist >= 0)
    times = (dist <= P).astype(int) + (dist % 4 == 0) + (dist % 16 == 0)
    ok = dist >= 0
    hot[BUCKETS] = np.where(ok & (times > 0), np.log(np.maximum(times, 1)), -FAR)
    hot[BUCKETS + 1] = np.where(ok, 0.0, -FAR)
    c["hot"] = hot
    pick = np.zeros((2, A_HEADS + B_HEADS), f)
    pick[0, :A_HEADS] = 1.0
    pick[1, A_HEADS:] = 1.0
    c["pick"] = pick
    c["fold"] = np.tile(np.eye(2, dtype=f), (2, 1))
    d2 = 384 + np.arange(P)[:, None] - np.arange(SEQ)[None, :]
    c["causal"] = np.where(d2 >= 0, 0.0, FAR).astype(f)
    init = [0.8 - 0.6 * np.exp(-0.3 * l) for l in range(DEPTH)]
    c["lam_init"] = np.array([[-i, 1.0 - i] for i in init], f)
    return c


def _program(nc, I, out, seen):
    ctx = ExitStack()
    with ctx:
        base = -(-nc.sbuf_base // 64) * 64
        names = {}

        def at(name, shape, off, dt=F32):
            n = 4 * int(np.prod(shape[1:]))
            assert base + off + n <= nc.sbuf_usable_end, (name, off, n)
            names[name] = (off, n)
            return nc.alloc_sbuf_tensor_at(name, shape, dt, offset=base + off)

        off = 0

        def put(name, shape, dt=F32):
            nonlocal off
            t = at(name, shape, off, dt)
            off += -(-4 * int(np.prod(shape[1:])) // 32) * 32
            return t

        raw = put("raw", [P, RAW, TILE])
        w_hi = put("w_hi", [P, SPLIT, TILE], F32R)
        w_lo = put("w_lo", [P, SPLIT, TILE], F32R)
        ident = put("ident", [P, P])
        ones = put("ones", [P, P])
        rot1 = put("rot1", [P, P])
        rot2 = put("rot2", [P, QC])
        vec = put("vec", [P, P])
        vec_t = put("vec_t", [P, P])
        cond = put("cond", [P, KD, 2])
        cond_hl = put("cond_hl", [P, KD, 4], F32R)
        mod = put("mod", [P, 2, 24])
        mod_a = put("mod_a", [P, 2, KD])
        mod_g = put("mod_g", [P, 2, KD])
        ssq = put("ssq", [P, 16])
        rstd = put("rstd", [P, 16])
        mean_var = put("mean_var", [P, XT, 2])
        bn = put("bn", [P, XT, 2, 6])
        small = put("small", [P, 3, 8])
        sinks = put("sinks", [P, DEPTH * HEADS])
        lam_c = put("lam_c", [P, 2])
        lam = put("lam", [P, 8])
        table = put("table", [BUCKETS + 2, A_HEADS + B_HEADS])
        res = put("res", [P, XT, D])
        res_c_at = off
        res_c = put("res_c", [P, CT, D])
        ph = off
        h_hi = put("h_hi", [P, KD, TOK], F32R)
        h_lo = put("h_lo", [P, KD, TOK], F32R)
        mix_at = off
        q1 = put("q1", [P, 4, TOK])
        k1 = put("k1", [P, TOK])
        ga = put("ga", [P, 4, TOK])
        gf = put("gf", [P, 2, TOK])
        cz = put("cz", [P, 2, TOK])
        cb = put("cb", [P, 2, TOK])
        v1 = put("v1", [P, NT, P])
        uf_at = off
        uf_hi = put("uf_hi", [P, NT, 256], F32R)
        uf_lo = put("uf_lo", [P, NT, 256], F32R)
        cos1 = put("cos1", [P, SEQ])
        sin1 = put("sin1", [P, SEQ])
        band_mid = put("band_mid", [P, 5 * P])
        band_last = put("band_last", [P, 4 * P])
        dft_ccos = put("dft_ccos", [P, P])
        dft_csin = put("dft_csin", [P, P])
        wf = put("wf", [P, DEPTH, 2, P])
        wf_m = put("wf_m", [P, 2, 2, P])
        mod_row = put("mod_row", [4, 2, 256])
        fold = put("fold", [4, 2])
        xn = at("xn", [P, NT, D], mix_at)
        tmp_n = at("tmp_n", [P, 2, TOK], names["cz"][0])
        tmp_p = at("tmp_p", [P, 2, TOK], names["ga"][0])
        four = at("four", [P, 2, 2, TOK], names["h_lo"][0])
        conv_y = at("conv_y", [P, 2, TOK], names["h_lo"][0] + 4 * 4 * TOK)
        sc = at("sc", [P, 4, 5 * P + 8], names["h_hi"][0])
        pt = at("pt", [P, 2, 5 * P], names["h_hi"][0] + 16 * (5 * P + 8))
        ao1 = at("ao1", [P, NT, 512], uf_at)
        tmp_m = at("tmp_m", [P, 2, 512], names["q1"][0])
        y1 = at("y1", [P, NT, D], mix_at)
        gate_b = at("gate_b", [P, 2, D], names["gf"][0])
        diag = at("diag", [P, 2, KD, P], names["gf"][0] + 8 * D)
        assert names["ga"][0] + names["ga"][1] - mix_at >= 4 * NT * D
        assert names["cb"][0] + names["cb"][1] - names["gf"][0] >= 16 * D
        off = res_c_at
        g_hi = put("g_hi", [P, KD, SEQ], F32R)
        g_lo = put("g_lo", [P, KD, SEQ], F32R)
        ao2 = put("ao2", [P, XT, D])
        att_at = off
        qa = put("qa", [P, 3, SEQ])
        ka = put("ka", [P, 3, SEQ])
        va = put("va", [P, XT, 384])
        qb = put("qb", [P, 2, SEQ])
        kb = put("kb", [P, 2, SEQ])
        vb = put("vb", [P, XT, 256])
        qc = put("qc", [P, C_HEADS, SEQ])
        kc = put("kc", [P, C_HEADS, SEQ])
        vc = put("vc", [P, XT, 384])
        strip_at = off
        strips = put("strips", [P, 11, SEQ])
        off = strip_at
        c_in = put("c_in", [P, XT, 416])
        cq_hi = put("cq_hi", [P, 2, SEQ], F32R)
        cq_lo = put("cq_lo", [P, 2, SEQ], F32R)
        ckv_hi = put("ckv_hi", [P, SEQ], F32R)
        ckv_lo = put("ckv_lo", [P, SEQ], F32R)
        cos2 = put("cos2", [P, SEQ])
        sin2 = put("sin2", [P, SEQ])
        subln = put("subln", [P, HD])
        dlam = put("dlam", [P, 4 * 32])
        tmp_c = at("tmp_c", [P, 2, SEQ], names["ao2"][0])
        sc2 = at("sc2", [P, 4, SEQ], names["g_hi"][0])
        pt2 = at("pt2", [P, 2, SEQ], names["g_lo"][0])
        sq_b = at("sq_b", [P, 16, HD], names["g_lo"][0] + 8 * SEQ)
        ln1 = at("ln1", [P, 2, D], att_at)
        ln2 = at("ln2", [P, 2, D], names["g_lo"][0])
        off = names["ao2"][0] + 4 * 4 * SEQ
        hid_hi = put("hid_hi", [P, FC, SEQ], F32R)
        hid_lo = put("hid_lo", [P, FC, SEQ], F32R)
        tmp_f = at("tmp_f", [P, 4, SEQ], names["ao2"][0])
        rr = at("rr", [A_HEADS + B_HEADS, SEQ + P], uf_at)
        hot = at("hot", [BUCKETS + 2, SEQ + P], uf_at + 4 * (SEQ + P))
        junk = at("junk", [P, D], uf_at)

        ps = ctx.enter_context(nc.psum_tensor("ps", [P, 8, 512], F32))
        ps_flat = ps[:].rearrange("p b n -> p (b n)")
        scratch = nc.dram_tensor("bias_rows", [A_HEADS + B_HEADS, P * (SEQ + P)], F32).ap()

        s_aot = Signal(nc, ctx, seen, "aot")
        s_bias_rows = Signal(nc, ctx, seen, "bias_rows")
        s_cond = Signal(nc, ctx, seen, "cond")
        s_cond_hi = Signal(nc, ctx, seen, "cond_hi")
        s_cond_lo = Signal(nc, ctx, seen, "cond_lo")
        s_consts = Signal(nc, ctx, seen, "consts")
        s_conv_gate = Signal(nc, ctx, seen, "conv_gate")
        s_conv_t = Signal(nc, ctx, seen, "conv_t")
        s_diag = Signal(nc, ctx, seen, "diag")
        s_dve_step = Signal(nc, ctx, seen, "dve_step")
        s_fmix = Signal(nc, ctx, seen, "fmix")
        s_four_out = Signal(nc, ctx, seen, "four_out")
        s_gate_b = Signal(nc, ctx, seen, "gate_b")
        s_gate_mm = Signal(nc, ctx, seen, "gate_mm")
        s_gated = Signal(nc, ctx, seen, "gated")
        s_glu = Signal(nc, ctx, seen, "glu")
        s_hi = Signal(nc, ctx, seen, "hi")
        s_ht = Signal(nc, ctx, seen, "ht")
        s_kr_all = Signal(nc, ctx, seen, "kr_all")
        s_kr_raw = Signal(nc, ctx, seen, "kr_raw")
        s_kr_rot = Signal(nc, ctx, seen, "kr_rot")
        s_lam_exp = Signal(nc, ctx, seen, "lam_exp")
        s_lam_sums = Signal(nc, ctx, seen, "lam_sums")
        s_lat = Signal(nc, ctx, seen, "lat")
        s_lat_t = Signal(nc, ctx, seen, "lat_t")
        s_latn = Signal(nc, ctx, seen, "latn")
        s_layer_consts = Signal(nc, ctx, seen, "layer_consts")
        s_ln = Signal(nc, ctx, seen, "ln")
        s_lo = Signal(nc, ctx, seen, "lo")
        s_mixed = Signal(nc, ctx, seen, "mixed")
        s_mm = Signal(nc, ctx, seen, "mm")
        s_mod = Signal(nc, ctx, seen, "mod")
        s_mod_out = Signal(nc, ctx, seen, "mod_out")
        s_mod_row = Signal(nc, ctx, seen, "mod_row")
        s_mod_x = Signal(nc, ctx, seen, "mod_x")
        s_normed = Signal(nc, ctx, seen, "normed")
        s_nt = Signal(nc, ctx, seen, "nt")
        s_o_out = Signal(nc, ctx, seen, "o_out")
        s_ones = Signal(nc, ctx, seen, "ones")
        s_probs = Signal(nc, ctx, seen, "probs")
        s_proj = Signal(nc, ctx, seen, "proj")
        s_pt = Signal(nc, ctx, seen, "pt")
        s_q_rot = Signal(nc, ctx, seen, "q_rot")
        s_recip = Signal(nc, ctx, seen, "recip")
        s_resid = Signal(nc, ctx, seen, "resid")
        s_root = Signal(nc, ctx, seen, "root")
        s_roped = Signal(nc, ctx, seen, "roped")
        s_rot = Signal(nc, ctx, seen, "rot")
        s_rr = Signal(nc, ctx, seen, "rr")
        s_rr_mm = Signal(nc, ctx, seen, "rr_mm")
        s_scored = Signal(nc, ctx, seen, "scored")
        s_scores = Signal(nc, ctx, seen, "scores")
        s_side = Signal(nc, ctx, seen, "side")
        s_silu = Signal(nc, ctx, seen, "silu")
        s_ssq = Signal(nc, ctx, seen, "ssq")
        s_stored = Signal(nc, ctx, seen, "stored")
        s_strips = Signal(nc, ctx, seen, "strips")
        s_sub = Signal(nc, ctx, seen, "sub")
        s_tile_hi = Signal(nc, ctx, seen, "tile_hi")
        s_tile_lo = Signal(nc, ctx, seen, "tile_lo")
        s_turned = Signal(nc, ctx, seen, "turned")
        s_uf_hi = Signal(nc, ctx, seen, "uf_hi")
        s_uf_lo = Signal(nc, ctx, seen, "uf_lo")
        s_var = Signal(nc, ctx, seen, "var")
        s_vec_mm = Signal(nc, ctx, seen, "vec_mm")
        s_vec_t = Signal(nc, ctx, seen, "vec_t")
        s_vectors = Signal(nc, ctx, seen, "vectors")
        s_wf_landed = Signal(nc, ctx, seen, "wf_landed")
        s_wf_m = Signal(nc, ctx, seen, "wf_m")
        s_wf_mm = Signal(nc, ctx, seen, "wf_mm")
        s_wf_zero = Signal(nc, ctx, seen, "wf_zero")
        s_x_final = Signal(nc, ctx, seen, "x_final")
        s_x_landed = Signal(nc, ctx, seen, "x_landed")
        s_xn = Signal(nc, ctx, seen, "xn")
        s_xt = Signal(nc, ctx, seen, "xt")
        s_y = Signal(nc, ctx, seen, "y")

        def cols(w, a, b):
            return w[:, a:b].rearrange("(k p) c -> p k c", p=P)

        def mod_tile(l, j):
            return ((l, "mod", j), [(lambda r: r.rearrange("p (k c) -> p k c", k=KD),
                                     cols(I["w_mod"][l], 256 * j, 256 * j + 256))], True)

        def mix_tiles(l):
            t = []

            def proj(what, parts):
                t.append(((l, *what), [(lambda r, o=o, n=n: r.rearrange("p (k c) -> p k c", k=KD)[:, :, o:o + n],
                                        cols(I["w_in"][l], a, a + n)) for o, a, n in parts], True))

            for j in range(2):
                proj(("q", j), [(HD * i, HD * h, HD) for i, h in enumerate((2 * j, 2 * j + 4, 2 * j + 1, 2 * j + 5))])
            proj(("kv",), [(0, 512, 256)])
            for what, a in (("uf", 1280), ("gf", 1536), ("zc", 1792), ("bc", 2048), ("cc", 2304), ("gc", 2560)):
                proj((what,), [(0, a, 256)])
            for j in range(2):
                proj(("ga", j), [(0, 768 + 256 * j, 256)])
            for part in ("cos", "sin"):
                t.append(((l, "dft", part), [(lambda r: r.rearrange("p (k c) -> p k c", k=XT),
                                              I[f"dft_{part}{SEQ}"].rearrange("(k p) c -> p k c", p=P))], True))
            if l < DEPTH - 1:
                t.append(((l, "dft", "ctx"), [
                    (lambda r, i=i: r[:, 512 * i:512 * i + 512].rearrange("p (k c) -> p k c", k=CT),
                     I[f"dft_{part}{CTX}"].rearrange("(k p) c -> p k c", p=P))
                    for i, part in enumerate(("cos", "sin"))], True))
            return t

        def square(w, ch, kh):
            return (lambda r: r.rearrange("p (k c) -> p k c", k=4),
                    w[512 * kh:512 * kh + 512, 512 * ch:512 * ch + 512].rearrange("(k p) c -> p k c", p=P))

        SECOND = ([("c", 0, 1920, 256), ("c", 1, 2176, 160)] + [("a", j, 256 * j, 256) for j in range(3)]
                  + [("av", 0, 768, 256), ("av", 1, 1024, 128), ("up",),
                     ("bq", 0, 1152, 256), ("bk", 0, 1408, 256), ("bv", 0, 1664, 256)])

        def second_tiles(l):
            y = DEPTH + l
            t = []
            for what, *cut in SECOND:
                if what == "up":
                    t.append(((y, "up"), [
                        (lambda r: r[:, 0:2 * 576].rearrange("p (k c) -> p k c", k=2),
                         I["w_uq_2"][l].rearrange("(k p) c -> p k c", p=P)),
                        (lambda r: r[:, 1152:1152 + 768], I["w_ukv_2"][l])], True))
                else:
                    j, a, n = cut
                    t.append(((y, what, j), [(lambda r, n=n: r[:, 0:KD * n].rearrange("p (k c) -> p k c", k=KD),
                                              cols(I["w_in_2"][l], a, a + n))], True))
            for ch in range(2):
                for kh in range(2):
                    t.append(((y, "o", ch, kh), [square(I["w_o_2"][l], ch, kh)], True))
            for j in range(FC):
                t.append(((y, "ff", j), [
                    (lambda r, i=i: r.rearrange("p (k c) -> p k c", k=KD)[:, :, P * i:P * i + P],
                     cols(I[w][l], P * j, P * j + P)) for i, w in enumerate(("w_gate_2", "w_up_2"))], True))
            for j in range(FC // 2):
                t.append(((y, "down", j), [(lambda r: r.rearrange("p (k c) -> p k c", k=2),
                                         I["w_down_2"][l][256 * j:256 * j + 256, :].rearrange("(k p) c -> p k c", p=P))], True))
            return t

        stream = []
        mods_in_attention = {0: [(0, j) for j in range(8, 12)] + [(1, j) for j in range(8)],
                             1: [(1, j) for j in range(8, 12)]}
        for j in range(8):
            stream.append(mod_tile(0, j))
        for l in range(DEPTH):
            outs = [((l, "out", ch, kh), [square(I["w_out"][l], ch, kh)], True) for ch in range(2) for kh in range(2)]
            stream += mix_tiles(l) + [mod_tile(*m) for m in mods_in_attention[l]] + outs
        for l in range(DEPTH):
            stream += second_tiles(l)
        place = {what: n for n, (what, _, _) in enumerate(stream)}
        splits = [what for what, _, is_split in stream if is_split]
        split_at = {what: i for i, what in enumerate(splits)}
        mods_all = [what for what, _, _ in stream if what[1] == "mod"]
        mod_at = {what: i for i, what in enumerate(mods_all)}
        landed, counts = [], [0] * RAW
        for n, (_, loads, _) in enumerate(stream):
            counts[n % RAW] += 16 * len(loads)
            landed.append(counts[n % RAW])
        landed_sems = [ctx.enter_context(nc.semaphore(f"tile_landed{r}")) for r in range(RAW)]

        def raw_of(what):
            return raw[:, place[what] % RAW, :]

        def wait_landed(eng, what):
            n = place[what]
            eng.wait_ge(landed_sems[n % RAW], landed[n])

        consts = [(rot1[:], I["rot1"]), (rot2[HD:QC, :], I["rot2"]),
                  (cos1[:], I["cos1"]), (sin1[:], I["sin1"]),
                  (band_mid[:], I["band_mid"]), (band_last[:], I["band_last"]),
                  (dft_ccos[:], I["dft_ccos"]), (dft_csin[:], I["dft_csin"]),
                  (sinks[:], I["sink"].rearrange("l h -> (l h)").partition_broadcast(P)),
                  (table[0:BUCKETS, :], I["rel_bias_2"]), (table[BUCKETS:, :], I["pick"]), (hot[:], I["hot"])]
        vectors = [(ident[:], I["ident"]), (fold[:], I["fold"]),
                   (vec[0:8, :], I["c"].rearrange("a (r p) -> (a r) p", p=P)),
                   (vec[8:16, :], I["c_ctx"].rearrange("(r p) -> r p", p=P))]
        VB = []
        for l in range(DEPTH):
            b0 = 16 + 48 * l
            VB.append(dict(b_mod=b0, g_pre=b0 + 24, g_post=b0 + 32, conv_w=b0 + 40, conv_b=b0 + 46))
            vectors += [(vec[b0:b0 + 24, :], I["b_mod"][l].rearrange("(r p) -> r p", p=P)),
                       (vec[b0 + 24:b0 + 32, :], I["g_pre"][l].rearrange("(r p) -> r p", p=P)),
                       (vec[b0 + 32:b0 + 40, :], I["g_post"][l].rearrange("(r p) -> r p", p=P)),
                       (vec[b0 + 40:b0 + 46, :], I["conv_w"][l].rearrange("t (r p) -> (t r) p", p=P)),
                       (vec[b0 + 46:b0 + 48, :], I["conv_b"][l].rearrange("(r p) -> r p", p=P))]
        LG = 16 + 48 * DEPTH
        vectors += [(vec[LG:LG + 4, :], I["q_norm_g_2"].rearrange("l (r p) -> (l r) p", p=P)), (vec[LG + 4:LG + 6, :], I["kv_norm_g_2"])]
        NV = LG + 6

        def units1(l):
            u = []
            for h in range(HEADS):
                b = HD * (h // 4)
                for i in range(XT + (CT if l < DEPTH - 1 else 0)):
                    ctx_v = [v1[:, XT + j, b:b + HD] for j in range(CT)]
                    ctx_k = [k1[b:b + HD, SEQ + P * j:SEQ + P * j + P] for j in range(CT)]
                    if i < XT:
                        lo, hi = max(0, i - 1), min(XT - 1, i + 1)
                        n = hi - lo + 1
                        segs = [(0, k1[b:b + HD, P * lo:P * hi + P])] + [(P * (n + j), k) for j, k in enumerate(ctx_k)]
                        vs = [v1[:, j, b:b + HD] for j in range(lo, hi + 1)] + ctx_v
                        mask = band_last[:] if i == XT - 1 else band_mid[:, P if i == 0 else 0:]
                    else:
                        segs, vs, mask = [(0, k1[b:b + HD, SEQ:TOK])], ctx_v, band_mid[:, 3 * P:]
                    u.append(dict(q=q1[b:b + HD, h % 4, P * i:P * i + P], segs=segs, vs=vs, mask=mask, second=False,
                                  out=ao1[:, i, HD * h:HD * h + HD], sink=sinks[:, l * HEADS + h:l * HEADS + h + 1]))
            return u

        def units2():
            u = []

            def add(q, k, v, head, out, second=False):
                for i in range(XT):
                    u.append(dict(q=q(i), segs=[(0, k(P * (i + 1)))], vs=[v(j) for j in range(i + 1)],
                                  mask=strips[:, head, 384 - P * i:SEQ], out=out(i), sink=None, second=second))

            for h in range(B_HEADS):
                for m in range(2):
                    b = HD * (h % 2) + 32 * m
                    add(lambda i: qb[b:b + 32, h // 2, P * i:P * i + P], lambda n: kb[b:b + 32, h // 2, 0:n],
                        lambda j: vb[:, j, HD * h:HD * h + HD], A_HEADS + h,
                        lambda i: ao2[:, i, 384 + HD * h:384 + HD * h + HD], second=m == 1)
            for h in range(A_HEADS):
                b = HD * (h % 2)
                add(lambda i: qa[b:b + HD, h // 2, P * i:P * i + P], lambda n: ka[b:b + HD, h // 2, 0:n],
                    lambda j: va[:, j, HD * h:HD * h + HD], h, lambda i: ao2[:, i, HD * h:HD * h + HD])
            for h in range(C_HEADS):
                add(lambda i: qc[0:QC, h, P * i:P * i + P], lambda n: kc[0:QC, h, 0:n],
                    lambda j: vc[:, j, HD * h:HD * h + HD], A_HEADS + B_HEADS,
                    lambda i: ao2[:, i, 640 + HD * h:640 + HD * h + HD])
            return u

        N_B = 2 * B_HEADS * XT
        MOD_STEP = (4, 6)

        def slots(y):
            return (sc, pt, 1024, (2, 1, 1)) if y < DEPTH else (sc2, pt2, 512, (3, 2, 2))

        block = ctx.enter_context(nc.Block())

        @block.sync
        def _(sp):
            for dst, src in vectors:
                sp.dma_start(dst, src).then_inc(s_vectors.sem, 16)
            for n, (what, loads, _) in enumerate(stream):
                if n >= RAW:
                    sp.wait_ge(s_tile_lo.sem, s_tile_lo.at(stream[n - RAW][0]))
                for into, src in loads:
                    sp.dma_start(into(raw[:, n % RAW, :]), src).then_inc(landed_sems[n % RAW], 16)
            for t in range(XT):
                sp.wait_ge(s_x_final.sem, s_x_final.at((2 * DEPTH - 1, t)))
                sp.dma_start(out[0, P * t:P * t + P, :], res[:, t, :]).then_inc(s_stored.sem, 16)
            sp.wait_ge(s_stored.sem, 16 * XT)

        @block.gpsimd
        def _(pool):
            for dst, src in consts:
                pool.dma_start(dst, src).then_inc(s_consts.sem, 16)
            pool.memset(ones[:], 1.0).then_inc(s_ones.sem, s_ones.nth(0))
            pool.memset(wf[:], 0.0).then_inc(s_wf_zero.sem, s_wf_zero.nth(0))
            pool.wait_ge(s_wf_zero.sem, s_wf_zero.at(0))
            for l in range(DEPTH):
                for h in range(2):
                    pool.dma_start(wf[HD * h:HD * h + HD, l, :, HD * h:HD * h + HD],
                                   I["w_fourier"][l].rearrange("(c h) a b -> h a c b", h=2)[h]).then_inc(s_wf_landed.sem, 16)
            for i, what in enumerate(splits):
                pool.wait_ge(s_tile_hi.sem, s_tile_hi.at(what))
                pool.tensor_tensor(w_lo[:, i % SPLIT, :], raw_of(what), w_hi[:, i % SPLIT, :].bitcast(F32),
                                         ALU.subtract).then_inc(s_tile_lo.sem, s_tile_lo.nth(what))

        @block.scalar
        def _(act):
            todo = list(splits)

            def split_next():
                if not todo:
                    return
                what = todo.pop(0)
                i = split_at[what]
                if i >= SPLIT:
                    act.wait_ge(s_mm.sem, s_mm.at(("tile", splits[i - SPLIT])))
                wait_landed(act, what)
                act.activation(w_hi[:, i % SPLIT, :], raw_of(what), ACT.Copy).then_inc(s_tile_hi.sem, s_tile_hi.nth(what))

            def root(key, n):
                act.wait_ge(s_var.sem, s_var.at(key))
                act.activation(rstd[:, 0:n], ssq[:, 0:n], ACT.Sqrt).then_inc(s_root.sem, s_root.nth(key))

            def mod_out_row(what):
                i = mod_at[what]
                act.wait_ge(s_mm.sem, s_mm.at(("tile", what)))
                if i >= 2:
                    act.wait_ge(s_mod.sem, s_mod.at(mods_all[i - 2]))
                act.activation(mod_row[:, i % 2, :], ps[0:4, 7, 0:256], ACT.Copy).then_inc(s_mod_row.sem, s_mod_row.nth(what))

            def exp_units(y, units, at_step):
                s_, t_, width, (n_s, n_t, n_o) = slots(y)
                for step in range(len(units) + 3):
                    i = step - 3
                    if i >= 0:
                        n = P * len(units[i]["vs"])
                        o0 = width * (n_s + i % n_t)
                        act.wait_ge(s_turned.sem, s_turned.at((y, i)))
                        if i >= 2:
                            act.wait_ge(s_mixed.sem, s_mixed.at((y, i - 2)))
                        act.activation(t_[:, i % 2, 0:n], ps_flat[:, o0:o0 + n], ACT.Copy).then_inc(s_pt.sem, s_pt.nth((y, i)))
                    i = step
                    if i < len(units):
                        u = units[i]
                        n = P * len(u["vs"]) + (u["sink"] is not None)
                        act.wait_ge(s_scored.sem, s_scored.at((y, i)))
                        act.activation(s_[:, i % 4, 0:n], s_[:, i % 4, 0:n], ACT.Exp, bias=small[:, 0, i % 8:i % 8 + 1], scale=-1.0,
                                       accum_out=small[:, 1, i % 8:i % 8 + 1]).then_inc(s_probs.sem, s_probs.nth((y, i)))
                    at_step(step)

            act.dma_start(res[:], I["x"][0].rearrange("(t p) d -> p t d", p=P)).then_inc(s_x_landed.sem, 16)
            act.dma_start(res_c[:], I["ctx"][0].rearrange("(t p) d -> p t d", p=P)).then_inc(s_x_landed.sem, 16)
            act.wait_ge(s_vec_t.sem, s_vec_t.at(0))
            act.activation(cond[:], vec_t[:, 0:16].rearrange("p (s k) -> p k s", s=2), ACT.Silu).then_inc(s_cond.sem, s_cond.nth(0))
            act.wait_ge(s_cond.sem, s_cond.at(0))
            act.activation(cond_hl[:, :, 0:2], cond[:], ACT.Copy).then_inc(s_cond_hi.sem, s_cond_hi.nth(0))
            split_next()
            split_next()
            for l in range(DEPTH):
                both = l < DEPTH - 1
                nt, nc_ = (NT, TOK) if both else (XT, SEQ)
                parts = 2 if both else 1
                def squares(t):
                    src = res[:, t, :] if t < XT else res_c[:, t - XT, :]
                    act.activation(xn[:, t, :], src, ACT.Square, accum_out=ssq[:, t:t + 1]).then_inc(s_ssq.sem, s_ssq.nth((l, "pre", t)))

                if l == 0:
                    for j in range(8):
                        if j == 2:
                            act.wait_ge(s_x_landed.sem, 32)
                        if j >= 2:
                            squares(j - 2)
                        mod_out_row((0, "mod", j))
                        split_next()
                else:
                    for t in range(NT):
                        act.wait_ge(s_x_final.sem, s_x_final.at((l - 1, t)))
                        squares(t)
                root((l, "pre"), NT)
                if l == 0:
                    act.wait_ge(s_rr.sem, s_rr.at(0))
                    for h in range(A_HEADS + B_HEADS):
                        act.dma_start(scratch[h].rearrange("(o p n) -> o p n", o=1, n=SEQ + P),
                                      rr[h:h + 1, :].unsqueeze(1).broadcast_to((1, P, SEQ + P))).then_inc(s_bias_rows.sem, 16)
                for k in range(KD):
                    act.wait_ge(s_mod_x.sem, s_mod_x.at((l, k)))
                    act.activation(h_hi[:, k, :], tmp_n[:, k % 2, :], ACT.Copy).then_inc(s_hi.sem, s_hi.nth((l, "n", k)))
                n_fm = 0

                def fm(what, c, func, dst, scale=1.0, n_parts=parts):
                    nonlocal n_fm
                    for part in range(n_parts):
                        act.wait_ge(s_mm.sem, s_mm.at((l, what, c, part)))
                        b, n, a = (n_fm % 4, SEQ, 0) if part == 0 else (4 + n_fm % 2, CTX, SEQ)
                        act.activation(dst[:, a:a + n], ps[:, b, 0:n], func, scale=scale).then_inc(s_proj.sem, s_proj.nth((l, what, c, part)))
                    n_fm += 1

                for j in range(2):
                    for c in range(2):
                        fm(("q", j), c, ACT.Copy, q1[:, 2 * j + c, :], scale=-HD ** -0.5)
                    split_next()
                fm(("kv",), 0, ACT.Copy, k1[:], n_parts=2)
                for part, n in ((0, XT), (1, CT)):
                    act.wait_ge(s_mm.sem, s_mm.at((l, ("kv",), 1, part)))
                    act.activation(v1[:, XT * part:XT * part + n, :].rearrange("p t c -> p (t c)"),
                                         ps[:, 6 + part, 0:n * P], ACT.Copy).then_inc(s_proj.sem, s_proj.nth((l, ("kv",), 1, part)))
                split_next()
                if l == 0:
                    act.wait_ge(s_bias_rows.sem, 16 * (A_HEADS + B_HEADS))
                for g in range(nt // 2):
                    act.wait_ge(s_mm.sem, s_mm.at((l, ("uf",), g, 0)))
                    act.activation(uf_hi[:, 2 * g:2 * g + 2, :].rearrange("p t c -> p (t c)"),
                                         ps[:, (6, 7, 5)[g], :], ACT.Copy).then_inc(s_uf_hi.sem, s_uf_hi.nth((l, g)))
                split_next()
                for what, func, dst in (("gf", ACT.Silu, gf), ("zc", ACT.Copy, cz), ("bc", ACT.Copy, cb)):
                    for c in range(2):
                        fm((what,), c, func, dst[:, c, :])
                    split_next()
                n_fm += 2
                split_next()
                act.wait_ge(s_roped.sem, s_roped.at((l, 4)))
                for c in range(2):
                    fm(("gc",), c, ACT.Silu, tmp_p[:, c, :])
                split_next()
                act.wait_ge(s_conv_gate.sem, s_conv_gate.at((l, 1)))
                for j in range(2):
                    for c in range(2):
                        fm(("ga", j), c, ACT.Silu, ga[:, 2 * j + c, :])
                    split_next()
                for i in range(2):
                    for c in range(2):
                        act.wait_ge(s_mm.sem, s_mm.at((l, "four", i, c)))
                        act.activation(four[:, i, c, 0:SEQ], ps[:, 2 * i + c, :], ACT.Copy).then_inc(s_four_out.sem, s_four_out.nth((l, i, c)))
                    split_next()
                if both:
                    for i in range(2):
                        act.wait_ge(s_mm.sem, s_mm.at((l, "four", i, "ctx")))
                        act.activation(four[:, i, :, SEQ:], ps[:, 4 + i, :].rearrange("p (c n) -> p c n", c=2),
                                             ACT.Copy).then_inc(s_four_out.sem, s_four_out.nth((l, i, "ctx")))
                    split_next()
                mods = [(m, "mod", j) for m, j in mods_in_attention[l]]

                def between(step):
                    if step >= 2 and step % MOD_STEP[l] == 0 and mods:
                        mod_out_row(mods.pop(0))
                        split_next()

                exp_units(l, units1(l), between)
                while mods:
                    mod_out_row(mods.pop(0))
                    split_next()
                for t in range(nt):
                    act.wait_ge(s_gated.sem, s_gated.at((l, t)))
                    act.activation(h_hi[:, 0:4, P * t:P * t + P],
                                         tmp_m[:, t % 2, :].rearrange("p (c n) -> p c n", c=4), ACT.Copy).then_inc(s_hi.sem, s_hi.nth((l, "m", t)))
                for c in range(4):
                    act.wait_ge(s_side.sem, s_side.at((l, c)))
                    src = gf[:, c, 0:nc_] if c < 2 else cb[:, c - 2, 0:nc_]
                    act.activation(h_hi[:, 4 + c, 0:nc_], src, ACT.Copy).then_inc(s_hi.sem, s_hi.nth((l, "s", c)))
                act.wait_ge(s_lo.sem, s_lo.at((l, "s", 3)))
                for ch in range(2):
                    split_next()
                    for t in range(nt):
                        act.wait_ge(s_mm.sem, s_mm.at((l, "out", ch, t)))
                        act.activation(y1[:, t, 512 * ch:512 * ch + 512], ps[:, t, :], ACT.Copy).then_inc(s_y.sem, s_y.nth((l, ch, t)))
                    if ch < parts:
                        for b in range(2):
                            act.wait_ge(s_gate_mm.sem, s_gate_mm.at((l, ch, b)))
                            act.activation(gate_b[:, ch, 512 * b:512 * b + 512], ps[:, 6 + b, :], ACT.Copy).then_inc(s_gate_b.sem, s_gate_b.nth((l, ch)))
                    if ch == 0:
                        split_next()
                for t in range(nt):
                    act.wait_ge(s_y.sem, s_y.at((l, 1, t)))
                    if t > 0:
                        act.wait_ge(s_ssq.sem, s_ssq.at((l, "post", t - 1)))
                    act.activation(junk[:], y1[:, t, :], ACT.Square, accum_out=ssq[:, t:t + 1]).then_inc(s_ssq.sem, s_ssq.nth((l, "post", t)))
                root((l, "post"), nt)
                split_next()

            for l in range(DEPTH):
                y = DEPTH + l
                for t in range(XT):
                    act.wait_ge(s_x_final.sem, s_x_final.at((y - 1, t)))
                for dst, src in ((cos2[HD:QC, :], I["cos2"]), (sin2[HD:QC, :], I["sin2"]),
                                 (dlam[:], I["diff_lambda_2"][l].rearrange("a b -> (a b)").partition_broadcast(P)),
                                 (lam_c[:], I["lam_init"][l].partition_broadcast(P)),
                                 (subln[:], I["subln_g_2"][l].partition_broadcast(P))):
                    act.dma_start(dst, src).then_inc(s_layer_consts.sem, s_layer_consts.nth(y, 16))
                for k in range(KD):
                    act.wait_ge(s_xt.sem, s_xt.at((y, k)))
                    act.activation(g_hi[:, k, :], ps[:, k % 4, :], ACT.Copy).then_inc(s_hi.sem, s_hi.nth((y, "t", k)))
                act.wait_ge(s_lam_sums.sem, s_lam_sums.at(y))
                act.activation(lam[:, 2:4], lam[:, 0:2], ACT.Exp).then_inc(s_lam_exp.sem, s_lam_exp.nth(y))
                for j, n in ((0, 256), (1, 160)):
                    for g in range(2):
                        act.wait_ge(s_mm.sem, s_mm.at((y, "c", j, g)))
                        act.activation(c_in[:, 2 * g:2 * g + 2, 256 * j:256 * j + n],
                                             ps[:, (6, 0)[j] + g, 0:2 * n].rearrange("p (t c) -> p t c", t=2), ACT.Copy).then_inc(s_proj.sem, s_proj.nth((y, "c", j, g)))
                    split_next()
                act.wait_ge(s_proj.sem, s_proj.at((y, "c", 1, 1)))
                for t in range(XT):
                    if t > 0:
                        act.wait_ge(s_ssq.sem, s_ssq.at((y, "c", 3 + t)))
                    act.activation(tmp_c[:, 0, 0:256], c_in[:, t, 0:256], ACT.Square, accum_out=ssq[:, t:t + 1]).then_inc(s_ssq.sem, s_ssq.nth((y, "c", t)))
                    act.activation(tmp_c[:, 1, 0:128], c_in[:, t, 256:384], ACT.Square, accum_out=ssq[:, 4 + t:5 + t]).then_inc(s_ssq.sem, s_ssq.nth((y, "c", 4 + t)))
                root((y, "c"), 8)
                for j in range(3):
                    for c in range(2):
                        i = 2 * j + c
                        act.wait_ge(s_mm.sem, s_mm.at((y, "a", i)))
                        dst, scale = (qa[:, i, :], -HD ** -0.5) if i < 3 else (ka[:, i - 3, :], 1.0)
                        act.activation(dst, ps[:, i % 4, :], ACT.Copy, scale=scale).then_inc(s_proj.sem, s_proj.nth((y, "a", i)))
                    split_next()
                for i in range(3):
                    act.wait_ge(s_lat.sem, s_lat.at((y, i)))
                    act.activation(cq_hi[:, i, :] if i < 2 else ckv_hi[:], tmp_c[:, i % 2, :], ACT.Copy).then_inc(s_hi.sem, s_hi.nth((y, "c", i)))
                for j, n in ((0, 256), (1, 128)):
                    for g in range(2):
                        act.wait_ge(s_mm.sem, s_mm.at((y, "av", j, g)))
                        act.activation(va[:, 2 * g:2 * g + 2, 256 * j:256 * j + n],
                                             ps[:, 4 + 2 * j + g, 0:2 * n].rearrange("p (t c) -> p t c", t=2), ACT.Copy).then_inc(s_proj.sem, s_proj.nth((y, "av", j, g)))
                    split_next()
                for h in range(C_HEADS):
                    act.wait_ge(s_mm.sem, s_mm.at((y, "qc", h)))
                    act.activation(qc[0:QC, h, :], ps[0:QC, h % 2, :], ACT.Copy, scale=-QC ** -0.5).then_inc(s_proj.sem, s_proj.nth((y, "qc", h)))
                    act.wait_ge(s_mm.sem, s_mm.at((y, "kc", h)))
                    act.activation(kc[0:HD, h, :], ps[0:HD, 2 + h % 2, :], ACT.Copy).then_inc(s_proj.sem, s_proj.nth((y, "kc", h)))
                for t in range(XT):
                    act.wait_ge(s_mm.sem, s_mm.at((y, "vc", t)))
                    act.activation(vc[:, t, :], ps[:, 4 + t, 0:384], ACT.Copy).then_inc(s_proj.sem, s_proj.nth((y, "vc", t)))
                split_next()
                for what, dst, b0, scale in (("bq", qb, 0, -32 ** -0.5), ("bk", kb, 2, 1.0)):
                    for c in range(2):
                        act.wait_ge(s_mm.sem, s_mm.at((y, what, c)))
                        act.activation(dst[:, c, :], ps[:, b0 + c, :], ACT.Copy, scale=scale).then_inc(s_proj.sem, s_proj.nth((y, what, c)))
                    split_next()
                act.wait_ge(s_roped.sem, s_roped.at((y, C_HEADS - 1)))
                act.wait_ge(s_kr_all.sem, s_kr_all.at(y))
                act.wait_ge(s_bias_rows.sem, 16 * (A_HEADS + B_HEADS))
                for h in range(A_HEADS + B_HEADS):
                    act.dma_start(strips[:, h, :], scratch[h, P - 1:P - 1 + P * (SEQ + P - 1)].rearrange(
                        "(p n) -> p n", n=SEQ + P - 1)[:, 0:SEQ]).then_inc(s_strips.sem, s_strips.nth(y, 16))
                act.dma_start(strips[:, A_HEADS + B_HEADS, :], I["causal"]).then_inc(s_strips.sem, s_strips.nth(y, 16))
                for g in range(2):
                    act.wait_ge(s_mm.sem, s_mm.at((y, "bv", 0, g)))
                    act.activation(vb[:, 2 * g:2 * g + 2, :].rearrange("p t c -> p (t c)"), ps[:, 4 + g, :], ACT.Copy).then_inc(s_proj.sem, s_proj.nth((y, "bv", 0, g)))
                split_next()
                units = units2()

                def between(step):
                    if step == N_B + 8:
                        root((y, "sub"), 16)

                exp_units(y, units, between)
                act.wait_ge(s_mixed.sem, s_mixed.at((y, len(units) - 1)))
                for i, w in enumerate(("ln1_g_2", "ln1_b_2")):
                    act.dma_start(ln1[:, i, :], I[w][l].partition_broadcast(P)).then_inc(s_ln.sem, s_ln.nth((y, 1), 16))
                for t in range(XT):
                    for g in range(2):
                        act.wait_ge(s_aot.sem, s_aot.at((y, t, g)))
                        act.activation(g_hi[:, 4 * g:4 * g + 4, P * t:P * t + P],
                                             ps[:, 2 * (t % 2) + g, :].rearrange("p (c n) -> p c n", c=4), ACT.Copy).then_inc(s_hi.sem, s_hi.nth((y, "m", t, g)))
                for _ in range(4):
                    split_next()
                root((y, 1), XT)
                for k in range(KD):
                    act.wait_ge(s_ht.sem, s_ht.at((y, k)))
                    act.activation(g_hi[:, k, :], ps[:, k % 4, :], ACT.Copy).then_inc(s_hi.sem, s_hi.nth((y, "h", k)))
                for j in range(FC):
                    act.wait_ge(s_mm.sem, s_mm.at((y, "gate", j)))
                    act.activation(tmp_f[:, j % 2, :], ps[:, 2 * (j % 3), :], ACT.Silu).then_inc(s_silu.sem, s_silu.nth((y, j)))
                    act.wait_ge(s_glu.sem, s_glu.at((y, j)))
                    act.activation(hid_hi[:, j, :], tmp_f[:, 2 + j % 2, :], ACT.Copy).then_inc(s_hi.sem, s_hi.nth((y, "f", j)))
                    split_next()
                for i, w in enumerate(("ln2_g_2", "ln2_b_2")):
                    act.dma_start(ln2[:, i, :], I[w][l].partition_broadcast(P)).then_inc(s_ln.sem, s_ln.nth((y, 2), 16))
                for j in range(FC // 2):
                    split_next()
                root((y, 2), XT)

        @block.tensor
        def _(pe):
            emptied = {b: (s_vectors.sem, 16 * len(vectors)) for b in range(8)}

            def begin(what):
                pe.wait_ge(s_tile_lo.sem, s_tile_lo.at(what))
                i = split_at[what] % SPLIT
                return w_hi[:, i, :], w_lo[:, i, :]

            def left(what):
                s_mm.name_latest(("tile", what))

            def mm3(o, lhs, rhs, first, last):
                pe.matmul(o, lhs[1], rhs[0], start=first, stop=False)
                pe.matmul(o, lhs[0], rhs[1], start=False, stop=False)
                return pe.matmul(o, lhs[0], rhs[0], start=False, stop=last)

            def both_parts(pair, f):
                return f(pair[0]), f(pair[1])

            def turn(o, src, key, ident_n=P):
                return pe.transpose(o, src, ident[0:ident_n, 0:ident_n])

            def mod(what):
                i = mod_at[what]
                o = ps[0:4, 7, 0:256]
                w = both_parts(begin(what), lambda r: r.rearrange("p (k c) -> p k c", k=KD))
                if i >= 1:
                    pe.wait_ge(s_mod_row.sem, s_mod_row.at(mods_all[i - 1]))
                for part in range(2):
                    for k in range(KD):
                        m = pe.matmul(o, cond_hl[:, k, :], w[1 - part][:, k, :], start=part == 0 and k == 0, stop=part == 1 and k == KD - 1)
                m.then_inc(s_mm.sem, s_mm.nth(what))
                left(what)

            def mod_fm(what):
                i = mod_at[what]
                l, _, j = what
                pe.wait_ge(s_mod_row.sem, s_mod_row.at(what))
                for c in range(2):
                    o = 256 + 64 * l + 2 * (2 * j + c)
                    m = pe.matmul(ps[:, 7, o:o + 2], mod_row[:, i % 2, P * c:P * c + P], fold[:], start=True, stop=True)
                m.then_inc(s_mod.sem, s_mod.nth(what))

            def attend(y, units, at_step):
                for b in range(7):
                    pe.wait_ge(*emptied[b])
                s_, t_, width, (n_s, n_t, n_o) = slots(y)
                for step in range(len(units) + 4):
                    i = step
                    if i < len(units):
                        u = units[i]
                        o0 = width * (i % n_s)
                        if i >= n_s:
                            pe.wait_ge(s_scored.sem, s_scored.at((y, i - n_s)))
                        for col, k in u["segs"]:
                            m = pe.matmul(ps_flat[:, o0 + col:o0 + col + k.shape[1]], u["q"], k, start=True, stop=True)
                        m.then_inc(s_scores.sem, s_scores.nth((y, i)))
                    i = step - 3
                    if 0 <= i < len(units):
                        o0 = width * (n_s + i % n_t)
                        pe.wait_ge(s_probs.sem, s_probs.at((y, i)))
                        if i >= n_t:
                            pe.wait_ge(s_pt.sem, s_pt.at((y, i - n_t)))
                        for j in range(len(units[i]["vs"])):
                            m = pe.transpose(ps_flat[:, o0 + P * j:o0 + P * j + P], s_[:, i % 4, P * j:P * j + P], ident[:])
                        m.then_inc(s_turned.sem, s_turned.nth((y, i)))
                    i = step - 4
                    if i >= 0:
                        u = units[i]
                        n = len(u["vs"])
                        pe.wait_ge(s_pt.sem, s_pt.at((y, i)))
                        if i >= n_o:
                            pe.wait_ge(s_o_out.sem, s_o_out.at((y, i - n_o)))
                        o0 = width * (n_s + n_t) + 512 * (i % n_o)
                        for j, v in enumerate(u["vs"]):
                            m = pe.matmul(ps_flat[:, o0:o0 + HD], t_[:, i % 2, P * j:P * j + P], v, start=j == 0, stop=j == n - 1)
                        m.then_inc(s_mixed.sem, s_mixed.nth((y, i)))
                    at_step(step)
                for b in range(7):
                    emptied[b] = s_o_out.after((y, len(units) - 1))

            pe.wait_ge(s_vectors.sem, 16 * len(vectors))
            emptied[7] = s_vec_t.after(0)
            pe.transpose(ps[:, 7, 0:NV], vec[0:NV, :], ident[0:NV, 0:NV]).then_inc(s_vec_mm.sem, s_vec_mm.nth(0))
            pe.wait_ge(s_cond_hi.sem, s_cond_hi.at(0))
            pe.wait_ge(s_cond_lo.sem, s_cond_lo.at(0))
            pe.wait_ge(*emptied[7])
            emptied[7] = s_mod_out.after((0, 0))
            for j in range(8):
                if j > 0:
                    mod_fm((0, "mod", j - 1))
                mod((0, "mod", j))
            mod_fm((0, "mod", 7))
            pe.wait_ge(s_consts.sem, 16 * len(consts))
            pe.wait_ge(*emptied[0])
            emptied[0] = s_rr.after(0)
            pe.wait_ge(*emptied[1])
            emptied[1] = s_rr.after(0)
            pe.matmul(ps[0:A_HEADS + B_HEADS, 0, :], table[:], hot[:, 0:SEQ], start=True, stop=True)
            pe.matmul(ps[0:A_HEADS + B_HEADS, 1, 0:P], table[:], hot[:, SEQ:SEQ + P], start=True, stop=True).then_inc(s_rr_mm.sem, s_rr_mm.nth(0))

            for l in range(DEPTH):
                both = l < DEPTH - 1
                nt, nc_ = (NT, TOK) if both else (XT, SEQ)
                parts = 2 if both else 1
                if l == 0:
                    pe.wait_ge(s_wf_landed.sem, 16 * 2 * DEPTH)
                pe.wait_ge(*emptied[6])
                emptied[6] = s_wf_m.after(l)
                for i, m_ in enumerate((dft_ccos, dft_csin)):
                    m = pe.matmul(ps[:, 6, 256 * i:256 * i + 256], m_[:], wf[:, l, :, :], start=True, stop=True)
                m.then_inc(s_wf_mm.sem, s_wf_mm.nth(l))
                for k in range(KD):
                    pe.wait_ge(*emptied[k % 4])
                    emptied[k % 4] = s_mod_x.after((l, k))
                    pe.wait_ge(*emptied[4 + k % 2])
                    emptied[4 + k % 2] = s_mod_x.after((l, k))
                    for t in range(NT):
                        if k == 0:
                            pe.wait_ge(s_xn.sem, s_xn.at((l, t)))
                        o = ps[:, k % 4, P * t:P * t + P] if t < XT else ps[:, 4 + k % 2, P * (t - XT):P * (t - XT) + P]
                        m = pe.transpose(o, xn[:, t, P * k:P * k + P], ident[:])
                    m.then_inc(s_nt.sem, s_nt.nth((l, k)))
                n_fm = 0
                H = (h_hi, h_lo)
                lo_seen = set()

                def rows_ready(k):
                    if k not in lo_seen:
                        lo_seen.add(k)
                        pe.wait_ge(s_lo.sem, s_lo.at((l, "n", k)))

                def fm(what, c, w, until, n_parts=parts):
                    nonlocal n_fm
                    w = both_parts(w, lambda r: r.rearrange("p (k c) -> p k c", k=KD))
                    for part in range(n_parts):
                        b, n, a = (n_fm % 4, SEQ, 0) if part == 0 else (4 + n_fm % 2, CTX, SEQ)
                        pe.wait_ge(*emptied[b])
                        emptied[b] = until.after((l, what, c, part))
                        for k in range(KD):
                            rows_ready(k)
                            m = mm3(ps[:, b, 0:n], both_parts(w, lambda r: r[:, k, P * c:P * c + P]),
                                    both_parts(H, lambda r: r[:, k, a:a + n]), k == 0, k == KD - 1)
                        m.then_inc(s_mm.sem, s_mm.nth((l, what, c, part)))
                    n_fm += 1

                def tm(o, t, w, c0, n):
                    w = both_parts(w, lambda r: r.rearrange("p (k c) -> p k c", k=KD))
                    for k in range(KD):
                        m = mm3(o, both_parts(H, lambda r: r[:, k, P * t:P * t + P]),
                                both_parts(w, lambda r: r[:, k, c0:c0 + n]), k == 0, k == KD - 1)
                    return m

                for j in range(2):
                    w = begin((l, "q", j))
                    for c in range(2):
                        fm(("q", j), c, w, s_proj)
                    left((l, "q", j))
                w = begin((l, "kv"))
                fm(("kv",), 0, w, s_proj, 2)
                for part, t0, n in ((0, 0, XT), (1, XT, CT)):
                    pe.wait_ge(*emptied[6 + part])
                    emptied[6 + part] = s_proj.after((l, ("kv",), 1, part))
                    for t in range(n):
                        m = tm(ps[:, 6 + part, P * t:P * t + P], t0 + t, w, P, P)
                    m.then_inc(s_mm.sem, s_mm.nth((l, ("kv",), 1, part)))
                left((l, "kv"))
                w = begin((l, "uf"))
                for g in range(nt // 2):
                    b = (6, 7, 5)[g]
                    pe.wait_ge(*emptied[b])
                    emptied[b] = s_uf_lo.after((l, g))
                    for t in range(2):
                        m = tm(ps[:, b, 256 * t:256 * t + 256], 2 * g + t, w, 0, 256)
                    m.then_inc(s_mm.sem, s_mm.nth((l, ("uf",), g, 0)))
                left((l, "uf"))
                for what in ("gf", "zc", "bc", "cc", "gc"):
                    w = begin((l, what))
                    for c in range(2):
                        fm((what,), c, w, s_conv_t if what == "cc" else s_proj)
                    left((l, what))
                    if what == "gf":
                        for i in range(5):
                            b = 6 + i % 2
                            pe.wait_ge(*emptied[b])
                            emptied[b] = s_roped.after((l, i))
                            pe.wait_ge(s_proj.sem, s_proj.at((l, ("q", i // 2), i % 2, 0) if i < 4 else (l, ("kv",), 0, 0)))
                            src = q1[:, i, 0:SEQ] if i < 4 else k1[:, 0:SEQ]
                            pe.matmul(ps[:, b, :], rot1[:], src, start=True, stop=True).then_inc(s_rot.sem, s_rot.nth((l, i)))
                for j in range(2):
                    w = begin((l, "ga", j))
                    for c in range(2):
                        fm(("ga", j), c, w, s_proj)
                    left((l, "ga", j))
                U = (uf_hi, uf_lo)
                pe.wait_ge(s_uf_lo.sem, s_uf_lo.at((l, nt // 2 - 1)))
                for i, part in enumerate(("cos", "sin")):
                    w = both_parts(begin((l, "dft", part)), lambda r: r.rearrange("p (k c) -> p k c", k=XT))
                    for c in range(2):
                        pe.wait_ge(*emptied[2 * i + c])
                        emptied[2 * i + c] = s_four_out.after((l, i, c))
                        for k in range(XT):
                            m = mm3(ps[:, 2 * i + c, :], both_parts(U, lambda r: r[:, k, P * c:P * c + P]),
                                    both_parts(w, lambda r: r[:, k, :]), k == 0, k == XT - 1)
                        m.then_inc(s_mm.sem, s_mm.nth((l, "four", i, c)))
                    left((l, "dft", part))
                if both:
                    w = both_parts(begin((l, "dft", "ctx")), lambda r: r[:, 0:1024].rearrange("p (i k c) -> p i k c", i=2, k=CT))
                    for i in range(2):
                        pe.wait_ge(*emptied[4 + i])
                        emptied[4 + i] = s_four_out.after((l, i, "ctx"))
                        for c in range(2):
                            for k in range(CT):
                                m = mm3(ps[:, 4 + i, CTX * c:CTX * c + CTX], both_parts(U, lambda r: r[:, XT + k, P * c:P * c + P]),
                                        both_parts(w, lambda r: r[:, i, k, :]), k == 0, k == CT - 1)
                        m.then_inc(s_mm.sem, s_mm.nth((l, "four", i, "ctx")))
                    left((l, "dft", "ctx"))
                pe.wait_ge(s_wf_m.sem, s_wf_m.at(l))
                for c in range(2):
                    for part in range(parts):
                        b, n, a = (6 + c, SEQ, 0) if part == 0 else (4 + c, CTX, SEQ)
                        pe.wait_ge(s_four_out.sem, s_four_out.at((l, 1, c if part == 0 else "ctx")))
                        pe.wait_ge(*emptied[b])
                        emptied[b] = s_side.after((l, c))
                        for i in range(2):
                            m = pe.matmul(ps[:, b, 0:n], wf_m[:, i, c, :], four[:, i, c, a:a + n], start=i == 0, stop=i == 1)
                        m.then_inc(s_fmix.sem, s_fmix.nth((l, c, part)))
                pe.wait_ge(s_roped.sem, s_roped.at((l, 4)))
                pe.wait_ge(s_proj.sem, s_proj.at((l, ("kv",), 1, 1)))
                units = units1(l)
                mods = [(m, "mod", j) for m, j in mods_in_attention[l]]
                before = []

                def between(step):
                    if step >= 2 and step % MOD_STEP[l] == 0 and mods:
                        what = mods.pop(0)
                        if before:
                            mod_fm(before.pop())
                        mod(what)
                        before.append(what)

                pe.wait_ge(*emptied[7])
                attend(l, units, between)
                while mods:
                    what = mods.pop(0)
                    mod_fm(before.pop())
                    mod(what)
                    before.append(what)
                mod_fm(before.pop())
                emptied[7] = s_mod_out.after((l, 1))
                for t in range(nt):
                    pe.wait_ge(*emptied[t % 4])
                    emptied[t % 4] = s_gated.after((l, t))
                    pe.wait_ge(s_o_out.sem, s_o_out.at((l, len(units) - 1)))
                    for c in range(4):
                        m = pe.transpose(ps[:, t % 4, P * c:P * c + P], ao1[:, t, P * c:P * c + P], ident[:])
                    m.then_inc(s_aot.sem, s_aot.nth((l, t)))
                pe.wait_ge(s_lo.sem, s_lo.at((l, "s", 3)))
                for ch in range(2):
                    for kh in range(2):
                        w = both_parts(begin((l, "out", ch, kh)), lambda r: r.rearrange("p (k c) -> p k c", k=4))
                        for t in range(nt):
                            if kh == 0:
                                pe.wait_ge(*emptied[t])
                                emptied[t] = s_y.after((l, ch, t))
                            for k in range(4):
                                m = mm3(ps[:, t, :], both_parts(H, lambda r: r[:, 4 * kh + k, P * t:P * t + P]),
                                        both_parts(w, lambda r: r[:, k, :]), kh == 0 and k == 0, kh == 1 and k == 3)
                            m.then_inc(s_mm.sem, s_mm.nth((l, "out", ch, t) if kh else (l, "out half", ch, t)))
                        left((l, "out", ch, kh))
                    if ch < parts:
                        pe.wait_ge(s_ones.sem, s_ones.at(0))
                        pe.wait_ge(s_diag.sem, s_diag.at((l, ch)))
                        for b in range(2):
                            pe.wait_ge(*emptied[6 + b])
                            emptied[6 + b] = s_gate_b.after((l, ch))
                            pe.matmul(ps[:, 6 + b, :], ones[:], diag[:, ch, 4 * b:4 * b + 4, :], start=True, stop=True).then_inc(s_gate_mm.sem, s_gate_mm.nth((l, ch, b)))

            G = (g_hi, g_lo)
            for l in range(DEPTH):
                y = DEPTH + l

                def rows_fm(turned, ready, before, what):
                    for k in range(KD):
                        pe.wait_ge(*emptied[k % 4])
                        emptied[k % 4] = s_lo.after((y, what, k))
                        for t in range(XT):
                            if k == 0:
                                pe.wait_ge(ready.sem, ready.at((before, t)))
                            m = pe.transpose(ps[:, k % 4, P * t:P * t + P], res[:, t, P * k:P * k + P], ident[:])
                        m.then_inc(turned.sem, turned.nth((y, k)))

                rows_fm(s_xt, s_x_final, y - 1, "t")
                pe.wait_ge(s_lo.sem, s_lo.at((y, "t", KD - 1)))

                def fm(b, w, c, until, key):
                    pe.wait_ge(*emptied[b])
                    emptied[b] = until
                    w = both_parts(w, lambda r: r.rearrange("p (k c) -> p k c", k=KD))
                    for k in range(KD):
                        m = mm3(ps[:, b, :], both_parts(w, lambda r: r[:, k, P * c:P * c + P]),
                                both_parts(G, lambda r: r[:, k, :]), k == 0, k == KD - 1)
                    m.then_inc(s_mm.sem, s_mm.nth(key))

                def tm(b0, w, n, what):
                    w = both_parts(w, lambda r: r[:, 0:KD * n].rearrange("p (k c) -> p k c", k=KD))
                    for g in range(2):
                        pe.wait_ge(*emptied[b0 + g])
                        emptied[b0 + g] = s_proj.after((y, *what, g))
                        for t in range(2):
                            for k in range(KD):
                                m = mm3(ps[:, b0 + g, n * t:n * t + n],
                                        both_parts(G, lambda r: r[:, k, P * (2 * g + t):P * (2 * g + t) + P]),
                                        both_parts(w, lambda r: r[:, k, :]), k == 0, k == KD - 1)
                        m.then_inc(s_mm.sem, s_mm.nth((y, *what, g)))

                for j, n in ((0, 256), (1, 160)):
                    tm((6, 0)[j], begin((y, "c", j)), n, ("c", j))
                    left((y, "c", j))
                for j in range(3):
                    w = begin((y, "a", j))
                    for c in range(2):
                        i = 2 * j + c
                        fm(i % 4, w, c, s_proj.after((y, "a", i)), (y, "a", i))
                    left((y, "a", j))
                for i in range(4):
                    pe.wait_ge(*emptied[i])
                    emptied[i] = s_lo.after((y, "c", i)) if i < 3 else s_kr_raw.after(y)
                    for t in range(XT):
                        if i == 0:
                            pe.wait_ge(s_latn.sem, s_latn.at((y, t)))
                        if i < 3:
                            m = pe.transpose(ps[:, i, P * t:P * t + P], c_in[:, t, P * i:P * i + P], ident[:])
                        else:
                            m = pe.transpose(ps[0:QC, 3, P * t:P * t + P], c_in[:, t, 416 - QC:416], ident[:])
                    m.then_inc(s_lat_t.sem, s_lat_t.nth((y, i)))
                for j, n in ((0, 256), (1, 128)):
                    tm(4 + 2 * j, begin((y, "av", j)), n, ("av", j))
                    left((y, "av", j))
                w = begin((y, "up"))
                uq = both_parts(w, lambda r: r[:, 0:2 * C_HEADS * QC].rearrange("p (k c) -> p k c", k=2))
                ukv = both_parts(w, lambda r: r[:, 2 * C_HEADS * QC:2 * C_HEADS * QC + 2 * C_HEADS * HD])

                def q_rot(h):
                    pe.wait_ge(*emptied[6 + h % 2])
                    emptied[6 + h % 2] = s_roped.after((y, h))
                    pe.wait_ge(s_proj.sem, s_proj.at((y, "qc", h)))
                    pe.matmul(ps[0:QC, 6 + h % 2, :], rot2[HD:QC, :], qc[HD:QC, h, :], start=True, stop=True).then_inc(s_q_rot.sem, s_q_rot.nth((y, h)))

                pe.wait_ge(s_lo.sem, s_lo.at((y, "c", 2)))
                for h in range(C_HEADS):
                    pe.wait_ge(*emptied[h % 2])
                    emptied[h % 2] = s_proj.after((y, "qc", h))
                    for k in range(2):
                        m = mm3(ps[0:QC, h % 2, :], both_parts(uq, lambda r: r[:, k, QC * h:QC * h + QC]),
                                both_parts((cq_hi, cq_lo), lambda r: r[:, k, :]), k == 0, k == 1)
                    m.then_inc(s_mm.sem, s_mm.nth((y, "qc", h)))
                    pe.wait_ge(*emptied[2 + h % 2])
                    emptied[2 + h % 2] = s_proj.after((y, "kc", h))
                    m = mm3(ps[:, 2 + h % 2, :], both_parts(ukv, lambda r: r[:, P * h:P * h + P]),
                            both_parts((ckv_hi, ckv_lo), lambda r: r[:]), True, True)
                    m.then_inc(s_mm.sem, s_mm.nth((y, "kc", h)))
                    if h == 0:
                        pe.wait_ge(*emptied[5])
                        emptied[5] = s_kr_all.after(y)
                        pe.wait_ge(s_kr_raw.sem, s_kr_raw.at(y))
                        pe.matmul(ps[0:QC, 5, :], rot2[HD:QC, :], kc[HD:QC, 0, :], start=True, stop=True).then_inc(s_kr_rot.sem, s_kr_rot.nth(y))
                    else:
                        q_rot(h - 1)
                q_rot(C_HEADS - 1)
                for t in range(XT):
                    pe.wait_ge(*emptied[4 + t])
                    emptied[4 + t] = s_proj.after((y, "vc", t))
                    m = mm3(ps[:, 4 + t, 0:C_HEADS * HD], both_parts((ckv_hi, ckv_lo), lambda r: r[:, P * t:P * t + P]),
                            both_parts(ukv, lambda r: r.rearrange("p (h c) -> p h c", h=C_HEADS)[:, :, HD:2 * HD]), True, True)
                    m.then_inc(s_mm.sem, s_mm.nth((y, "vc", t)))
                left((y, "up"))
                for what, b0 in (("bq", 0), ("bk", 2)):
                    w = begin((y, what, 0))
                    for c in range(2):
                        fm(b0 + c, w, c, s_proj.after((y, what, c)), (y, what, c))
                    left((y, what, 0))
                tm(4, begin((y, "bv", 0)), 256, ("bv", 0))
                left((y, "bv", 0))
                pe.wait_ge(s_roped.sem, s_roped.at((y, C_HEADS - 1)))
                pe.wait_ge(s_kr_all.sem, s_kr_all.at(y))
                units = units2()
                attend(y, units, lambda step: None)
                pe.wait_ge(s_sub.sem, s_sub.at(y))
                pe.wait_ge(s_o_out.sem, s_o_out.at((y, len(units) - 1)))
                for t in range(XT):
                    for g in range(2):
                        b = 2 * (t % 2) + g
                        pe.wait_ge(*emptied[b])
                        emptied[b] = s_lo.after((y, "m", t, g))
                        for c in range(4):
                            m = pe.transpose(ps[:, b, P * c:P * c + P], ao2[:, t, P * (4 * g + c):P * (4 * g + c) + P], ident[:])
                        m.then_inc(s_aot.sem, s_aot.nth((y, t, g)))
                pe.wait_ge(s_lo.sem, s_lo.at((y, "m", XT - 1, 1)))
                for ch in range(2):
                    for kh in range(2):
                        w = both_parts(begin((y, "o", ch, kh)), lambda r: r.rearrange("p (k c) -> p k c", k=4))
                        for t in range(XT):
                            b = 4 * ch + t
                            if kh == 0:
                                pe.wait_ge(*emptied[b])
                                emptied[b] = s_resid.after((y, 1, ch, t))
                            for k in range(4):
                                m = mm3(ps[:, b, :], both_parts(G, lambda r: r[:, 4 * kh + k, P * t:P * t + P]),
                                        both_parts(w, lambda r: r[:, k, :]), kh == 0 and k == 0, kh == 1 and k == 3)
                            m.then_inc(s_mm.sem, s_mm.nth((y, "o", ch, t) if kh else (y, "o half", ch, t)))
                        left((y, "o", ch, kh))
                rows_fm(s_ht, s_normed, y, "h")
                pe.wait_ge(s_lo.sem, s_lo.at((y, "h", KD - 1)))
                for j in range(FC):
                    w = begin((y, "ff", j))
                    b = 2 * (j % 3)
                    fm(b, w, 0, s_silu.after((y, j)), (y, "gate", j))
                    fm(b + 1, w, 1, s_glu.after((y, j)), (y, "ffup", j))
                    left((y, "ff", j))
                for j in range(FC // 2):
                    w = both_parts(begin((y, "down", j)), lambda r: r.rearrange("p (k c) -> p k c", k=2))
                    pe.wait_ge(s_lo.sem, s_lo.at((y, "f", 2 * j + 1)))
                    for t in range(XT):
                        for ch in range(2):
                            b = 2 * t + ch
                            if j == 0:
                                pe.wait_ge(*emptied[b])
                                emptied[b] = s_resid.after((y, 2, ch, t))
                            for k in range(2):
                                m = mm3(ps[:, b, :], both_parts((hid_hi, hid_lo), lambda r: r[:, 2 * j + k, P * t:P * t + P]),
                                        both_parts(w, lambda r: r[:, k, 512 * ch:512 * ch + 512]),
                                        j == 0 and k == 0, j == FC // 2 - 1 and k == 1)
                            m.then_inc(s_mm.sem, s_mm.nth((y, "down", j, ch, t)))
                    left((y, "down", j))

        @block.vector
        def _(dve):
            V = nc.vector

            def step(ins):
                ins.then_inc(s_dve_step.sem, s_dve_step.nth("latest"))
                dve.wait_ge(s_dve_step.sem, s_dve_step.count)

            def inverse(key, n):
                dve.wait_ge(s_root.sem, s_root.at(key))
                step(V.reciprocal(rstd[:, 0:n], rstd[:, 0:n]))

            def lo_part(dst, src, hi, key, wait_key):
                dve.wait_ge(s_hi.sem, s_hi.at(wait_key))
                V.tensor_tensor(dst, src, hi.bitcast(F32), ALU.subtract).then_inc(s_lo.sem, s_lo.nth(key))

            def attend(y, units, second):
                s_, t_, width, (n_s, n_t, n_o) = slots(y)
                for st in range(len(units) + 4):
                    i = st
                    if i < len(units):
                        u = units[i]
                        n = P * len(u["vs"])
                        o0 = width * (i % n_s)
                        if i >= 4:
                            dve.wait_ge(s_turned.sem, s_turned.at((y, i - 4)))
                        if u["sink"] is not None:
                            V.tensor_copy(s_[:, i % 4, n:n + 1], u["sink"]).then_inc(s_scored.sem, s_scored.nth((y, i, "sink")))
                        dve.wait_ge(s_scores.sem, s_scores.at((y, i)))
                        V.tensor_tensor_reduce(s_[:, i % 4, 0:n], ps_flat[:, o0:o0 + n], u["mask"], 1.0,
                                               3.0e38 if u["sink"] is None else u["sink"], ALU.add, ALU.min,
                                               small[:, 0, i % 8:i % 8 + 1]).then_inc(s_scored.sem, s_scored.nth((y, i)))
                    i = st - 2
                    if 0 <= i < len(units):
                        total, r = small[:, 1, i % 8:i % 8 + 1], small[:, 2, i % 8:i % 8 + 1]
                        dve.wait_ge(s_probs.sem, s_probs.at((y, i)))
                        if units[i]["second"]:
                            step(V.reciprocal(r, total))
                            V.tensor_scalar(r, r, lam[:, 4:5], None, ALU.mult).then_inc(s_recip.sem, s_recip.nth((y, i)))
                        else:
                            V.reciprocal(r, total).then_inc(s_recip.sem, s_recip.nth((y, i)))
                    i = st - 4
                    if i >= 0:
                        u = units[i]
                        o0 = width * (n_s + n_t) + 512 * (i % n_o)
                        r, o = small[:, 2, i % 8:i % 8 + 1], ps_flat[:, o0:o0 + HD]
                        dve.wait_ge(s_mixed.sem, s_mixed.at((y, i)))
                        dve.wait_ge(s_recip.sem, s_recip.at((y, i)))
                        if u["second"]:
                            dve.wait_ge(s_o_out.sem, s_o_out.at((y, i - XT)))
                            V.scalar_tensor_tensor(u["out"], o, r, u["out"], ALU.mult, ALU.add).then_inc(s_o_out.sem, s_o_out.nth((y, i)))
                        else:
                            V.tensor_scalar(u["out"], o, r, None, ALU.mult).then_inc(s_o_out.sem, s_o_out.nth((y, i)))
                    second(st)

            dve.wait_ge(s_vec_mm.sem, s_vec_mm.at(0))
            V.tensor_copy(vec_t[:, 0:NV], ps[:, 7, 0:NV]).then_inc(s_vec_t.sem, s_vec_t.nth(0))
            dve.wait_ge(s_vec_t.sem, s_vec_t.at(0))
            dve.wait_ge(s_cond_hi.sem, s_cond_hi.at(0))
            V.tensor_tensor(cond_hl[:, :, 2:4], cond[:], cond_hl[:, :, 0:2].bitcast(F32), ALU.subtract).then_inc(s_cond_lo.sem, s_cond_lo.nth(0))

            def mods_out(l, a, b, key):
                dve.wait_ge(s_mod.sem, s_mod.at((l, "mod", b // 2 - 1)))
                for s in range(2):
                    p_ = ps[:, 7, 256 + 64 * l + 2 * a:256 + 64 * l + 2 * b].rearrange("p (c s) -> p s c", s=2)[:, s, :]
                    m = V.tensor_tensor(mod[:, s, a:b], p_, vec_t[:, VB[l]["b_mod"] + a:VB[l]["b_mod"] + b], ALU.add)
                    if s == 0:
                        step(m)
                m.then_inc(s_mod_out.sem, s_mod_out.nth(key))
                dve.wait_ge(s_mod_out.sem, s_mod_out.at(key))

            def scale_and_shift(l):
                g = vec_t[:, VB[l]["g_pre"]:VB[l]["g_pre"] + KD]
                for s in range(2):
                    step(V.scalar_tensor_tensor(mod_a[:, s, :], mod[:, s, KD:2 * KD], 1.0, g, ALU.add, ALU.mult))

            for l in range(DEPTH):
                both = l < DEPTH - 1
                nt, nc_ = (NT, TOK) if both else (XT, SEQ)
                parts = 2 if both else 1
                dve.wait_ge(s_ssq.sem, s_ssq.at((l, "pre", NT - 1)))
                V.tensor_scalar(ssq[:, 0:NT], ssq[:, 0:NT], 1.0 / D, EPS, ALU.mult, ALU.add).then_inc(s_var.sem, s_var.nth((l, "pre")))
                inverse((l, "pre"), NT)
                for t in range(NT):
                    src = res[:, t, :] if t < XT else res_c[:, t - XT, :]
                    V.tensor_scalar(xn[:, t, :], src, rstd[:, t:t + 1], None, ALU.mult).then_inc(s_xn.sem, s_xn.nth((l, t)))
                if l == 0:
                    mods_out(0, 0, 16, (0, 0))
                    scale_and_shift(0)
                    dve.wait_ge(s_consts.sem, 16 * len(consts))
                    step(V.tensor_scalar(sinks[:], sinks[:], -1.0, None, ALU.mult))
                    dve.wait_ge(s_rr_mm.sem, s_rr_mm.at(0))
                    V.tensor_scalar(rr[:], ps_flat[0:A_HEADS + B_HEADS, 0:SEQ + P], -1.0, None, ALU.mult).then_inc(s_rr.sem, s_rr.nth(0))
                dve.wait_ge(s_wf_mm.sem, s_wf_mm.at(l))
                V.tensor_copy(wf_m[:].rearrange("p i c n -> p (i c n)"), ps[:, 6, :]).then_inc(s_wf_m.sem, s_wf_m.nth(l))
                for k in range(KD + 1):
                    if k < KD:
                        dve.wait_ge(s_nt.sem, s_nt.at((l, k)))
                        if k >= 2:
                            dve.wait_ge(s_lo.sem, s_lo.at((l, "n", k - 2)))
                        step(V.tensor_scalar(tmp_n[:, k % 2, 0:SEQ], ps[:, k % 4, :], mod_a[:, 0, k:k + 1], mod[:, 0, k:k + 1], ALU.mult, ALU.add))
                        V.tensor_scalar(tmp_n[:, k % 2, SEQ:], ps[:, 4 + k % 2, 0:CTX], mod_a[:, 1, k:k + 1], mod[:, 1, k:k + 1],
                                              ALU.mult, ALU.add).then_inc(s_mod_x.sem, s_mod_x.nth((l, k)))
                    if k > 0:
                        lo_part(h_lo[:, k - 1, :], tmp_n[:, (k - 1) % 2, :], h_hi[:, k - 1, :], (l, "n", k - 1), (l, "n", k - 1))
                for g in range(nt // 2):
                    dve.wait_ge(s_uf_hi.sem, s_uf_hi.at((l, g)))
                    V.tensor_tensor(uf_lo[:, 2 * g:2 * g + 2, :].rearrange("p t c -> p (t c)"), ps[:, (6, 7, 5)[g], :],
                                          uf_hi[:, 2 * g:2 * g + 2, :].rearrange("p t c -> p (t c)").bitcast(F32), ALU.subtract).then_inc(s_uf_lo.sem, s_uf_lo.nth((l, g)))
                for i in range(5):
                    x_ = q1[:, i, 0:SEQ] if i < 4 else k1[:, 0:SEQ]
                    dve.wait_ge(s_rot.sem, s_rot.at((l, i)))
                    step(V.tensor_tensor(tmp_p[:, i % 2, 0:SEQ], ps[:, 6 + i % 2, :], sin1[:], ALU.mult))
                    step(V.tensor_tensor(x_, x_, cos1[:], ALU.mult))
                    V.tensor_tensor(x_, x_, tmp_p[:, i % 2, 0:SEQ], ALU.add).then_inc(s_roped.sem, s_roped.nth((l, i)))
                n_fm = 5 + 6
                for c in range(2):
                    for part in range(parts):
                        b, n, a = (n_fm % 4, SEQ, 0) if part == 0 else (4 + n_fm % 2, CTX, SEQ)
                        dve.wait_ge(s_mm.sem, s_mm.at((l, ("cc",), c, part)))
                        dve.wait_ge(s_proj.sem, s_proj.at((l, ("zc",), c, part)))
                        V.tensor_tensor(cz[:, c, a:a + n], ps[:, b, 0:n], cz[:, c, a:a + n], ALU.mult).then_inc(s_conv_t.sem, s_conv_t.nth((l, ("cc",), c, part)))
                    n_fm += 1
                for c in range(2):
                    dve.wait_ge(s_proj.sem, s_proj.at((l, ("gc",), c, parts - 1)))
                    V.tensor_tensor(cb[:, c, 0:nc_], cb[:, c, 0:nc_], tmp_p[:, c, 0:nc_], ALU.mult).then_inc(s_conv_gate.sem, s_conv_gate.nth((l, c)))
                dve.wait_ge(s_conv_gate.sem, s_conv_gate.at((l, 1)))
                dve.wait_ge(s_mm.sem, s_mm.at((l, ("ga", 1), 1, parts - 1)))
                cw, bias = VB[l]["conv_w"], VB[l]["conv_b"]
                for c in range(2):
                    tap = [vec_t[:, cw + 2 * j + c:cw + 2 * j + c + 1] for j in range(3)]
                    for part in range(parts):
                        a, n = (0, SEQ) if part == 0 else (SEQ, CTX)
                        z, o = cz[:, c, a:a + n], conv_y[:, c, a:a + n]
                        step(V.tensor_scalar(o, z, tap[1], vec_t[:, bias + c:bias + c + 1], ALU.mult, ALU.add))
                        step(V.scalar_tensor_tensor(o[:, 1:n], z[:, 0:n - 1], tap[0], o[:, 1:n], ALU.mult, ALU.add))
                        step(V.scalar_tensor_tensor(o[:, 0:n - 1], z[:, 1:n], tap[2], o[:, 0:n - 1], ALU.mult, ALU.add))
                    V.tensor_tensor(cb[:, c, 0:nc_], cb[:, c, 0:nc_], conv_y[:, c, 0:nc_], ALU.mult).then_inc(s_side.sem, s_side.nth((l, 2 + c)))
                for c in range(2):
                    for part in range(parts):
                        b, n, a = (6 + c, SEQ, 0) if part == 0 else (4 + c, CTX, SEQ)
                        dve.wait_ge(s_fmix.sem, s_fmix.at((l, c, part)))
                        V.tensor_tensor(gf[:, c, a:a + n], ps[:, b, 0:n], gf[:, c, a:a + n], ALU.mult).then_inc(s_side.sem, s_side.nth((l, c)))
                attend(l, units1(l), lambda st: None)
                for t in range(nt + 1):
                    if t < nt:
                        dve.wait_ge(s_aot.sem, s_aot.at((l, t)))
                        if t >= 2:
                            dve.wait_ge(s_lo.sem, s_lo.at((l, "m", t - 2)))
                        V.tensor_tensor(tmp_m[:, t % 2, :].rearrange("p (c n) -> p c n", c=4),
                                              ps[:, t % 4, :].rearrange("p (c n) -> p c n", c=4), ga[:, :, P * t:P * t + P], ALU.mult).then_inc(s_gated.sem, s_gated.nth((l, t)))
                    if t > 0:
                        lo_part(h_lo[:, 0:4, P * (t - 1):P * t], tmp_m[:, (t - 1) % 2, :].rearrange("p (c n) -> p c n", c=4),
                                h_hi[:, 0:4, P * (t - 1):P * t], (l, "m", t - 1), (l, "m", t - 1))
                for c in range(4):
                    src = gf[:, c, 0:nc_] if c < 2 else cb[:, c - 2, 0:nc_]
                    lo_part(h_lo[:, 4 + c, 0:nc_], src, h_hi[:, 4 + c, 0:nc_], (l, "s", c), (l, "s", c))
                if l + 1 < DEPTH:
                    mods_out(l + 1, 0, 16, (l + 1, 0))
                    scale_and_shift(l + 1)
                mods_out(l, 16, 24, (l, 1))
                dve.wait_ge(s_lo.sem, s_lo.at((l, "s", 3)))
                for s in range(parts):
                    step(V.tensor_tensor(mod_g[:, s, :], mod[:, s, 16:24], vec_t[:, VB[l]["g_post"]:VB[l]["g_post"] + KD], ALU.mult))
                    for c in range(KD):
                        m = V.tensor_scalar(diag[:, s, c, :], ident[:], mod_g[:, s, c:c + 1], None, ALU.mult).then_inc(s_diag.sem, s_diag.nth((l, s)))
                dve.wait_ge(s_ssq.sem, s_ssq.at((l, "post", nt - 1)))
                V.tensor_scalar(ssq[:, 0:nt], ssq[:, 0:nt], 1.0 / D, EPS, ALU.mult, ALU.add).then_inc(s_var.sem, s_var.nth((l, "post")))
                inverse((l, "post"), nt)
                for t in range(nt):
                    s = 0 if t < XT else 1
                    x_ = res[:, t, :] if t < XT else res_c[:, t - XT, :]
                    dve.wait_ge(s_gate_b.sem, s_gate_b.at((l, s)))
                    step(V.scalar_tensor_tensor(y1[:, t, :], y1[:, t, :], rstd[:, t:t + 1], gate_b[:, s, :], ALU.mult, ALU.mult))
                    V.tensor_tensor(x_, x_, y1[:, t, :], ALU.add).then_inc(s_x_final.sem, s_x_final.nth((l, t)))

            for l in range(DEPTH):
                y = DEPTH + l
                for k in range(KD):
                    lo_part(g_lo[:, k, :], ps[:, k % 4, :], g_hi[:, k, :], (y, "t", k), (y, "t", k))
                dve.wait_ge(s_layer_consts.sem, s_layer_consts.at(y))
                for i in range(2):
                    m = V.tensor_tensor_reduce(dlam[:, 64 * i:64 * i + 32], dlam[:, 64 * i:64 * i + 32], dlam[:, 64 * i + 32:64 * i + 64],
                                               1.0, 0.0, ALU.mult, ALU.add, lam[:, i:i + 1])
                    if i == 0:
                        step(m)
                m.then_inc(s_lam_sums.sem, s_lam_sums.nth(y))
                dve.wait_ge(s_lam_exp.sem, s_lam_exp.at(y))
                step(V.scalar_tensor_tensor(lam[:, 4:5], lam[:, 3:4], lam[:, 2:3], lam_c[:, 0:1], ALU.subtract, ALU.add))
                dve.wait_ge(s_ssq.sem, s_ssq.at((y, "c", 7)))
                step(V.tensor_scalar(ssq[:, 0:4], ssq[:, 0:4], 1.0 / 256, EPS, ALU.mult, ALU.add))
                V.tensor_scalar(ssq[:, 4:8], ssq[:, 4:8], 1.0 / 128, EPS, ALU.mult, ALU.add).then_inc(s_var.sem, s_var.nth((y, "c")))
                inverse((y, "c"), 8)
                for t in range(XT):
                    step(V.tensor_scalar(c_in[:, t, 0:256], c_in[:, t, 0:256], rstd[:, t:t + 1], None, ALU.mult))
                    V.tensor_scalar(c_in[:, t, 256:384], c_in[:, t, 256:384], rstd[:, 4 + t:5 + t], None, ALU.mult).then_inc(s_latn.sem, s_latn.nth((y, t)))
                for i in range(3):
                    dve.wait_ge(s_lat_t.sem, s_lat_t.at((y, i)))
                    gain = LG + 2 * l + i if i < 2 else LG + 4 + l
                    V.tensor_scalar(tmp_c[:, i % 2, :], ps[:, i, :], vec_t[:, gain:gain + 1], None, ALU.mult).then_inc(s_lat.sem, s_lat.nth((y, i)))
                    dve.wait_ge(s_lat.sem, s_lat.at((y, i)))
                    hi, lo = (cq_hi[:, i, :], cq_lo[:, i, :]) if i < 2 else (ckv_hi[:], ckv_lo[:])
                    lo_part(lo, tmp_c[:, i % 2, :], hi, (y, "c", i), (y, "c", i))
                dve.wait_ge(s_lo.sem, s_lo.at((y, "c", 2)))
                R = slice(HD, QC)

                def rope(x_, bank, slot):
                    step(V.tensor_tensor(tmp_c[R, slot, :], ps[R, bank, :], sin2[R, :], ALU.mult))
                    step(V.tensor_tensor(x_, x_, cos2[R, :], ALU.mult))
                    return V.tensor_tensor(x_, x_, tmp_c[R, slot, :], ALU.add)

                dve.wait_ge(s_lat_t.sem, s_lat_t.at((y, 3)))
                V.tensor_copy(kc[R, 0, :], ps[R, 3, :]).then_inc(s_kr_raw.sem, s_kr_raw.nth(y))
                dve.wait_ge(s_kr_rot.sem, s_kr_rot.at(y))
                step(rope(kc[R, 0, :], 5, 0))
                for h in range(1, C_HEADS):
                    m = V.tensor_copy(kc[R, h, :], kc[R, 0, :]).then_inc(s_kr_all.sem, s_kr_all.nth(y))
                for h in range(C_HEADS):
                    dve.wait_ge(s_q_rot.sem, s_q_rot.at((y, h)))
                    rope(qc[R, h, :], 6 + h % 2, h % 2).then_inc(s_roped.sem, s_roped.nth((y, h)))
                dve.wait_ge(s_strips.sem, s_strips.at(y))

                def sub_norm(st):
                    o = ao2[:, :, 384:640].rearrange("p t (h d) -> p t h d", d=HD)
                    sq = sq_b[:].rearrange("p (t h) d -> p t h d", t=XT)
                    if st == N_B + 5:
                        dve.wait_ge(s_o_out.sem, s_o_out.at((y, N_B - 1)))
                        step(V.tensor_tensor(sq, o, o, ALU.mult))
                        step(V.tensor_reduce(ssq[:, 0:16], sq_b[:], AX_X, ALU.add))
                        V.tensor_scalar(ssq[:, 0:16], ssq[:, 0:16], 1.0 / HD, 1e-5, ALU.mult, ALU.add).then_inc(s_var.sem, s_var.nth((y, "sub")))
                    if st == N_B + 13:
                        inverse((y, "sub"), 16)
                        step(V.tensor_scalar(rstd[:, 0:16], rstd[:, 0:16], lam_c[:, 1:2], None, ALU.mult))
                        r = rstd[:, 0:16].rearrange("p (t h) -> p t h", t=XT).unsqueeze(3).broadcast_to((P, XT, B_HEADS, HD))
                        g = subln[:].unsqueeze(1).unsqueeze(1).broadcast_to((P, XT, B_HEADS, HD))
                        step(V.tensor_tensor(o, o, r, ALU.mult))
                        V.tensor_tensor(o, o, g, ALU.mult).then_inc(s_sub.sem, s_sub.nth(y))

                attend(y, units2(), sub_norm)
                for t in range(XT):
                    for g in range(2):
                        lo_part(g_lo[:, 4 * g:4 * g + 4, P * t:P * t + P], ps[:, 2 * (t % 2) + g, :].rearrange("p (c n) -> p c n", c=4),
                                g_hi[:, 4 * g:4 * g + 4, P * t:P * t + P], (y, "m", t, g), (y, "m", t, g))

                def residual(n, ch, t, key, bank):
                    dve.wait_ge(s_mm.sem, s_mm.at(key))
                    x_ = res[:, t, 512 * ch:512 * ch + 512]
                    V.scalar_tensor_tensor(x_, x_, ALPHA, ps[:, bank, :], ALU.mult, ALU.add).then_inc(s_resid.sem, s_resid.nth((y, n, ch, t)))
                    dve.wait_ge(s_resid.sem, s_resid.at((y, n, ch, t)))
                    step(V.bn_stats(bn[:, t, ch, :], x_))

                def norm(n, w, done):
                    for t in range(XT):
                        step(V.bn_aggr(mean_var[:, t, :], bn[:, t, :, :].rearrange("p c s -> p (c s)")))
                    V.tensor_scalar(ssq[:, 0:XT], mean_var[:, :, 1], LN_EPS, None, ALU.add).then_inc(s_var.sem, s_var.nth((y, n)))
                    inverse((y, n), XT)
                    dve.wait_ge(s_ln.sem, s_ln.at((y, n)))
                    for t in range(XT):
                        step(V.tensor_scalar(res[:, t, :], res[:, t, :], mean_var[:, t, 0:1], rstd[:, t:t + 1], ALU.subtract, ALU.mult))
                        step(V.tensor_tensor(res[:, t, :], res[:, t, :], w[:, 0, :], ALU.mult))
                        V.tensor_tensor(res[:, t, :], res[:, t, :], w[:, 1, :], ALU.add).then_inc(done.sem, done.nth((y, t)))

                for ch in range(2):
                    for t in range(XT):
                        residual(1, ch, t, (y, "o", ch, t), 4 * ch + t)
                norm(1, ln1, s_normed)
                for k in range(KD):
                    lo_part(g_lo[:, k, :], ps[:, k % 4, :], g_hi[:, k, :], (y, "h", k), (y, "h", k))
                for j in range(FC):
                    dve.wait_ge(s_silu.sem, s_silu.at((y, j)))
                    dve.wait_ge(s_mm.sem, s_mm.at((y, "ffup", j)))
                    V.tensor_tensor(tmp_f[:, 2 + j % 2, :], ps[:, 2 * (j % 3) + 1, :], tmp_f[:, j % 2, :], ALU.mult).then_inc(s_glu.sem, s_glu.nth((y, j)))
                    dve.wait_ge(s_glu.sem, s_glu.at((y, j)))
                    lo_part(hid_lo[:, j, :], tmp_f[:, 2 + j % 2, :], hid_hi[:, j, :], (y, "f", j), (y, "f", j))
                for t in range(XT):
                    for ch in range(2):
                        residual(2, ch, t, (y, "down", FC // 2 - 1, ch, t), 2 * t + ch)
                norm(2, ln2, s_x_final)


_INS = ["x", "c", "ctx", "c_ctx", "w_mod", "b_mod", "g_pre", "g_post", "w_in", "w_out", "sink", "w_fourier",
        "conv_w", "conv_b", "rel_bias_2", "w_in_2", "q_norm_g_2", "kv_norm_g_2", "w_uq_2", "w_ukv_2",
        "diff_lambda_2", "subln_g_2", "w_o_2", "ln1_g_2", "ln1_b_2", "ln2_g_2", "ln2_b_2", "w_gate_2", "w_up_2", "w_down_2"]


def kernel(**inputs):
    import concourse.bacc as bacc
    from concourse.bass_utils import run_bass_kernel_spmd

    arrays = {f"in_{n}": np.ascontiguousarray(inputs[n]) for n in _INS}
    arrays.update({f"in_{n}": np.ascontiguousarray(a) for n, a in _constants().items()})
    seen = {}
    for _ in range(2):
        nc = bacc.Bacc("TRN2", target_bir_lowering=False, num_devices=1)
        aps = {n[3:]: nc.dram_tensor(n, a.shape, F32, kind="ExternalInput").ap() for n, a in arrays.items()}
        y = nc.dram_tensor("y", (1, SEQ, D), F32, kind="ExternalOutput").ap()
        _program(nc, aps, y, seen)
    return run_bass_kernel_spmd(nc, [arrays], core_ids=[0]).results[0]["y"]
```

```python
from contextlib import ExitStack

import numpy as np

import concourse.bass as bass
from concourse import mybir

F32 = mybir.dt.float32
F32R = mybir.dt.float32r
ALU = mybir.AluOpType
ACT = mybir.ActivationFunctionType
AX_X = mybir.AxisListType.X

P = 128
D = 1024
KD = D // P
SEQ, CTX, DEPTH = 512, 256, 2
XT, CT = SEQ // P, CTX // P
TOK = SEQ + CTX
NT = XT + CT
HD = 64
EPS = 1e-6
HEADS, KVH = 8, 2
FF = 2816
FC = FF // P
A_HEADS, B_HEADS, C_HEADS = 6, 4, 6
BUCKETS = 32
ALPHA = (2 * DEPTH) ** 0.25
LN_EPS = 1e-5
FAR = 1.0e30
RAW, SPLIT = 3, 2
TILE = 2048
ROPE = 32
QC = HD + ROPE


class Signal:

    def __init__(self, nc, ctx, seen, name):
        self.sem = ctx.enter_context(nc.semaphore(name))
        self.seen = seen.setdefault(name, {})
        self.count = 0

    def nth(self, key, by=1):
        self.count += by
        self.seen[key] = self.count
        return by

    def name_latest(self, key):
        self.seen[key] = self.count

    def at(self, key):
        return self.seen.get(key, 1)

    def after(self, key):
        return self.sem, self.at(key)


def _constants():
    f = np.float32
    c = {}
    c["ident"] = np.eye(P, dtype=f)
    pos = np.arange(SEQ)
    inv = np.power(f(10000.0), -np.arange(16, dtype=f) / f(16)).astype(f)
    ang = np.stack([(pos // 64).astype(f)[:, None] * inv, (pos % 64).astype(f)[:, None] * inv], 1)
    rows = np.arange(P)
    axis, freq = (rows % 64) // 32, rows % 16
    c["cos1"] = np.ascontiguousarray(np.cos(ang)[:, axis, freq].T.astype(f))
    c["sin1"] = np.ascontiguousarray(np.sin(ang)[:, axis, freq].T.astype(f))

    def rotation(n, half):
        r = np.zeros((n, n), f)
        for i in range(n):
            first = (i % (2 * half)) < half
            r[i + half if first else i - half, i] = -1.0 if first else 1.0
        return r

    c["rot1"] = rotation(P, 16)
    inv2 = np.power(f(10000.0), -np.arange(16, dtype=f) / f(16)).astype(f)
    ang2 = pos.astype(f)[:, None] * inv2
    c["cos2"] = np.ascontiguousarray(np.tile(np.cos(ang2).T, (2, 1)).astype(f))
    c["sin2"] = np.ascontiguousarray(np.tile(np.sin(ang2).T, (2, 1)).astype(f))
    rot2 = np.zeros((ROPE, QC), f)
    rot2[:, HD:] = rotation(ROPE, 16)
    c["rot2"] = rot2
    q, k = np.arange(P)[:, None], np.arange(3 * P)[None, :] - P
    band = np.where(np.abs(q - k) <= P, 0.0, FAR).astype(f)
    c["band_mid"] = np.concatenate([band, np.zeros((P, CTX), f)], 1)
    c["band_last"] = np.concatenate([band[:, :2 * P], np.zeros((P, CTX), f)], 1)
    for n in (SEQ, CTX):
        t = np.outer(np.arange(n), np.arange(n)) % n * (2 * np.pi / n)
        c[f"dft_cos{n}"] = (np.cos(t) / np.sqrt(n)).astype(f)
        c[f"dft_sin{n}"] = (np.sin(t) / np.sqrt(n)).astype(f)
    t = np.outer(np.arange(HD), np.arange(HD)) % HD * (2 * np.pi / HD)
    two = np.eye(2)
    c["dft_ccos"] = np.kron(two, np.cos(t) / 8.0).astype(f)
    c["dft_csin"] = np.kron(two, -np.sin(t) / 8.0).astype(f)
    dist = SEQ - 1 - np.arange(SEQ + P)
    df = np.maximum(dist, 1).astype(f)
    large = 16 + (np.log(df / f(16)) / f(np.log(2048 / 16)) * f(16)).astype(np.int32)
    bucket = np.where(dist < 16, np.maximum(dist, 0), np.minimum(large, BUCKETS - 1))
    hot = np.zeros((BUCKETS + 2, SEQ + P), f)
    hot[bucket, np.arange(SEQ + P)] = (dist >= 0)
    times = (dist <= P).astype(int) + (dist % 4 == 0) + (dist % 16 == 0)
    ok = dist >= 0
    hot[BUCKETS] = np.where(ok & (times > 0), np.log(np.maximum(times, 1)), -FAR)
    hot[BUCKETS + 1] = np.where(ok, 0.0, -FAR)
    c["hot"] = hot
    pick = np.zeros((2, A_HEADS + B_HEADS), f)
    pick[0, :A_HEADS] = 1.0
    pick[1, A_HEADS:] = 1.0
    c["pick"] = pick
    c["fold"] = np.tile(np.eye(2, dtype=f), (2, 1))
    d2 = 384 + np.arange(P)[:, None] - np.arange(SEQ)[None, :]
    c["causal"] = np.where(d2 >= 0, 0.0, FAR).astype(f)
    init = [0.8 - 0.6 * np.exp(-0.3 * l) for l in range(DEPTH)]
    c["lam_init"] = np.array([[-i, 1.0 - i] for i in init], f)
    return c


def _program(nc, I, out, seen):
    ctx = ExitStack()
    with ctx:
        base = -(-nc.sbuf_base // 64) * 64
        names = {}

        def at(name, shape, off, dt=F32):
            n = 4 * int(np.prod(shape[1:]))
            assert base + off + n <= nc.sbuf_usable_end, (name, off, n)
            names[name] = (off, n)
            return nc.alloc_sbuf_tensor_at(name, shape, dt, offset=base + off)

        off = 0

        def put(name, shape, dt=F32):
            nonlocal off
            t = at(name, shape, off, dt)
            off += -(-4 * int(np.prod(shape[1:])) // 32) * 32
            return t

        raw = put("raw", [P, RAW, TILE])
        w_hi = put("w_hi", [P, SPLIT, TILE], F32R)
        w_lo = put("w_lo", [P, SPLIT, TILE], F32R)
        ident = put("ident", [P, P])
        ones = put("ones", [P, P])
        rot1 = put("rot1", [P, P])
        rot2 = put("rot2", [P, QC])
        vec = put("vec", [P, P])
        vec_t = put("vec_t", [P, P])
        cond = put("cond", [P, KD, 2])
        cond_hl = put("cond_hl", [P, KD, 4], F32R)
        mod = put("mod", [P, 2, 24])
        mod_a = put("mod_a", [P, 2, KD])
        mod_g = put("mod_g", [P, 2, KD])
        ssq = put("ssq", [P, 16])
        rstd = put("rstd", [P, 16])
        mean_var = put("mean_var", [P, XT, 2])
        bn = put("bn", [P, XT, 2, 6])
        small = put("small", [P, 3, 8])
        sinks = put("sinks", [P, DEPTH * HEADS])
        lam_c = put("lam_c", [P, 2])
        lam = put("lam", [P, 8])
        table = put("table", [BUCKETS + 2, A_HEADS + B_HEADS])
        res = put("res", [P, XT, D])
        res_c_at = off
        res_c = put("res_c", [P, CT, D])
        ph = off
        h_hi = put("h_hi", [P, KD, TOK], F32R)
        h_lo = put("h_lo", [P, KD, TOK], F32R)
        mix_at = off
        q1 = put("q1", [P, 4, TOK])
        k1 = put("k1", [P, TOK])
        ga = put("ga", [P, 4, TOK])
        gf = put("gf", [P, 2, TOK])
        cz = put("cz", [P, 2, TOK])
        cb = put("cb", [P, 2, TOK])
        v1 = put("v1", [P, NT, P])
        uf_at = off
        uf_hi = put("uf_hi", [P, NT, 256], F32R)
        uf_lo = put("uf_lo", [P, NT, 256], F32R)
        cos1 = put("cos1", [P, SEQ])
        sin1 = put("sin1", [P, SEQ])
        band_mid = put("band_mid", [P, 5 * P])
        band_last = put("band_last", [P, 4 * P])
        dft_ccos = put("dft_ccos", [P, P])
        dft_csin = put("dft_csin", [P, P])
        wf = put("wf", [P, DEPTH, 2, P])
        wf_m = put("wf_m", [P, 2, 2, P])
        mod_row = put("mod_row", [4, 2, 256])
        fold = put("fold", [4, 2])
        xn = at("xn", [P, NT, D], mix_at)
        tmp_n = at("tmp_n", [P, 3, SEQ], names["cz"][0])
        tmp_x = at("tmp_x", [P, KD, CTX], names["cb"][0])
        assert names["cb"][1] + names["v1"][1] >= 4 * KD * CTX
        tmp_p = at("tmp_p", [P, 2, TOK], names["ga"][0])
        four = at("four", [P, 2, 2, TOK], names["h_hi"][0] + 4 * 4 * TOK)
        conv_y = at("conv_y", [P, 2, TOK], names["h_lo"][0] + 4 * 4 * TOK)
        sc = at("sc", [P, 4, 5 * P + 8], names["h_hi"][0])
        pt = at("pt", [P, 2, 5 * P], names["h_lo"][0])
        k_twice = at("k_twice", [P, KVH, TOK], names["h_lo"][0] + 4 * 2 * 5 * P, F32R)
        k1_lo = at("k1_lo", [P, TOK], names["k1"][0], F32R)
        q_parts = at("q_parts", [P, 2, TOK], names["cz"][0], F32R)
        assert 4 * (2 * 5 * P + KVH * TOK) <= 4 * 4 * TOK
        ao1 = at("ao1", [P, NT, 512], uf_at)
        tmp_m = at("tmp_m", [P, 2, 512], names["q1"][0])
        y1 = at("y1", [P, NT, D], mix_at)
        gate_b = at("gate_b", [P, 2, D], names["gf"][0])
        diag = at("diag", [P, 2, KD, P], names["gf"][0] + 8 * D)
        assert names["ga"][0] + names["ga"][1] - mix_at >= 4 * NT * D
        assert names["cb"][0] + names["cb"][1] - names["gf"][0] >= 16 * D
        off = res_c_at
        g_hi = put("g_hi", [P, KD, SEQ], F32R)
        g_lo = put("g_lo", [P, KD, SEQ], F32R)
        ao2_at = off
        ao_fm = put("ao_fm", [P, 6, SEQ])
        ao_b = put("ao_b", [P, XT, 256])
        att_at = off
        qa = put("qa", [P, 3, SEQ])
        ka = put("ka", [P, 3, SEQ])
        va = put("va", [P, XT, 384])
        qb = put("qb", [P, 2, SEQ])
        kb = put("kb", [P, 2, SEQ])
        vb = put("vb", [P, XT, 256])
        qc = put("qc", [P, C_HEADS, SEQ])
        kc = put("kc", [P, C_HEADS, SEQ])
        vc = put("vc", [P, XT, 384])
        strip_at = off
        strips = put("strips", [P, 11, SEQ])
        off = strip_at
        c_in = put("c_in", [P, XT, 416])
        cq_hi = put("cq_hi", [P, 2, SEQ], F32R)
        cq_lo = put("cq_lo", [P, 2, SEQ], F32R)
        ckv_hi = put("ckv_hi", [P, SEQ], F32R)
        ckv_lo = put("ckv_lo", [P, SEQ], F32R)
        cos2 = put("cos2", [P, SEQ])
        sin2 = put("sin2", [P, SEQ])
        subln = put("subln", [P, HD])
        dlam = put("dlam", [P, 4 * 32])
        tmp_c = at("tmp_c", [P, 2, SEQ], ao2_at)
        va_fm = at("va_fm", [P, SEQ], ao2_at + 8 * SEQ)
        sc2 = at("sc2", [P, 5, SEQ], names["g_hi"][0])
        pt2 = at("pt2", [P, 2, SEQ], names["g_lo"][0])
        sq_b = at("sq_b", [P, 16, HD], names["g_lo"][0] + 8 * SEQ)
        ln1 = at("ln1", [P, 2, D], att_at)
        ln2 = at("ln2", [P, 2, D], ao2_at)
        off = ao2_at + 4 * 4 * SEQ
        hid_hi = put("hid_hi", [P, FC, SEQ], F32R)
        hid_lo = put("hid_lo", [P, FC, SEQ], F32R)
        tmp_f = at("tmp_f", [P, 4, SEQ], ao2_at)
        rr = at("rr", [A_HEADS + B_HEADS, SEQ + P], uf_at)
        hot = at("hot", [BUCKETS + 2, SEQ + P], uf_at + 4 * (SEQ + P))
        junk = at("junk", [P, D], uf_at)

        ps = ctx.enter_context(nc.psum_tensor("ps", [P, 8, 512], F32))
        ps_flat = ps[:].rearrange("p b n -> p (b n)")
        scratch = nc.dram_tensor("bias_rows", [A_HEADS + B_HEADS, P * (SEQ + P)], F32).ap()

        s_aot = Signal(nc, ctx, seen, "aot")
        s_bias_rows = Signal(nc, ctx, seen, "bias_rows")
        s_cond = Signal(nc, ctx, seen, "cond")
        s_cond_hi = Signal(nc, ctx, seen, "cond_hi")
        s_cond_lo = Signal(nc, ctx, seen, "cond_lo")
        s_consts = Signal(nc, ctx, seen, "consts")
        s_conv_gate = Signal(nc, ctx, seen, "conv_gate")
        s_conv_t = Signal(nc, ctx, seen, "conv_t")
        s_diag = Signal(nc, ctx, seen, "diag")
        s_dve_step = Signal(nc, ctx, seen, "dve_step")
        s_fmix = Signal(nc, ctx, seen, "fmix")
        s_four_out = Signal(nc, ctx, seen, "four_out")
        s_gate_b = Signal(nc, ctx, seen, "gate_b")
        s_gate_mm = Signal(nc, ctx, seen, "gate_mm")
        s_gated = Signal(nc, ctx, seen, "gated")
        s_glu = Signal(nc, ctx, seen, "glu")
        s_hi = Signal(nc, ctx, seen, "hi")
        s_hi_c = Signal(nc, ctx, seen, "hi_c")
        s_ht = Signal(nc, ctx, seen, "ht")
        s_k_hi = Signal(nc, ctx, seen, "k_hi")
        s_k_lo = Signal(nc, ctx, seen, "k_lo")
        s_kr_all = Signal(nc, ctx, seen, "kr_all")
        s_kr_raw = Signal(nc, ctx, seen, "kr_raw")
        s_kr_rot = Signal(nc, ctx, seen, "kr_rot")
        s_lam_exp = Signal(nc, ctx, seen, "lam_exp")
        s_lam_sums = Signal(nc, ctx, seen, "lam_sums")
        s_lat = Signal(nc, ctx, seen, "lat")
        s_lat_t = Signal(nc, ctx, seen, "lat_t")
        s_latn = Signal(nc, ctx, seen, "latn")
        s_layer_consts = Signal(nc, ctx, seen, "layer_consts")
        s_ln = Signal(nc, ctx, seen, "ln")
        s_lo = Signal(nc, ctx, seen, "lo")
        s_lo_c = Signal(nc, ctx, seen, "lo_c")
        s_mixed = Signal(nc, ctx, seen, "mixed")
        s_mm = Signal(nc, ctx, seen, "mm")
        s_mod = Signal(nc, ctx, seen, "mod")
        s_mod_c = Signal(nc, ctx, seen, "mod_c")
        s_mod_out = Signal(nc, ctx, seen, "mod_out")
        s_mod_row = Signal(nc, ctx, seen, "mod_row")
        s_mod_x = Signal(nc, ctx, seen, "mod_x")
        s_normed = Signal(nc, ctx, seen, "normed")
        s_nt = Signal(nc, ctx, seen, "nt")
        s_o_out = Signal(nc, ctx, seen, "o_out")
        s_ones = Signal(nc, ctx, seen, "ones")
        s_paired = Signal(nc, ctx, seen, "paired")
        s_probs = Signal(nc, ctx, seen, "probs")
        s_proj = Signal(nc, ctx, seen, "proj")
        s_pt = Signal(nc, ctx, seen, "pt")
        s_q_hi = Signal(nc, ctx, seen, "q_hi")
        s_q_lo = Signal(nc, ctx, seen, "q_lo")
        s_q_rot = Signal(nc, ctx, seen, "q_rot")
        s_recip = Signal(nc, ctx, seen, "recip")
        s_resid = Signal(nc, ctx, seen, "resid")
        s_root = Signal(nc, ctx, seen, "root")
        s_roped = Signal(nc, ctx, seen, "roped")
        s_rot = Signal(nc, ctx, seen, "rot")
        s_rr = Signal(nc, ctx, seen, "rr")
        s_rr_mm = Signal(nc, ctx, seen, "rr_mm")
        s_scored = Signal(nc, ctx, seen, "scored")
        s_scores = Signal(nc, ctx, seen, "scores")
        s_shared_lo = Signal(nc, ctx, seen, "shared_lo")
        s_side = Signal(nc, ctx, seen, "side")
        s_silu = Signal(nc, ctx, seen, "silu")
        s_ssq = Signal(nc, ctx, seen, "ssq")
        s_stored = Signal(nc, ctx, seen, "stored")
        s_strips = Signal(nc, ctx, seen, "strips")
        s_sub = Signal(nc, ctx, seen, "sub")
        s_tile_hi = Signal(nc, ctx, seen, "tile_hi")
        s_tile_lo = Signal(nc, ctx, seen, "tile_lo")
        s_turned = Signal(nc, ctx, seen, "turned")
        s_uf_hi = Signal(nc, ctx, seen, "uf_hi")
        s_uf_lo = Signal(nc, ctx, seen, "uf_lo")
        s_v_out = Signal(nc, ctx, seen, "v_out")
        s_v_turned = Signal(nc, ctx, seen, "v_turned")
        s_var = Signal(nc, ctx, seen, "var")
        s_vec_mm = Signal(nc, ctx, seen, "vec_mm")
        s_vec_t = Signal(nc, ctx, seen, "vec_t")
        s_vectors = Signal(nc, ctx, seen, "vectors")
        s_wf_landed = Signal(nc, ctx, seen, "wf_landed")
        s_wf_m = Signal(nc, ctx, seen, "wf_m")
        s_wf_mm = Signal(nc, ctx, seen, "wf_mm")
        s_wf_zero = Signal(nc, ctx, seen, "wf_zero")
        s_x_final = Signal(nc, ctx, seen, "x_final")
        s_x_landed = Signal(nc, ctx, seen, "x_landed")
        s_xn = Signal(nc, ctx, seen, "xn")
        s_xt = Signal(nc, ctx, seen, "xt")
        s_y = Signal(nc, ctx, seen, "y")
        s_y_gated = Signal(nc, ctx, seen, "y_gated")

        def cols(w, a, b):
            return w[:, a:b].rearrange("(k p) c -> p k c", p=P)

        def mod_tile(l, j):
            return ((l, "mod", j), [(lambda r: r.rearrange("p (k c) -> p k c", k=KD),
                                     cols(I["w_mod"][l], 256 * j, 256 * j + 256))], True)

        def mix_tiles(l):
            t = []

            def proj(what, parts):
                t.append(((l, *what), [(lambda r, o=o, n=n: r.rearrange("p (k c) -> p k c", k=KD)[:, :, o:o + n],
                                        cols(I["w_in"][l], a, a + n)) for o, a, n in parts], True))

            for j in range(2):
                proj(("q", j), [(HD * i, HD * h, HD) for i, h in enumerate((2 * j, 2 * j + 4, 2 * j + 1, 2 * j + 5))])
            proj(("kv",), [(0, 512, 256)])
            for what, a in (("uf", 1280), ("gf", 1536), ("zc", 1792), ("bc", 2048), ("cc", 2304), ("gc", 2560)):
                proj((what,), [(0, a, 256)])
            for j in range(2):
                proj(("ga", j), [(0, 768 + 256 * j, 256)])
            for part in ("cos", "sin"):
                t.append(((l, "dft", part), [(lambda r: r.rearrange("p (k c) -> p k c", k=XT),
                                              I[f"dft_{part}{SEQ}"].rearrange("(k p) c -> p k c", p=P))], True))
            if l < DEPTH - 1:
                t.append(((l, "dft", "ctx"), [
                    (lambda r, i=i: r[:, 512 * i:512 * i + 512].rearrange("p (k c) -> p k c", k=CT),
                     I[f"dft_{part}{CTX}"].rearrange("(k p) c -> p k c", p=P))
                    for i, part in enumerate(("cos", "sin"))], True))
            return t

        def square(w, ch, kh):
            return (lambda r: r.rearrange("p (k c) -> p k c", k=4),
                    w[512 * kh:512 * kh + 512, 512 * ch:512 * ch + 512].rearrange("(k p) c -> p k c", p=P))

        SECOND = ([("c", 0, 1920, 256), ("c", 1, 2176, 160)] + [("a", j, 256 * j, 256) for j in range(3)]
                  + [("av", 0, 768, 256), ("av", 1, 1024, 128), ("up",),
                     ("bq", 0, 1152, 256), ("bk", 0, 1408, 256), ("bv", 0, 1664, 256)])

        def second_tiles(l):
            y = DEPTH + l
            t = []
            for what, *cut in SECOND:
                if what == "up":
                    t.append(((y, "up"), [
                        (lambda r: r[:, 0:2 * 576].rearrange("p (k c) -> p k c", k=2),
                         I["w_uq_2"][l].rearrange("(k p) c -> p k c", p=P)),
                        (lambda r: r[:, 1152:1152 + 768], I["w_ukv_2"][l])], True))
                else:
                    j, a, n = cut
                    t.append(((y, what, j), [(lambda r, n=n: r[:, 0:KD * n].rearrange("p (k c) -> p k c", k=KD),
                                              cols(I["w_in_2"][l], a, a + n))], True))
            for ch in range(2):
                for kh in (1 - ch, ch):
                    t.append(((y, "o", ch, kh), [square(I["w_o_2"][l], ch, kh)], True))
            for j in range(FC):
                t.append(((y, "ff", j), [
                    (lambda r, i=i: r.rearrange("p (k c) -> p k c", k=KD)[:, :, P * i:P * i + P],
                     cols(I[w][l], P * j, P * j + P)) for i, w in enumerate(("w_gate_2", "w_up_2"))], True))
            for j in range(FC // 2):
                t.append(((y, "down", j), [(lambda r: r.rearrange("p (k c) -> p k c", k=2),
                                         I["w_down_2"][l][256 * j:256 * j + 256, :].rearrange("(k p) c -> p k c", p=P))], True))
            return t

        stream = []
        mods_in_attention = {0: [(0, j) for j in range(8, 12)] + [(1, j) for j in range(8)],
                             1: [(1, j) for j in range(8, 12)]}
        for j in range(8):
            stream.append(mod_tile(0, j))
        for l in range(DEPTH):
            outs = [((l, "out", ch, kh), [square(I["w_out"][l], ch, kh)], True) for ch, kh in ((0, 1), (0, 0), (1, 0), (1, 1))]
            stream += mix_tiles(l) + [mod_tile(*m) for m in mods_in_attention[l]] + outs
        for l in range(DEPTH):
            stream += second_tiles(l)
        place = {what: n for n, (what, _, _) in enumerate(stream)}
        splits = [what for what, _, is_split in stream if is_split]
        split_at = {what: i for i, what in enumerate(splits)}
        mods_all = [what for what, _, _ in stream if what[1] == "mod"]
        mod_at = {what: i for i, what in enumerate(mods_all)}
        shared = [what for what, _, _ in stream[:8]]
        POOL_COLS = 640
        landed, counts = [], [0] * RAW
        for n, (_, loads, _) in enumerate(stream):
            counts[n % RAW] += 16 * len(loads)
            landed.append(counts[n % RAW])
        landed_sems = [ctx.enter_context(nc.semaphore(f"tile_landed{r}")) for r in range(RAW)]

        def raw_of(what):
            return raw[:, place[what] % RAW, :]

        def wait_landed(eng, what):
            n = place[what]
            eng.wait_ge(landed_sems[n % RAW], landed[n])

        consts = [(rot1[:], I["rot1"]), (rot2[HD:QC, :], I["rot2"]),
                  (cos1[:], I["cos1"]), (sin1[:], I["sin1"]),
                  (band_mid[:], I["band_mid"]), (band_last[:], I["band_last"]),
                  (sinks[:], I["sink"].rearrange("l h -> (l h)").partition_broadcast(P)),
                  (table[0:BUCKETS, :], I["rel_bias_2"]), (table[BUCKETS:, :], I["pick"]), (hot[:], I["hot"])]
        vectors = [(ident[:], I["ident"]), (fold[:], I["fold"]),
                   (vec[0:8, :], I["c"].rearrange("a (r p) -> (a r) p", p=P)),
                   (vec[8:16, :], I["c_ctx"].rearrange("(r p) -> r p", p=P))]
        VB = []
        for l in range(DEPTH):
            b0 = 16 + 48 * l
            VB.append(dict(b_mod=b0, g_pre=b0 + 24, g_post=b0 + 32, conv_w=b0 + 40, conv_b=b0 + 46))
            vectors += [(vec[b0:b0 + 24, :], I["b_mod"][l].rearrange("(r p) -> r p", p=P)),
                       (vec[b0 + 24:b0 + 32, :], I["g_pre"][l].rearrange("(r p) -> r p", p=P)),
                       (vec[b0 + 32:b0 + 40, :], I["g_post"][l].rearrange("(r p) -> r p", p=P)),
                       (vec[b0 + 40:b0 + 46, :], I["conv_w"][l].rearrange("t (r p) -> (t r) p", p=P)),
                       (vec[b0 + 46:b0 + 48, :], I["conv_b"][l].rearrange("(r p) -> r p", p=P))]
        LG = 16 + 48 * DEPTH
        vectors += [(vec[LG:LG + 4, :], I["q_norm_g_2"].rearrange("l (r p) -> (l r) p", p=P)), (vec[LG + 4:LG + 6, :], I["kv_norm_g_2"])]
        NV = LG + 6

        def units1(l):
            u = []
            for h in range(HEADS):
                b = HD * (h // 4)
                for i in range(XT + (CT if l < DEPTH - 1 else 0)):
                    ctx_v = [v1[:, XT + j, b:b + HD] for j in range(CT)]
                    if i < XT:
                        lo, hi = max(0, i - 1), min(XT - 1, i + 1)
                        n = hi - lo + 1
                        near, past = [(0, P * lo, P * n)], [(P * n, SEQ, CTX)]
                        if hi == XT - 1:
                            near, past = [(0, P * lo, P * n + CTX)], []
                        keys = [(c + a, k + a, min(512, w - a)) for c, k, w in near + past for a in range(0, w, 512)]
                        if keys[-1][0] < 512 < keys[-1][0] + keys[-1][2]:
                            c, k, w = keys.pop()
                            keys += [(c, k, 512 - c), (512, k + 512 - c, w - 512 + c)]
                        vs = [v1[:, j, b:b + HD] for j in range(lo, hi + 1)] + ctx_v
                        mask = band_last[:] if i == XT - 1 else band_mid[:, P if i == 0 else 0:]
                    else:
                        keys, vs, mask = [(0, SEQ, CTX)], ctx_v, band_mid[:, 3 * P:]
                    both, hi_only = q_parts[:, h % 2, P * i:P * i + P], q_parts[b:b + HD, h % 2, P * i:P * i + P]
                    segs = [(c, [(both, k_twice[:, h // 4, k:k + w]), (hi_only, k1_lo[b:b + HD, k:k + w])]) for c, k, w in keys]
                    u.append(dict(head=h, fm=False, segs=segs, vs=vs, mask=mask, pair=None, rank=len(u),
                                  out=ao1[:, i, HD * h:HD * h + HD], sink=sinks[:, l * HEADS + h:l * HEADS + h + 1]))
            return u

        def units2():
            pairs, others = [], [[] for _ in range(XT)]

            def unit(i, q, k, v, head, out, pair=None):
                return dict(head=None, segs=[(0, [(q, k)])], vs=v, mask=strips[:, head, 384 - P * i:SEQ], out=out, sink=None, pair=pair, fm=pair is None, latent=q.shape[0] == QC)

            for h in range(B_HEADS):
                for i in range(XT):
                    pairs.append([])
                    for m, pair in enumerate(("first", "second")):
                        b = HD * (h % 2) + 32 * m
                        pairs[-1].append(unit(i, qb[b:b + 32, h // 2, P * i:P * i + P], kb[b:b + 32, h // 2, 0:P * (i + 1)],
                                              [vb[:, j, HD * h:HD * h + HD] for j in range(i + 1)], A_HEADS + h,
                                              ao_b[:, i, HD * h:HD * h + HD], pair))
            for h in range(A_HEADS):
                b = HD * (h % 2)
                for i in range(XT):
                    others[i].append(unit(i, qa[b:b + HD, h // 2, P * i:P * i + P], ka[b:b + HD, h // 2, 0:P * (i + 1)],
                                       [va[:, j, HD * h:HD * h + HD] for j in range(i + 1)], h, ao_fm[b:b + HD, h // 2, P * i:P * i + P]))
            for h in range(C_HEADS):
                for i in range(XT):
                    others[i].append(unit(i, qc[0:QC, h, P * i:P * i + P], kc[0:QC, h, 0:P * (i + 1)],
                                       [vc[:, j, HD * h:HD * h + HD] for j in range(i + 1)], A_HEADS + B_HEADS,
                                       ao_fm[HD * (h % 2):HD * (h % 2) + HD, 3 + h // 2, P * i:P * i + P]))
            around = ((3, 2), (3, 1), (2, 0), (1, 0))
            u = [others[i].pop() for i in (3, 2, 3, 2)]
            for n, two in enumerate(pairs):
                before, behind = around[n % XT]
                u += [others[before].pop(), *two, others[behind].pop()]
            u += [others[i].pop() for i in (3, 0, 1, 2, 0, 1, 3, 0, 1, 2, 0, 1)]
            assert not any(others)
            rank = 0
            for x in u:
                x["rank"] = None if x["pair"] == "first" else rank
                rank += x["pair"] != "first"
            return u

        LAST_PAIR = max(i for i, u in enumerate(units2()) if u["pair"])
        LAST_LATENT = max(i for i, u in enumerate(units2()) if u["latent"])
        LATENT_SPLIT = LAST_LATENT + 8
        HEAD_CHUNKS = (4, 0, 1, 2, 3)
        MOD_STEP = (4, 6)

        def slots(y):
            return (sc, pt, 1024, (2, 1, 1, 4)) if y < DEPTH else (sc2, pt2, 512, (3, 2, 2, 5))

        block = ctx.enter_context(nc.Block())

        @block.sync
        def _(sp):
            for dst, src in vectors[::2]:
                sp.dma_start(dst, src).then_inc(s_vectors.sem, 16)
            for n, (what, loads, _) in enumerate(stream):
                if n >= RAW:
                    sp.wait_ge(s_tile_lo.sem, s_tile_lo.at(stream[n - RAW][0]))
                    if stream[n - RAW][0] in shared:
                        sp.wait_ge(s_shared_lo.sem, s_shared_lo.at(stream[n - RAW][0]))
                for into, src in loads:
                    sp.dma_start(into(raw[:, n % RAW, :]), src).then_inc(landed_sems[n % RAW], 16)
                if n == RAW - 1:
                    sp.dma_start(res[:], I["x"][0].rearrange("(t p) d -> p t d", p=P)).then_inc(s_x_landed.sem, 16)
                    sp.dma_start(res_c[:], I["ctx"][0].rearrange("(t p) d -> p t d", p=P)).then_inc(s_x_landed.sem, 16)
                if n == 9:
                    for dst, src in consts:
                        sp.dma_start(dst, src).then_inc(s_consts.sem, 16)
                if n == 7:
                    for dst, src in ((dft_ccos[:], I["dft_ccos"]), (dft_csin[:], I["dft_csin"])):
                        sp.dma_start(dst, src).then_inc(s_wf_landed.sem, 16)
                    sp.wait_ge(s_wf_zero.sem, s_wf_zero.at(0))
                    for l in range(DEPTH):
                        for h in range(2):
                            sp.dma_start(wf[HD * h:HD * h + HD, l, :, HD * h:HD * h + HD],
                                         I["w_fourier"][l].rearrange("(c h) a b -> h a c b", h=2)[h]).then_inc(s_wf_landed.sem, 16)
            for t in range(XT):
                sp.wait_ge(s_x_final.sem, s_x_final.at((2 * DEPTH - 1, t)))
                sp.dma_start(out[0, P * t:P * t + P, :], res[:, t, :]).then_inc(s_stored.sem, 16)
            sp.wait_ge(s_stored.sem, 16 * XT)

        @block.gpsimd
        def _(pool):
            pool.memset(ones[:], 1.0).then_inc(s_ones.sem, s_ones.nth(0))
            pool.memset(wf[:], 0.0).then_inc(s_wf_zero.sem, s_wf_zero.nth(0))
            for i, what in enumerate(splits):
                if what == (1, "q", 0):
                    for t in range(NT - 1):
                        x_ = res[:, t, :] if t < XT else res_c[:, t - XT, :]
                        pool.wait_ge(s_y_gated.sem, s_y_gated.at((0, t)))
                        pool.tensor_tensor(x_, x_, y1[:, t, :], ALU.add).then_inc(s_x_final.sem, s_x_final.nth((0, t)))
                if what[1] == "kv":
                    for k in range(KD):
                        pool.wait_ge(s_hi_c.sem, s_hi_c.at((what[0], k)))
                        pool.tensor_tensor(h_lo[:, k, SEQ:], tmp_x[:, k, :], h_hi[:, k, SEQ:].bitcast(F32),
                                           ALU.subtract).then_inc(s_lo_c.sem, s_lo_c.nth((what[0], k)))
                pool.wait_ge(s_tile_hi.sem, s_tile_hi.at(what))
                b = POOL_COLS if what in shared else TILE
                pool.tensor_tensor(w_lo[:, i % SPLIT, 0:b], raw_of(what)[:, 0:b], w_hi[:, i % SPLIT, 0:b].bitcast(F32),
                                         ALU.subtract).then_inc(s_tile_lo.sem, s_tile_lo.nth(what))

        @block.scalar
        def _(act):
            todo = list(splits)

            def split_next(a=0, b=TILE):
                if not todo:
                    return
                what = todo[0]
                i = split_at[what]
                if a == 0:
                    if i >= SPLIT:
                        act.wait_ge(s_mm.sem, s_mm.at(("tile", splits[i - SPLIT])))
                    wait_landed(act, what)
                act.activation(w_hi[:, i % SPLIT, a:b], raw_of(what)[:, a:b], ACT.Copy).then_inc(s_tile_hi.sem, s_tile_hi.nth(what))
                if b == TILE:
                    todo.pop(0)

            def root(key, a, n):
                act.wait_ge(s_var.sem, s_var.at(key))
                act.activation(rstd[:, a:a + n], ssq[:, a:a + n], ACT.Sqrt).then_inc(s_root.sem, s_root.nth(key))

            def squares(l, t):
                src = res[:, t, :] if t < XT else res_c[:, t - XT, :]
                act.activation(xn[:, t, :], src, ACT.Square, accum_out=ssq[:, 8 + t:9 + t]).then_inc(s_ssq.sem, s_ssq.nth((l, "pre", t)))

            def hi_rows(turned, y, what, t):
                for g in range(2):
                    act.wait_ge(turned.sem, turned.at((y, t, g)))
                    act.activation(g_hi[:, 4 * g:4 * g + 4, P * t:P * t + P], ps[:, 2 * (t % 2) + g, :].rearrange("p (c n) -> p c n", c=4),
                                   ACT.Copy).then_inc(s_hi.sem, s_hi.nth((y, what, t, g)))

            def mod_out_row(what):
                i = mod_at[what]
                act.wait_ge(s_mm.sem, s_mm.at(("tile", what)))
                if i >= 2:
                    act.wait_ge(s_mod.sem, s_mod.at(mods_all[i - 2]))
                act.activation(mod_row[:, i % 2, :], ps[0:4, 7, 0:256], ACT.Copy).then_inc(s_mod_row.sem, s_mod_row.nth(what))

            def q_hi(l, h):
                b = HD * (h // 4)
                n = TOK if l < DEPTH - 1 else SEQ
                act.activation(q_parts[b:b + HD, h % 2, 0:n], q1[b:b + HD, h % 4, 0:n], ACT.Copy).then_inc(s_q_hi.sem, s_q_hi.nth((l, h)))

            def exp_units(y, units, at_step):
                s_, t_, width, (n_s, n_t, n_o, n_b) = slots(y)
                for step in range(len(units) + n_b - 1):
                    i = step - (n_b - 1)
                    if i >= 0 and units[i]["rank"] is not None:
                        r = units[i]["rank"]
                        n = P * len(units[i]["vs"])
                        o0 = width * (n_s + r % n_t)
                        act.wait_ge(s_turned.sem, s_turned.at((y, r)))
                        if r >= 2:
                            act.wait_ge(s_mixed.sem, s_mixed.at((y, r - 2)))
                        act.activation(t_[:, r % 2, 0:n], ps_flat[:, o0:o0 + n], ACT.Copy).then_inc(s_pt.sem, s_pt.nth((y, r)))
                    i = step
                    if i < len(units):
                        u = units[i]
                        n = P * len(u["vs"]) + (u["sink"] is not None)
                        act.wait_ge(s_scored.sem, s_scored.at((y, i)))
                        act.activation(s_[:, i % n_b, 0:n], s_[:, i % n_b, 0:n], ACT.Exp, bias=small[:, 0, i % 8:i % 8 + 1], scale=-1.0,
                                       accum_out=small[:, 1, i % 8:i % 8 + 1]).then_inc(s_probs.sem, s_probs.nth((y, i)))
                    at_step(step)

            for dst, src in vectors[1::2]:
                act.dma_start(dst, src).then_inc(s_vectors.sem, 16)
            act.wait_ge(s_vec_t.sem, s_vec_t.at(0))
            act.activation(cond[:], vec_t[:, 0:16].rearrange("p (s k) -> p k s", s=2), ACT.Silu).then_inc(s_cond.sem, s_cond.nth(0))
            act.wait_ge(s_cond.sem, s_cond.at(0))
            act.activation(cond_hl[:, :, 0:2], cond[:], ACT.Copy).then_inc(s_cond_hi.sem, s_cond_hi.nth(0))
            split_next()
            split_next()
            for l in range(DEPTH):
                both = l < DEPTH - 1
                nt, nc_ = (NT, TOK) if both else (XT, SEQ)
                parts = 2 if both else 1
                if l == 0:
                    for j in range(8):
                        mod_out_row((0, "mod", j))
                        split_next()
                        if j == 2:
                            act.wait_ge(s_x_landed.sem, 32)
                        if 2 <= j < 5:
                            squares(0, 2 * j - 4)
                            squares(0, 2 * j - 3)
                        if j == 5:
                            for t in range(NT):
                                root((0, "pre", t), 8 + t, 1)
                for k in range(KD):
                    act.wait_ge(s_mod_x.sem, s_mod_x.at((l, k)))
                    act.activation(tmp_x[:, k, :], ps[:, 4 + k % 2, 0:CTX], ACT.Identity, scale=mod_a[:, 1, k:k + 1],
                                   bias=mod[:, 1, k:k + 1]).then_inc(s_mod_c.sem, s_mod_c.nth((l, k)))
                    act.activation(h_hi[:, k, 0:SEQ], tmp_n[:, k % 3, :], ACT.Copy).then_inc(s_hi.sem, s_hi.nth((l, "n", k)))
                    if k > 0:
                        act.wait_ge(s_mod_c.sem, s_mod_c.at((l, k - 1)))
                        act.activation(h_hi[:, k - 1, SEQ:], tmp_x[:, k - 1, :], ACT.Copy).then_inc(s_hi_c.sem, s_hi_c.nth((l, k - 1)))
                act.wait_ge(s_mod_c.sem, s_mod_c.at((l, KD - 1)))
                act.activation(h_hi[:, KD - 1, SEQ:], tmp_x[:, KD - 1, :], ACT.Copy).then_inc(s_hi_c.sem, s_hi_c.nth((l, KD - 1)))
                n_fm = 0

                def fm(what, c, func, dst, scale=1.0, n_parts=parts):
                    nonlocal n_fm
                    for part in range(n_parts):
                        act.wait_ge(s_mm.sem, s_mm.at((l, what, c, part)))
                        b, n, a = (n_fm % 4, SEQ, 0) if part == 0 else (4 + n_fm % 2, CTX, SEQ)
                        act.activation(dst[:, a:a + n], ps[:, b, 0:n], func, scale=scale).then_inc(s_proj.sem, s_proj.nth((l, what, c, part)))
                    n_fm += 1

                for j in range(2):
                    for c in range(2):
                        fm(("q", j), c, ACT.Copy, q1[:, 2 * j + c, :], scale=-HD ** -0.5)
                    split_next()
                if l == 0:
                    act.wait_ge(s_rr.sem, s_rr.at(0))
                    for h in range(A_HEADS + B_HEADS):
                        act.dma_start(scratch[h].rearrange("(o p n) -> o p n", o=1, n=SEQ + P),
                                      rr[h:h + 1, :].unsqueeze(1).broadcast_to((1, P, SEQ + P))).then_inc(s_bias_rows.sem, 16)
                fm(("kv",), 0, ACT.Copy, k1[:], n_parts=2)
                fm(("kv",), 1, ACT.Copy, cb[:, 0, :], n_parts=2)
                split_next()
                if l == 0:
                    act.wait_ge(s_bias_rows.sem, 16 * (A_HEADS + B_HEADS))
                for g in range(nt // 2):
                    act.wait_ge(s_mm.sem, s_mm.at((l, ("uf",), g, 0)))
                    act.activation(uf_hi[:, 2 * g:2 * g + 2, :].rearrange("p t c -> p (t c)"),
                                         ps[:, (6, 7, 5)[g], :], ACT.Copy).then_inc(s_uf_hi.sem, s_uf_hi.nth((l, g)))
                split_next()
                for part, n in ((0, XT), (1, CT)):
                    act.wait_ge(s_v_turned.sem, s_v_turned.at((l, part)))
                    act.activation(v1[:, XT * part:XT * part + n, :].rearrange("p t c -> p (t c)"),
                                   ps[:, 6 + part, 0:n * P], ACT.Copy).then_inc(s_v_out.sem, s_v_out.nth((l, part)))
                for what, func, dst in (("gf", ACT.Silu, gf), ("zc", ACT.Copy, cz), ("bc", ACT.Copy, cb)):
                    for c in range(2):
                        fm((what,), c, func, dst[:, c, :])
                    split_next()
                n_fm += 2
                split_next()
                act.wait_ge(s_roped.sem, s_roped.at((l, 4)))
                for c in range(2):
                    fm(("gc",), c, ACT.Silu, tmp_p[:, c, :])
                split_next()
                act.wait_ge(s_conv_gate.sem, s_conv_gate.at((l, 1)))
                for j in range(2):
                    for c in range(2):
                        fm(("ga", j), c, ACT.Silu, ga[:, 2 * j + c, :])
                    split_next()
                act.wait_ge(s_proj.sem, s_proj.at((l, ("ga", 1), 1, parts - 1)))
                for g in range(KVH):
                    for half in range(2):
                        act.activation(k_twice[HD * half:HD * half + HD, g, :], k1[HD * g:HD * g + HD, :],
                                       ACT.Copy).then_inc(s_k_hi.sem, s_k_hi.nth((l, g)))
                for i in range(2):
                    for c in range(2):
                        act.wait_ge(s_mm.sem, s_mm.at((l, "four", i, c)))
                        act.activation(four[:, i, c, 0:SEQ], ps[:, 2 * i + c, :], ACT.Copy).then_inc(s_four_out.sem, s_four_out.nth((l, i, c)))
                    if i == 1:
                        act.wait_ge(s_side.sem, s_side.at((l, 3)))
                        q_hi(l, 0)
                        q_hi(l, 1)
                    split_next()
                if both:
                    for i in range(2):
                        act.wait_ge(s_mm.sem, s_mm.at((l, "four", i, "ctx")))
                        act.activation(four[:, i, :, SEQ:], ps[:, 4 + i, :].rearrange("p (c n) -> p c n", c=2),
                                             ACT.Copy).then_inc(s_four_out.sem, s_four_out.nth((l, i, "ctx")))
                    split_next()
                mods = [(m, "mod", j) for m, j in mods_in_attention[l]]

                n_q = len(units1(l)) // HEADS

                halves = []

                def between(step):
                    h = step // n_q + 2
                    if step % n_q == n_q - 1 and h < HEADS:
                        act.wait_ge(s_scores.sem, s_scores.at((l, step)))
                        q_hi(l, h)
                    if step == 0:
                        act.wait_ge(s_fmix.sem, s_fmix.at((l, 1, parts - 1)))
                    if step < 4:
                        act.wait_ge(s_side.sem, s_side.at((l, step)))
                        src = gf[:, step, 0:nc_] if step < 2 else cb[:, step - 2, 0:nc_]
                        act.activation(h_hi[:, 4 + step, 0:nc_], src, ACT.Copy).then_inc(s_hi.sem, s_hi.nth((l, "s", step)))
                    if step % MOD_STEP[l] == 3 and mods:
                        mod_out_row(mods.pop(0))
                        split_next(0, TILE // 2)
                        halves.append(step)
                    elif halves and step == halves[-1] + 2:
                        halves.pop()
                        split_next(TILE // 2, TILE)

                exp_units(l, units1(l), between)
                while mods:
                    mod_out_row(mods.pop(0))
                    split_next()
                for t in range(nt):
                    act.wait_ge(s_gated.sem, s_gated.at((l, t)))
                    act.activation(h_hi[:, 0:4, P * t:P * t + P],
                                         tmp_m[:, t % 2, :].rearrange("p (c n) -> p c n", c=4), ACT.Copy).then_inc(s_hi.sem, s_hi.nth((l, "m", t)))
                act.wait_ge(s_lo.sem, s_lo.at((l, "m", nt - 1)))
                split_next()
                for t in range(nt):
                    act.wait_ge(s_mm.sem, s_mm.at((l, "out", 0, t)))
                    act.activation(y1[:, t, 0:512], ps[:, t, :], ACT.Copy).then_inc(s_y.sem, s_y.nth((l, 0, t)))
                for s in range(parts):
                    for b in range(2):
                        act.wait_ge(s_gate_mm.sem, s_gate_mm.at((l, s, b)))
                        act.activation(gate_b[:, s, 512 * b:512 * b + 512], ps[:, 6 + b, :], ACT.Copy).then_inc(s_gate_b.sem, s_gate_b.nth((l, s)))
                split_next()
                for st in range(nt + 3):
                    t = st - 1
                    if 0 <= t < nt:
                        root((l, "post", t), t, 1)
                    t = st
                    if t < nt:
                        act.wait_ge(s_mm.sem, s_mm.at((l, "out", 1, t)))
                        act.activation(y1[:, t, 512:1024], ps[:, t, :], ACT.Copy).then_inc(s_y.sem, s_y.nth((l, 1, t)))
                        act.wait_ge(s_y.sem, s_y.at((l, 1, t)))
                        if t > 0:
                            act.wait_ge(s_ssq.sem, s_ssq.at((l, "post", t - 1)))
                        act.activation(junk[:], y1[:, t, :], ACT.Square, accum_out=ssq[:, t:t + 1]).then_inc(s_ssq.sem, s_ssq.nth((l, "post", t)))
                    t = st - 2
                    if both and 0 <= t < NT:
                        act.wait_ge(s_x_final.sem, s_x_final.at((l, t)))
                        squares(l + 1, t)
                    t = st - 3
                    if both and t >= 0:
                        root((l + 1, "pre", t), 8 + t, 1)
                split_next()
                split_next()

            for l in range(DEPTH):
                y = DEPTH + l
                if y == DEPTH:
                    for t in range(XT):
                        hi_rows(s_xt, y, "t", t)
                for t in range(XT):
                    act.wait_ge(s_x_final.sem, s_x_final.at((y - 1, t)))
                for dst, src in ((cos2[HD:QC, :], I["cos2"]), (sin2[HD:QC, :], I["sin2"]),
                                 (dlam[:], I["diff_lambda_2"][l].rearrange("a b -> (a b)").partition_broadcast(P)),
                                 (lam_c[:], I["lam_init"][l].partition_broadcast(P)),
                                 (subln[:], I["subln_g_2"][l].partition_broadcast(P))):
                    act.dma_start(dst, src).then_inc(s_layer_consts.sem, s_layer_consts.nth(y, 16))
                act.wait_ge(s_lam_sums.sem, s_lam_sums.at(y))
                act.activation(lam[:, 2:4], lam[:, 0:2], ACT.Exp).then_inc(s_lam_exp.sem, s_lam_exp.nth(y))
                for j, n in ((0, 256), (1, 160)):
                    for g in range(2):
                        act.wait_ge(s_mm.sem, s_mm.at((y, "c", j, g)))
                        act.activation(c_in[:, 2 * g:2 * g + 2, 256 * j:256 * j + n],
                                             ps[:, (6, 0)[j] + g, 0:2 * n].rearrange("p (t c) -> p t c", t=2), ACT.Copy).then_inc(s_proj.sem, s_proj.nth((y, "c", j, g)))
                    split_next()
                act.wait_ge(s_proj.sem, s_proj.at((y, "c", 1, 1)))
                for t in range(XT):
                    if t > 0:
                        act.wait_ge(s_ssq.sem, s_ssq.at((y, "c", 3 + t)))
                    act.activation(tmp_c[:, 0, 0:256], c_in[:, t, 0:256], ACT.Square, accum_out=ssq[:, t:t + 1]).then_inc(s_ssq.sem, s_ssq.nth((y, "c", t)))
                    act.activation(tmp_c[:, 1, 0:128], c_in[:, t, 256:384], ACT.Square, accum_out=ssq[:, 4 + t:5 + t]).then_inc(s_ssq.sem, s_ssq.nth((y, "c", 4 + t)))
                root((y, "c"), 0, 8)
                for j in range(3):
                    for c in range(2):
                        i = 2 * j + c
                        act.wait_ge(s_mm.sem, s_mm.at((y, "a", i)))
                        dst, scale = (qa[:, i, :], -HD ** -0.5) if i < 3 else (ka[:, i - 3, :], 1.0)
                        act.activation(dst, ps[:, i % 4, :], ACT.Copy, scale=scale).then_inc(s_proj.sem, s_proj.nth((y, "a", i)))
                    split_next()
                for i in range(3):
                    act.wait_ge(s_lat.sem, s_lat.at((y, i)))
                    act.activation(cq_hi[:, i, :] if i < 2 else ckv_hi[:], tmp_c[:, i % 2, :], ACT.Copy).then_inc(s_hi.sem, s_hi.nth((y, "c", i)))
                for g in range(2):
                    act.wait_ge(s_mm.sem, s_mm.at((y, "av", 0, g)))
                    act.activation(va[:, 2 * g:2 * g + 2, 0:256], ps[:, 4 + g, :].rearrange("p (t c) -> p t c", t=2),
                                   ACT.Copy).then_inc(s_proj.sem, s_proj.nth((y, "av", 0, g)))
                split_next()
                act.wait_ge(s_mm.sem, s_mm.at((y, "av", 1)))
                act.activation(va_fm[:], ps[:, 6, :], ACT.Copy).then_inc(s_proj.sem, s_proj.nth((y, "av", 1)))
                split_next()
                for h in range(C_HEADS):
                    act.wait_ge(s_mm.sem, s_mm.at((y, "qc", h)))
                    act.activation(qc[0:QC, h, :], ps[0:QC, h % 2, :], ACT.Copy, scale=-QC ** -0.5).then_inc(s_proj.sem, s_proj.nth((y, "qc", h)))
                    act.wait_ge(s_mm.sem, s_mm.at((y, "kc", h)))
                    act.activation(kc[0:HD, h, :], ps[0:HD, 2 + h % 2, :], ACT.Copy).then_inc(s_proj.sem, s_proj.nth((y, "kc", h)))
                for t in range(XT):
                    act.wait_ge(s_mm.sem, s_mm.at((y, "vc", t)))
                    act.activation(vc[:, t, :], ps[:, 4 + t, 0:384], ACT.Copy).then_inc(s_proj.sem, s_proj.nth((y, "vc", t)))
                split_next()
                act.wait_ge(s_v_turned.sem, s_v_turned.at((y, 0)))
                act.activation(va[:, :, 256:384], ps[:, 0, :].rearrange("p (t c) -> p t c", t=XT), ACT.Copy).then_inc(s_v_out.sem, s_v_out.nth((y, 0)))
                for what, dst, b0, scale in (("bq", qb, 0, -32 ** -0.5), ("bk", kb, 2, 1.0)):
                    for c in range(2):
                        act.wait_ge(s_mm.sem, s_mm.at((y, what, c)))
                        act.activation(dst[:, c, :], ps[:, b0 + c, :], ACT.Copy, scale=scale).then_inc(s_proj.sem, s_proj.nth((y, what, c)))
                    split_next()
                act.wait_ge(s_roped.sem, s_roped.at((y, C_HEADS - 1)))
                act.wait_ge(s_kr_all.sem, s_kr_all.at(y))
                act.wait_ge(s_bias_rows.sem, 16 * (A_HEADS + B_HEADS))
                for h in range(A_HEADS + B_HEADS):
                    act.dma_start(strips[:, h, :], scratch[h, P - 1:P - 1 + P * (SEQ + P - 1)].rearrange(
                        "(p n) -> p n", n=SEQ + P - 1)[:, 0:SEQ]).then_inc(s_strips.sem, s_strips.nth(y, 16))
                act.dma_start(strips[:, A_HEADS + B_HEADS, :], I["causal"]).then_inc(s_strips.sem, s_strips.nth(y, 16))
                for g in range(2):
                    act.wait_ge(s_mm.sem, s_mm.at((y, "bv", 0, g)))
                    act.activation(vb[:, 2 * g:2 * g + 2, :].rearrange("p t c -> p (t c)"), ps[:, 4 + g, :], ACT.Copy).then_inc(s_proj.sem, s_proj.nth((y, "bv", 0, g)))
                units = units2()

                def between(step):
                    if step == 8:
                        split_next(0, TILE // 2)
                    if step == 10:
                        split_next(TILE // 2, TILE)
                    if step == LAST_PAIR + 9:
                        root((y, "sub"), 0, 16)
                    if 0 <= step - LATENT_SPLIT < 3:
                        k = 5 + step - LATENT_SPLIT
                        act.wait_ge(s_o_out.sem, s_o_out.at((y, units[LAST_LATENT]["rank"])))
                        act.activation(g_hi[:, k, :], ao_fm[:, k - 2, :], ACT.Copy).then_inc(s_hi.sem, s_hi.nth((y, "m", k)))

                exp_units(y, units, between)
                act.wait_ge(s_mixed.sem, s_mixed.at((y, units[-1]["rank"])))
                for i, w in enumerate(("ln1_g_2", "ln1_b_2")):
                    act.dma_start(ln1[:, i, :], I[w][l].partition_broadcast(P)).then_inc(s_ln.sem, s_ln.nth((y, 1), 16))
                for k in HEAD_CHUNKS:
                    if 3 <= k < 5:
                        act.wait_ge(s_aot.sem, s_aot.at((y, k - 3)))
                        src = ps[:, k - 3, :]
                    else:
                        act.wait_ge(s_o_out.sem, s_o_out.at((y, units[-1]["rank"])))
                        src = ao_fm[:, k if k < 3 else k - 2, :]
                    act.activation(g_hi[:, k, :], src, ACT.Copy).then_inc(s_hi.sem, s_hi.nth((y, "m", k)))
                split_next()
                split_next()
                for t in range(XT):
                    if t == 2:
                        split_next()
                    root((y, 1, t), t, 1)
                    if t == 2:
                        hi_rows(s_ht, y, "h", 0)
                hi_rows(s_ht, y, "h", 1)
                split_next()
                for t in (2, 3):
                    hi_rows(s_ht, y, "h", t)
                for j in range(FC):
                    act.wait_ge(s_mm.sem, s_mm.at((y, "gate", j)))
                    act.activation(tmp_f[:, j % 2, :], ps[:, 2 * ((j + 2) % 4), :], ACT.Silu).then_inc(s_silu.sem, s_silu.nth((y, j)))
                    act.wait_ge(s_glu.sem, s_glu.at((y, j)))
                    act.activation(hid_hi[:, j, :], tmp_f[:, 2 + j % 2, :], ACT.Copy).then_inc(s_hi.sem, s_hi.nth((y, "f", j)))
                    split_next()
                act.wait_ge(s_lo.sem, s_lo.at((y, "f", FC - 1)))
                act.wait_ge(s_hi.sem, s_hi.at((y, "f", FC - 1)))
                for i, w in enumerate(("ln2_g_2", "ln2_b_2")):
                    act.dma_start(ln2[:, i, :], I[w][l].partition_broadcast(P)).then_inc(s_ln.sem, s_ln.nth((y, 2), 16))
                for j in range(FC // 2 - 2):
                    split_next()
                for t in range(XT):
                    if t == 2 and l + 1 < DEPTH:
                        split_next()
                    root((y, 2, t), t, 1)
                    if t == 2 and l + 1 < DEPTH:
                        hi_rows(s_xt, y + 1, "t", 0)
                if l + 1 < DEPTH:
                    hi_rows(s_xt, y + 1, "t", 1)
                    split_next()
                    for t in (2, 3):
                        hi_rows(s_xt, y + 1, "t", t)

        @block.tensor
        def _(pe):
            emptied = {b: (s_vectors.sem, 16 * len(vectors)) for b in range(8)}

            def begin(what):
                pe.wait_ge(s_tile_lo.sem, s_tile_lo.at(what))
                if what in shared:
                    pe.wait_ge(s_shared_lo.sem, s_shared_lo.at(what))
                i = split_at[what] % SPLIT
                return w_hi[:, i, :], w_lo[:, i, :]

            def left(what):
                s_mm.name_latest(("tile", what))

            def mm3(o, lhs, rhs, first, last):
                pe.matmul(o, lhs[1], rhs[0], start=first, stop=False)
                pe.matmul(o, lhs[0], rhs[1], start=False, stop=False)
                return pe.matmul(o, lhs[0], rhs[0], start=False, stop=last)

            def both_parts(pair, f):
                return f(pair[0]), f(pair[1])

            def staggered(n):
                order = [(t, 0) for t in range(3)]
                for t in range(n):
                    order.append((t, 1))
                    if t + 3 < n:
                        order.append((t + 3, 0))
                return order

            def mod(what):
                i = mod_at[what]
                o = ps[0:4, 7, 0:256]
                w = both_parts(begin(what), lambda r: r.rearrange("p (k c) -> p k c", k=KD))
                if i >= 1:
                    pe.wait_ge(s_mod_row.sem, s_mod_row.at(mods_all[i - 1]))
                for part in range(2):
                    for k in range(KD):
                        m = pe.matmul(o, cond_hl[:, k, :], w[1 - part][:, k, :], start=part == 0 and k == 0, stop=part == 1 and k == KD - 1)
                m.then_inc(s_mm.sem, s_mm.nth(what))
                left(what)

            def mod_fm(what):
                i = mod_at[what]
                l, _, j = what
                pe.wait_ge(s_mod_row.sem, s_mod_row.at(what))
                for c in range(2):
                    o = 256 + 64 * l + 2 * (2 * j + c)
                    m = pe.matmul(ps[:, 7, o:o + 2], mod_row[:, i % 2, P * c:P * c + P], fold[:], start=True, stop=True)
                m.then_inc(s_mod.sem, s_mod.nth(what))

            def attend(y, units, at_step):
                for b in range(7):
                    pe.wait_ge(*emptied[b])
                s_, t_, width, (n_s, n_t, n_o, n_b) = slots(y)
                for step in range(len(units) + n_b):
                    i = step
                    if i < len(units):
                        u = units[i]
                        o0 = width * (i % n_s)
                        if i >= n_s:
                            pe.wait_ge(s_scored.sem, s_scored.at((y, i - n_s)))
                        if u["head"] is not None:
                            pe.wait_ge(s_q_lo.sem, s_q_lo.at((y, u["head"])))
                        for col, products in u["segs"]:
                            for j, (q, k) in enumerate(products):
                                m = pe.matmul(ps_flat[:, o0 + col:o0 + col + k.shape[1]], q, k, start=j == 0, stop=j == len(products) - 1)
                        m.then_inc(s_scores.sem, s_scores.nth((y, i)))
                    i = step - (n_b - 1)
                    if 0 <= i < len(units) and units[i]["rank"] is not None:
                        r = units[i]["rank"]
                        o0 = width * (n_s + r % n_t)
                        if units[i]["pair"] or units[i]["fm"]:
                            pe.wait_ge(s_paired.sem, s_paired.at((y, i)))
                        else:
                            pe.wait_ge(s_probs.sem, s_probs.at((y, i)))
                        if r >= n_t:
                            pe.wait_ge(s_pt.sem, s_pt.at((y, r - n_t)))
                        for j in range(len(units[i]["vs"])):
                            m = pe.transpose(ps_flat[:, o0 + P * j:o0 + P * j + P], s_[:, i % n_b, P * j:P * j + P], ident[:])
                        m.then_inc(s_turned.sem, s_turned.nth((y, r)))
                    i = step - n_b
                    if i >= 0 and units[i]["rank"] is not None:
                        u = units[i]
                        n, r = len(u["vs"]), u["rank"]
                        pe.wait_ge(s_pt.sem, s_pt.at((y, r)))
                        if r >= n_o:
                            pe.wait_ge(s_o_out.sem, s_o_out.at((y, r - n_o)))
                        o0 = width * (n_s + n_t) + 512 * (r % n_o)
                        for j, v in enumerate(u["vs"]):
                            turned = t_[:, r % 2, P * j:P * j + P]
                            if u["fm"]:
                                m = pe.matmul(ps_flat[0:HD, o0:o0 + P], v, turned, start=j == 0, stop=j == n - 1)
                            else:
                                m = pe.matmul(ps_flat[:, o0:o0 + HD], turned, v, start=j == 0, stop=j == n - 1)
                        m.then_inc(s_mixed.sem, s_mixed.nth((y, r)))
                    at_step(step)
                for b in range(7):
                    if 512 * b < width * n_s:
                        emptied[b] = s_scored.after((y, len(units) - 1))
                    elif 512 * b < width * (n_s + n_t):
                        emptied[b] = s_pt.after((y, units[-1]["rank"]))
                    else:
                        emptied[b] = s_o_out.after((y, units[-1]["rank"]))

            pe.wait_ge(s_vectors.sem, 16 * len(vectors))
            emptied[7] = s_vec_t.after(0)
            pe.transpose(ps[:, 7, 0:NV], vec[0:NV, :], ident[0:NV, 0:NV]).then_inc(s_vec_mm.sem, s_vec_mm.nth(0))
            pe.wait_ge(s_cond_hi.sem, s_cond_hi.at(0))
            pe.wait_ge(s_cond_lo.sem, s_cond_lo.at(0))
            pe.wait_ge(*emptied[7])
            emptied[7] = s_mod_out.after((0, 0))
            for j in range(8):
                if j > 0:
                    mod_fm((0, "mod", j - 1))
                mod((0, "mod", j))
            mod_fm((0, "mod", 7))

            for l in range(DEPTH):
                both = l < DEPTH - 1
                nt, nc_ = (NT, TOK) if both else (XT, SEQ)
                parts = 2 if both else 1
                if l == 0:
                    pe.wait_ge(s_wf_landed.sem, 16 * (2 * DEPTH + 2))
                pe.wait_ge(*emptied[6])
                emptied[6] = s_wf_m.after(l)
                for i, m_ in enumerate((dft_ccos, dft_csin)):
                    m = pe.matmul(ps[:, 6, 256 * i:256 * i + 256], m_[:], wf[:, l, :, :], start=True, stop=True)
                m.then_inc(s_wf_mm.sem, s_wf_mm.nth(l))
                for k in range(KD):
                    pe.wait_ge(*emptied[k % 4])
                    emptied[k % 4] = s_mod_x.after((l, k))
                    pe.wait_ge(*emptied[4 + k % 2])
                    emptied[4 + k % 2] = s_mod_c.after((l, k))
                    for t in range(NT):
                        if k == 0:
                            pe.wait_ge(s_xn.sem, s_xn.at((l, t)))
                        o = ps[:, k % 4, P * t:P * t + P] if t < XT else ps[:, 4 + k % 2, P * (t - XT):P * (t - XT) + P]
                        m = pe.transpose(o, xn[:, t, P * k:P * k + P], ident[:])
                    m.then_inc(s_nt.sem, s_nt.nth((l, k)))
                if l == 0:
                    pe.wait_ge(s_consts.sem, 16 * len(consts))
                n_fm = 0
                H = (h_hi, h_lo)
                lo_seen = set()

                def rows_ready(k, part):
                    if (k, part) in lo_seen:
                        return
                    lo_seen.add((k, part))
                    if part == 0:
                        pe.wait_ge(s_lo.sem, s_lo.at((l, "n", k)))
                    else:
                        pe.wait_ge(s_lo_c.sem, s_lo_c.at((l, k)))

                def fm(what, c, w, until, n_parts=parts):
                    nonlocal n_fm
                    w = both_parts(w, lambda r: r.rearrange("p (k c) -> p k c", k=KD))
                    for part in range(n_parts):
                        b, n, a = (n_fm % 4, SEQ, 0) if part == 0 else (4 + n_fm % 2, CTX, SEQ)
                        pe.wait_ge(*emptied[b])
                        emptied[b] = until.after((l, what, c, part))
                        for k in range(KD):
                            rows_ready(k, part)
                            m = mm3(ps[:, b, 0:n], both_parts(w, lambda r: r[:, k, P * c:P * c + P]),
                                    both_parts(H, lambda r: r[:, k, a:a + n]), k == 0, k == KD - 1)
                        m.then_inc(s_mm.sem, s_mm.nth((l, what, c, part)))
                    n_fm += 1

                def tm(o, t, w, c0, n):
                    w = both_parts(w, lambda r: r.rearrange("p (k c) -> p k c", k=KD))
                    for k in range(KD):
                        m = mm3(o, both_parts(H, lambda r: r[:, k, P * t:P * t + P]),
                                both_parts(w, lambda r: r[:, k, c0:c0 + n]), k == 0, k == KD - 1)
                    return m

                for j in range(2):
                    w = begin((l, "q", j))
                    for c in range(2):
                        fm(("q", j), c, w, s_proj)
                    left((l, "q", j))
                if l == 0:
                    for b in (6, 7):
                        pe.wait_ge(*emptied[b])
                        emptied[b] = s_rr.after(0)
                    pe.matmul(ps[0:A_HEADS + B_HEADS, 6, :], table[:], hot[:, 0:SEQ], start=True, stop=True)
                    pe.matmul(ps[0:A_HEADS + B_HEADS, 7, 0:P], table[:], hot[:, SEQ:SEQ + P], start=True, stop=True).then_inc(s_rr_mm.sem, s_rr_mm.nth(0))
                w = begin((l, "kv"))
                fm(("kv",), 0, w, s_proj, 2)
                fm(("kv",), 1, w, s_proj, 2)
                left((l, "kv"))
                w = begin((l, "uf"))
                for g in range(nt // 2):
                    b = (6, 7, 5)[g]
                    pe.wait_ge(*emptied[b])
                    emptied[b] = s_uf_lo.after((l, g))
                    for t in range(2):
                        m = tm(ps[:, b, 256 * t:256 * t + 256], 2 * g + t, w, 0, 256)
                    m.then_inc(s_mm.sem, s_mm.nth((l, ("uf",), g, 0)))
                left((l, "uf"))
                for part, t0, n in ((0, 0, XT), (1, XT, CT)):
                    pe.wait_ge(s_proj.sem, s_proj.at((l, ("kv",), 1, part)))
                    pe.wait_ge(*emptied[6 + part])
                    emptied[6 + part] = s_v_out.after((l, part))
                    for t in range(n):
                        m = pe.transpose(ps[:, 6 + part, P * t:P * t + P], cb[:, 0, P * (t0 + t):P * (t0 + t) + P], ident[:])
                    m.then_inc(s_v_turned.sem, s_v_turned.nth((l, part)))
                n_rot = 0
                for what in ("gf", "zc", "bc", "cc", "gc"):
                    w = begin((l, what))
                    for c in range(2):
                        if n_rot < 5:
                            i, b = n_rot, 6 + n_rot % 2
                            pe.wait_ge(*emptied[b])
                            emptied[b] = s_roped.after((l, i))
                            pe.wait_ge(s_proj.sem, s_proj.at((l, ("q", i // 2), i % 2, 0) if i < 4 else (l, ("kv",), 0, 0)))
                            src = q1[:, i, 0:SEQ] if i < 4 else k1[:, 0:SEQ]
                            pe.matmul(ps[:, b, :], rot1[:], src, start=True, stop=True).then_inc(s_rot.sem, s_rot.nth((l, i)))
                            n_rot += 1
                        fm((what,), c, w, s_conv_t if what == "cc" else s_proj)
                    left((l, what))
                for j in range(2):
                    w = begin((l, "ga", j))
                    for c in range(2):
                        fm(("ga", j), c, w, s_proj)
                    left((l, "ga", j))
                U = (uf_hi, uf_lo)
                pe.wait_ge(s_uf_lo.sem, s_uf_lo.at((l, nt // 2 - 1)))
                for i, part in enumerate(("cos", "sin")):
                    w = both_parts(begin((l, "dft", part)), lambda r: r.rearrange("p (k c) -> p k c", k=XT))
                    for c in range(2):
                        pe.wait_ge(*emptied[2 * i + c])
                        emptied[2 * i + c] = s_four_out.after((l, i, c))
                        for k in range(XT):
                            m = mm3(ps[:, 2 * i + c, :], both_parts(U, lambda r: r[:, k, P * c:P * c + P]),
                                    both_parts(w, lambda r: r[:, k, :]), k == 0, k == XT - 1)
                        m.then_inc(s_mm.sem, s_mm.nth((l, "four", i, c)))
                    left((l, "dft", part))
                if both:
                    w = both_parts(begin((l, "dft", "ctx")), lambda r: r[:, 0:1024].rearrange("p (i k c) -> p i k c", i=2, k=CT))
                    for i in range(2):
                        pe.wait_ge(*emptied[4 + i])
                        emptied[4 + i] = s_four_out.after((l, i, "ctx"))
                        for c in range(2):
                            for k in range(CT):
                                m = mm3(ps[:, 4 + i, CTX * c:CTX * c + CTX], both_parts(U, lambda r: r[:, XT + k, P * c:P * c + P]),
                                        both_parts(w, lambda r: r[:, i, k, :]), k == 0, k == CT - 1)
                        m.then_inc(s_mm.sem, s_mm.nth((l, "four", i, "ctx")))
                    left((l, "dft", "ctx"))
                pe.wait_ge(s_wf_m.sem, s_wf_m.at(l))
                for c in range(2):
                    for part in range(parts):
                        b, n, a = (6 + c, SEQ, 0) if part == 0 else (4 + c, CTX, SEQ)
                        pe.wait_ge(s_four_out.sem, s_four_out.at((l, 1, c if part == 0 else "ctx")))
                        pe.wait_ge(*emptied[b])
                        emptied[b] = s_side.after((l, c))
                        for i in range(2):
                            m = pe.matmul(ps[:, b, 0:n], wf_m[:, i, c, :], four[:, i, c, a:a + n], start=i == 0, stop=i == 1)
                        m.then_inc(s_fmix.sem, s_fmix.nth((l, c, part)))
                pe.wait_ge(s_k_lo.sem, s_k_lo.at((l, KVH - 1)))
                pe.wait_ge(s_v_out.sem, s_v_out.at((l, 1)))
                units = units1(l)
                mods = [(m, "mod", j) for m, j in mods_in_attention[l]]
                before = []

                def between(step):
                    if step % MOD_STEP[l] == 2 and mods:
                        what = mods.pop(0)
                        if before:
                            mod_fm(before.pop())
                        mod(what)
                        before.append(what)

                pe.wait_ge(*emptied[7])
                attend(l, units, between)
                while mods:
                    what = mods.pop(0)
                    mod_fm(before.pop())
                    mod(what)
                    before.append(what)
                mod_fm(before.pop())
                emptied[7] = s_mod_out.after((l, 1))
                pe.wait_ge(s_lo.sem, s_lo.at((l, "s", 3)))
                for kh in (1, 0):
                    w = both_parts(begin((l, "out", 0, kh)), lambda r: r.rearrange("p (k c) -> p k c", k=4))
                    for t in range(nt):
                        if kh == 1:
                            pe.wait_ge(*emptied[t])
                            emptied[t] = s_y.after((l, 0, t))
                        else:
                            pe.wait_ge(s_lo.sem, s_lo.at((l, "m", t)))
                        for k in range(4):
                            m = mm3(ps[:, t, :], both_parts(H, lambda r: r[:, 4 * kh + k, P * t:P * t + P]),
                                    both_parts(w, lambda r: r[:, k, :]), kh == 1 and k == 0, kh == 0 and k == 3)
                        m.then_inc(s_mm.sem, s_mm.nth((l, "out half", 0, t) if kh else (l, "out", 0, t)))
                        if kh == 1:
                            pe.wait_ge(*emptied[6])
                            emptied[6] = s_gated.after((l, t))
                            for c in range(4):
                                m = pe.transpose(ps[:, 6, P * c:P * c + P], ao1[:, t, P * c:P * c + P], ident[:])
                            m.then_inc(s_aot.sem, s_aot.nth((l, t)))
                    left((l, "out", 0, kh))
                pe.wait_ge(s_ones.sem, s_ones.at(0))
                for s in range(parts):
                    pe.wait_ge(s_diag.sem, s_diag.at((l, s)))
                    for b in range(2):
                        pe.wait_ge(*emptied[6 + b])
                        emptied[6 + b] = s_gate_b.after((l, s))
                        pe.matmul(ps[:, 6 + b, :], ones[:], diag[:, s, 4 * b:4 * b + 4, :], start=True, stop=True).then_inc(s_gate_mm.sem, s_gate_mm.nth((l, s, b)))
                ws = []
                for t, kh in staggered(nt):
                    if len(ws) == kh:
                        ws.append(both_parts(begin((l, "out", 1, kh)), lambda r: r.rearrange("p (k c) -> p k c", k=4)))
                    if kh == 0:
                        pe.wait_ge(*emptied[t])
                        emptied[t] = s_y.after((l, 1, t))
                    for k in range(4):
                        m = mm3(ps[:, t, :], both_parts(H, lambda r: r[:, 4 * kh + k, P * t:P * t + P]),
                                both_parts(ws[kh], lambda r: r[:, k, :]), kh == 0 and k == 0, kh == 1 and k == 3)
                    m.then_inc(s_mm.sem, s_mm.nth((l, "out", 1, t) if kh else (l, "out half", 1, t)))
                    if t == nt - 1:
                        left((l, "out", 1, kh))

            G = (g_hi, g_lo)

            def turn_rows(turned, ready, before, y, what, t):
                pe.wait_ge(ready.sem, ready.at((before, t)))
                for g in range(2):
                    b = 2 * (t % 2) + g
                    pe.wait_ge(*emptied[b])
                    emptied[b] = s_lo.after((y, what, t, g))
                    for c in range(4):
                        m = pe.transpose(ps[:, b, P * c:P * c + P], res[:, t, P * (4 * g + c):P * (4 * g + c) + P], ident[:])
                    m.then_inc(turned.sem, turned.nth((y, t, g)))

            for l in range(DEPTH):
                y = DEPTH + l

                if y == DEPTH:
                    for t in range(2):
                        turn_rows(s_xt, s_x_final, y - 1, y, "t", t)
                turn_rows(s_xt, s_x_final, y - 1, y, "t", 2)

                def fm(b, w, c, until, key):
                    pe.wait_ge(*emptied[b])
                    emptied[b] = until
                    w = both_parts(w, lambda r: r.rearrange("p (k c) -> p k c", k=KD))
                    for k in range(KD):
                        m = mm3(ps[:, b, :], both_parts(w, lambda r: r[:, k, P * c:P * c + P]),
                                both_parts(G, lambda r: r[:, k, :]), k == 0, k == KD - 1)
                    m.then_inc(s_mm.sem, s_mm.nth(key))

                def tm(b0, w, n, what):
                    w = both_parts(w, lambda r: r[:, 0:KD * n].rearrange("p (k c) -> p k c", k=KD))
                    for g in range(2):
                        pe.wait_ge(*emptied[b0 + g])
                        emptied[b0 + g] = s_proj.after((y, *what, g))
                        for t in range(2):
                            if what == ("c", 0):
                                pe.wait_ge(s_lo.sem, s_lo.at((y, "t", 2 * g + t, 1)))
                            for k in range(KD):
                                m = mm3(ps[:, b0 + g, n * t:n * t + n],
                                        both_parts(G, lambda r: r[:, k, P * (2 * g + t):P * (2 * g + t) + P]),
                                        both_parts(w, lambda r: r[:, k, :]), k == 0, k == KD - 1)
                        m.then_inc(s_mm.sem, s_mm.nth((y, *what, g)))
                        if what == ("c", 0) and g == 0:
                            turn_rows(s_xt, s_x_final, y - 1, y, "t", 3)

                for j, n in ((0, 256), (1, 160)):
                    tm((6, 0)[j], begin((y, "c", j)), n, ("c", j))
                    left((y, "c", j))
                for j in range(3):
                    w = begin((y, "a", j))
                    for c in range(2):
                        i = 2 * j + c
                        fm(i % 4, w, c, s_proj.after((y, "a", i)), (y, "a", i))
                    left((y, "a", j))
                for i in range(4):
                    pe.wait_ge(*emptied[i])
                    emptied[i] = s_lo.after((y, "c", i)) if i < 3 else s_kr_raw.after(y)
                    for t in range(XT):
                        if i == 0:
                            pe.wait_ge(s_latn.sem, s_latn.at((y, t)))
                        if i < 3:
                            m = pe.transpose(ps[:, i, P * t:P * t + P], c_in[:, t, P * i:P * i + P], ident[:])
                        else:
                            m = pe.transpose(ps[0:QC, 3, P * t:P * t + P], c_in[:, t, 416 - QC:416], ident[:])
                    m.then_inc(s_lat_t.sem, s_lat_t.nth((y, i)))
                tm(4, begin((y, "av", 0)), 256, ("av", 0))
                left((y, "av", 0))
                w = begin((y, "av", 1))
                fm(6, (w[0][:, 0:KD * P], w[1][:, 0:KD * P]), 0, s_proj.after((y, "av", 1)), (y, "av", 1))
                left((y, "av", 1))
                w = begin((y, "up"))
                uq = both_parts(w, lambda r: r[:, 0:2 * C_HEADS * QC].rearrange("p (k c) -> p k c", k=2))
                ukv = both_parts(w, lambda r: r[:, 2 * C_HEADS * QC:2 * C_HEADS * QC + 2 * C_HEADS * HD])

                def q_rot(h):
                    pe.wait_ge(*emptied[6 + h % 2])
                    emptied[6 + h % 2] = s_roped.after((y, h))
                    pe.wait_ge(s_proj.sem, s_proj.at((y, "qc", h)))
                    pe.matmul(ps[0:QC, 6 + h % 2, :], rot2[HD:QC, :], qc[HD:QC, h, :], start=True, stop=True).then_inc(s_q_rot.sem, s_q_rot.nth((y, h)))

                pe.wait_ge(s_lo.sem, s_lo.at((y, "c", 2)))
                for h in range(C_HEADS):
                    pe.wait_ge(*emptied[h % 2])
                    emptied[h % 2] = s_proj.after((y, "qc", h))
                    for k in range(2):
                        m = mm3(ps[0:QC, h % 2, :], both_parts(uq, lambda r: r[:, k, QC * h:QC * h + QC]),
                                both_parts((cq_hi, cq_lo), lambda r: r[:, k, :]), k == 0, k == 1)
                    m.then_inc(s_mm.sem, s_mm.nth((y, "qc", h)))
                    pe.wait_ge(*emptied[2 + h % 2])
                    emptied[2 + h % 2] = s_proj.after((y, "kc", h))
                    m = mm3(ps[:, 2 + h % 2, :], both_parts(ukv, lambda r: r[:, P * h:P * h + P]),
                            both_parts((ckv_hi, ckv_lo), lambda r: r[:]), True, True)
                    m.then_inc(s_mm.sem, s_mm.nth((y, "kc", h)))
                    if h == 0:
                        pe.wait_ge(*emptied[5])
                        emptied[5] = s_kr_all.after(y)
                        pe.wait_ge(s_kr_raw.sem, s_kr_raw.at(y))
                        pe.matmul(ps[0:QC, 5, :], rot2[HD:QC, :], kc[HD:QC, 0, :], start=True, stop=True).then_inc(s_kr_rot.sem, s_kr_rot.nth(y))
                    else:
                        q_rot(h - 1)
                q_rot(C_HEADS - 1)
                for t in range(XT):
                    pe.wait_ge(*emptied[4 + t])
                    emptied[4 + t] = s_proj.after((y, "vc", t))
                    m = mm3(ps[:, 4 + t, 0:C_HEADS * HD], both_parts((ckv_hi, ckv_lo), lambda r: r[:, P * t:P * t + P]),
                            both_parts(ukv, lambda r: r.rearrange("p (h c) -> p h c", h=C_HEADS)[:, :, HD:2 * HD]), True, True)
                    m.then_inc(s_mm.sem, s_mm.nth((y, "vc", t)))
                left((y, "up"))
                pe.wait_ge(s_proj.sem, s_proj.at((y, "av", 1)))
                pe.wait_ge(*emptied[0])
                emptied[0] = s_v_out.after((y, 0))
                for t in range(XT):
                    m = pe.transpose(ps[:, 0, P * t:P * t + P], va_fm[:, P * t:P * t + P], ident[:])
                m.then_inc(s_v_turned.sem, s_v_turned.nth((y, 0)))
                for what, b0 in (("bq", 0), ("bk", 2)):
                    w = begin((y, what, 0))
                    for c in range(2):
                        fm(b0 + c, w, c, s_proj.after((y, what, c)), (y, what, c))
                    left((y, what, 0))
                tm(4, begin((y, "bv", 0)), 256, ("bv", 0))
                left((y, "bv", 0))
                pe.wait_ge(s_roped.sem, s_roped.at((y, C_HEADS - 1)))
                pe.wait_ge(s_kr_all.sem, s_kr_all.at(y))
                units = units2()
                attend(y, units, lambda step: None)
                for kh in (1, 0):
                    w = both_parts(begin((y, "o", 0, kh)), lambda r: r.rearrange("p (k c) -> p k c", k=4))
                    for ks in ((1, 2, 3), (0,)) if kh == 1 else ((0, 1, 2, 3),):
                        if ks == (0,):
                            pe.wait_ge(s_sub.sem, s_sub.at(y))
                            for c in range(2):
                                pe.wait_ge(*emptied[c])
                                emptied[c] = s_lo.after((y, "m", 3 + c))
                                for t in range(XT):
                                    m = pe.transpose(ps[:, c, P * t:P * t + P], ao_b[:, t, P * c:P * c + P], ident[:])
                                m.then_inc(s_aot.sem, s_aot.nth((y, c)))
                        for t in range(XT):
                            if kh == 1 and ks[0] == 1:
                                pe.wait_ge(*emptied[4 + t])
                                emptied[4 + t] = s_resid.after((y, 1, 0, t))
                            for k in ks:
                                if t == 0:
                                    pe.wait_ge(s_lo.sem, s_lo.at((y, "m", 4 * kh + k)))
                                m = mm3(ps[:, 4 + t, :], both_parts(G, lambda r: r[:, 4 * kh + k, P * t:P * t + P]),
                                        both_parts(w, lambda r: r[:, k, :]), kh == 1 and k == 1, kh == 0 and k == 3)
                            m.then_inc(s_mm.sem, s_mm.nth((y, "o part", kh, ks[0], t) if kh else (y, "o", 0, t)))
                    left((y, "o", 0, kh))
                ws = []
                for t, kh in staggered(XT):
                    if len(ws) == kh:
                        ws.append(both_parts(begin((y, "o", 1, kh)), lambda r: r.rearrange("p (k c) -> p k c", k=4)))
                    if kh == 0:
                        pe.wait_ge(*emptied[4 + t])
                        emptied[4 + t] = s_resid.after((y, 1, 1, t))
                    for k in range(4):
                        m = mm3(ps[:, 4 + t, :], both_parts(G, lambda r: r[:, 4 * kh + k, P * t:P * t + P]),
                                both_parts(ws[kh], lambda r: r[:, k, :]), kh == 0 and k == 0, kh == 1 and k == 3)
                    m.then_inc(s_mm.sem, s_mm.nth((y, "o", 1, t) if kh else (y, "o half", 1, t)))
                    if t == XT - 1:
                        left((y, "o", 1, kh))
                    if kh == 1 and t >= 2:
                        turn_rows(s_ht, s_normed, y, y, "h", t - 2)
                def half_rows(j, half):
                    w = both_parts(begin((y, "ff", j)), lambda r: r.rearrange("p (k c) -> p k c", k=KD))
                    b = 2 * ((j + 2) % 4)
                    if half == 0:
                        pe.wait_ge(*emptied[b])
                        pe.wait_ge(*emptied[b + 1])
                        emptied[b], emptied[b + 1] = s_silu.after((y, j)), s_glu.after((y, j))
                    pe.wait_ge(s_lo.sem, s_lo.at((y, "h", 2 * half + 1, 1)))
                    for c, key in enumerate(("gate", "ffup")):
                        for k in range(KD):
                            m = mm3(ps[:, b + c, 256 * half:256 * half + 256], both_parts(w, lambda r: r[:, k, P * c:P * c + P]),
                                    both_parts(G, lambda r: r[:, k, 256 * half:256 * half + 256]), k == 0, k == KD - 1)
                        m.then_inc(s_mm.sem, s_mm.nth((y, key, j) if half else (y, key + " half", j)))
                    if half == 1:
                        left((y, "ff", j))

                turn_rows(s_ht, s_normed, y, y, "h", 2)
                half_rows(0, 0)
                turn_rows(s_ht, s_normed, y, y, "h", 3)
                half_rows(1, 0)
                half_rows(0, 1)
                half_rows(1, 1)
                for j in range(2, FC):
                    w = begin((y, "ff", j))
                    b = 2 * ((j + 2) % 4)
                    fm(b, w, 0, s_silu.after((y, j)), (y, "gate", j))
                    fm(b + 1, w, 1, s_glu.after((y, j)), (y, "ffup", j))
                    left((y, "ff", j))
                def down(w, j, t, ch):
                    for k in range(2):
                        m = mm3(ps[:, 2 * t + ch, :], both_parts((hid_hi, hid_lo), lambda r: r[:, 2 * j + k, P * t:P * t + P]),
                                both_parts(w, lambda r: r[:, k, 512 * ch:512 * ch + 512]),
                                j == 0 and k == 0, j == FC // 2 - 1 and k == 1)
                    return m

                for j in range(FC // 2 - 2):
                    w = both_parts(begin((y, "down", j)), lambda r: r.rearrange("p (k c) -> p k c", k=2))
                    pe.wait_ge(s_lo.sem, s_lo.at((y, "f", 2 * j + 1)))
                    for t in range(XT):
                        for ch in range(2):
                            if j == 0:
                                pe.wait_ge(*emptied[2 * t + ch])
                                emptied[2 * t + ch] = s_resid.after((y, 2, ch, t))
                            down(w, j, t, ch).then_inc(s_mm.sem, s_mm.nth((y, "down", j, ch, t)))
                    left((y, "down", j))
                last = (FC // 2 - 2, FC // 2 - 1)
                ws = []
                for t, i in staggered(XT):
                    j = last[i]
                    if len(ws) == i:
                        ws.append(both_parts(begin((y, "down", j)), lambda r: r.rearrange("p (k c) -> p k c", k=2)))
                        pe.wait_ge(s_lo.sem, s_lo.at((y, "f", 2 * j + 1)))
                    for ch in range(2):
                        down(ws[i], j, t, ch).then_inc(s_mm.sem, s_mm.nth((y, "down", j, ch, t)))
                    if t == XT - 1:
                        left((y, "down", j))
                    if i == 1 and t >= 2 and l + 1 < DEPTH:
                        turn_rows(s_xt, s_x_final, y, y + 1, "t", t - 2)

        @block.vector
        def _(dve):
            V = nc.vector

            def step(ins):
                ins.then_inc(s_dve_step.sem, s_dve_step.nth("latest"))
                dve.wait_ge(s_dve_step.sem, s_dve_step.count)

            def inverse(key, a, n):
                dve.wait_ge(s_root.sem, s_root.at(key))
                step(V.reciprocal(rstd[:, a:a + n], rstd[:, a:a + n]))

            def lo_part(dst, src, hi, key, wait_key):
                dve.wait_ge(s_hi.sem, s_hi.at(wait_key))
                V.tensor_tensor(dst, src, hi.bitcast(F32), ALU.subtract).then_inc(s_lo.sem, s_lo.nth(key))

            def attend(y, units, second):
                s_, t_, width, (n_s, n_t, n_o, n_b) = slots(y)
                late = n_b - 1 + n_o

                def divide(st):
                    i = st - 2
                    if 0 <= i < len(units) and units[i]["rank"] is not None:
                        total, r = small[:, 1, i % 8:i % 8 + 1], small[:, 2, i % 8:i % 8 + 1]
                        dve.wait_ge(s_probs.sem, s_probs.at((y, i)))
                        if units[i]["fm"]:
                            n = P * len(units[i]["vs"])
                            step(V.reciprocal(r, total))
                            V.tensor_scalar(s_[:, i % n_b, 0:n], s_[:, i % n_b, 0:n], r, None, ALU.mult).then_inc(s_paired.sem, s_paired.nth((y, i)))
                        if units[i]["pair"]:
                            n = P * len(units[i]["vs"])
                            first, ratio = small[:, 1, (i - 1) % 8:(i - 1) % 8 + 1], small[:, 2, (i - 1) % 8:(i - 1) % 8 + 1]
                            step(V.reciprocal(ratio, total))
                            step(V.tensor_scalar(ratio, ratio, first, lam[:, 4:5], ALU.mult, ALU.mult))
                            V.scalar_tensor_tensor(s_[:, i % n_b, 0:n], s_[:, i % n_b, 0:n], ratio, s_[:, (i - 1) % n_b, 0:n],
                                                   ALU.mult, ALU.add).then_inc(s_paired.sem, s_paired.nth((y, i)))
                            total = first
                        if not units[i]["fm"]:
                            V.reciprocal(r, total).then_inc(s_recip.sem, s_recip.nth((y, i)))

                def rows_out(st):
                    i = st - late
                    if i >= 0 and units[i]["rank"] is not None:
                        u = units[i]
                        o0 = width * (n_s + n_t) + 512 * (u["rank"] % n_o)
                        dve.wait_ge(s_mixed.sem, s_mixed.at((y, u["rank"])))
                        if u["fm"]:
                            V.tensor_copy(u["out"], ps_flat[0:HD, o0:o0 + P]).then_inc(s_o_out.sem, s_o_out.nth((y, u["rank"])))
                        else:
                            dve.wait_ge(s_recip.sem, s_recip.at((y, i)))
                            V.tensor_scalar(u["out"], ps_flat[:, o0:o0 + HD], small[:, 2, i % 8:i % 8 + 1], None,
                                            ALU.mult).then_inc(s_o_out.sem, s_o_out.nth((y, u["rank"])))

                for st in range(len(units) + late):
                    i = st
                    if i < len(units):
                        u = units[i]
                        n = P * len(u["vs"])
                        o0 = width * (i % n_s)
                        if i >= n_b and units[i - n_b]["rank"] is None:
                            dve.wait_ge(s_paired.sem, s_paired.at((y, i - n_b + 1)))
                        elif i >= n_b:
                            dve.wait_ge(s_turned.sem, s_turned.at((y, units[i - n_b]["rank"])))
                        if u["sink"] is not None:
                            V.tensor_copy(s_[:, i % n_b, n:n + 1], u["sink"]).then_inc(s_scored.sem, s_scored.nth((y, i, "sink")))
                        dve.wait_ge(s_scores.sem, s_scores.at((y, i)))
                        V.tensor_tensor_reduce(s_[:, i % n_b, 0:n], ps_flat[:, o0:o0 + n], u["mask"], 1.0,
                                               3.0e38 if u["sink"] is None else u["sink"], ALU.add, ALU.min,
                                               small[:, 0, i % 8:i % 8 + 1]).then_inc(s_scored.sem, s_scored.nth((y, i)))
                    if n_o > 1:
                        rows_out(st)
                    divide(st)
                    if n_o == 1:
                        rows_out(st)
                    second(st)

            dve.wait_ge(s_vec_mm.sem, s_vec_mm.at(0))
            V.tensor_copy(vec_t[:, 0:NV], ps[:, 7, 0:NV]).then_inc(s_vec_t.sem, s_vec_t.nth(0))
            dve.wait_ge(s_vec_t.sem, s_vec_t.at(0))
            dve.wait_ge(s_cond_hi.sem, s_cond_hi.at(0))
            V.tensor_tensor(cond_hl[:, :, 2:4], cond[:], cond_hl[:, :, 0:2].bitcast(F32), ALU.subtract).then_inc(s_cond_lo.sem, s_cond_lo.nth(0))

            def mods_out(l, a, b, key):
                dve.wait_ge(s_mod.sem, s_mod.at((l, "mod", b // 2 - 1)))
                for s in range(2):
                    p_ = ps[:, 7, 256 + 64 * l + 2 * a:256 + 64 * l + 2 * b].rearrange("p (c s) -> p s c", s=2)[:, s, :]
                    m = V.tensor_tensor(mod[:, s, a:b], p_, vec_t[:, VB[l]["b_mod"] + a:VB[l]["b_mod"] + b], ALU.add)
                    if s == 0:
                        step(m)
                m.then_inc(s_mod_out.sem, s_mod_out.nth(key))
                dve.wait_ge(s_mod_out.sem, s_mod_out.at(key))

            def scale_and_shift(l):
                g = vec_t[:, VB[l]["g_pre"]:VB[l]["g_pre"] + KD]
                for s in range(2):
                    step(V.scalar_tensor_tensor(mod_a[:, s, :], mod[:, s, KD:2 * KD], 1.0, g, ALU.add, ALU.mult))

            def pre_var(l, t):
                dve.wait_ge(s_ssq.sem, s_ssq.at((l, "pre", t)))
                V.tensor_scalar(ssq[:, 8 + t:9 + t], ssq[:, 8 + t:9 + t], 1.0 / D, EPS, ALU.mult, ALU.add).then_inc(s_var.sem, s_var.nth((l, "pre", t)))

            def pre_norm(l, t):
                inverse((l, "pre", t), 8 + t, 1)
                src = res[:, t, :] if t < XT else res_c[:, t - XT, :]
                V.tensor_scalar(xn[:, t, :], src, rstd[:, 8 + t:9 + t], None, ALU.mult).then_inc(s_xn.sem, s_xn.nth((l, t)))

            def lo_rows(y, what, t):
                for g in range(2):
                    lo_part(g_lo[:, 4 * g:4 * g + 4, P * t:P * t + P], ps[:, 2 * (t % 2) + g, :].rearrange("p (c n) -> p c n", c=4),
                            g_hi[:, 4 * g:4 * g + 4, P * t:P * t + P], (y, what, t, g), (y, what, t, g))

            for i, what in enumerate(shared):
                dve.wait_ge(s_tile_hi.sem, s_tile_hi.at(what))
                V.tensor_tensor(w_lo[:, i % SPLIT, POOL_COLS:], raw_of(what)[:, POOL_COLS:], w_hi[:, i % SPLIT, POOL_COLS:].bitcast(F32),
                                ALU.subtract).then_inc(s_shared_lo.sem, s_shared_lo.nth(what))
                for t in {5: (0, 1), 6: (2, 3, 4, 5)}.get(i, ()):
                    pre_var(0, t)
            for t in range(NT):
                pre_norm(0, t)
            mods_out(0, 0, 16, (0, 0))
            scale_and_shift(0)
            for l in range(DEPTH):
                both = l < DEPTH - 1
                nt, nc_ = (NT, TOK) if both else (XT, SEQ)
                parts = 2 if both else 1
                dve.wait_ge(s_wf_mm.sem, s_wf_mm.at(l))
                V.tensor_copy(wf_m[:].rearrange("p i c n -> p (i c n)"), ps[:, 6, :]).then_inc(s_wf_m.sem, s_wf_m.nth(l))
                for st in range(KD + 2):
                    k = st
                    if k < KD:
                        dve.wait_ge(s_nt.sem, s_nt.at((l, k)))
                        if k >= 3:
                            dve.wait_ge(s_lo.sem, s_lo.at((l, "n", k - 3)))
                        V.tensor_scalar(tmp_n[:, k % 3, :], ps[:, k % 4, :], mod_a[:, 0, k:k + 1], mod[:, 0, k:k + 1],
                                        ALU.mult, ALU.add).then_inc(s_mod_x.sem, s_mod_x.nth((l, k)))
                    k = st - 2
                    if k >= 0:
                        dve.wait_ge(s_mod_x.sem, s_mod_x.at((l, k)))
                        lo_part(h_lo[:, k, 0:SEQ], tmp_n[:, k % 3, :], h_hi[:, k, 0:SEQ], (l, "n", k), (l, "n", k))
                if l == 0:
                    dve.wait_ge(s_consts.sem, 16 * len(consts))
                    dve.wait_ge(s_rr_mm.sem, s_rr_mm.at(0))
                    V.tensor_scalar(rr[:], ps_flat[0:A_HEADS + B_HEADS, 6 * 512:6 * 512 + SEQ + P], -1.0, None, ALU.mult).then_inc(s_rr.sem, s_rr.nth(0))
                    step(V.tensor_scalar(sinks[:], sinks[:], -1.0, None, ALU.mult))
                for g in range(nt // 2):
                    dve.wait_ge(s_uf_hi.sem, s_uf_hi.at((l, g)))
                    V.tensor_tensor(uf_lo[:, 2 * g:2 * g + 2, :].rearrange("p t c -> p (t c)"), ps[:, (6, 7, 5)[g], :],
                                          uf_hi[:, 2 * g:2 * g + 2, :].rearrange("p t c -> p (t c)").bitcast(F32), ALU.subtract).then_inc(s_uf_lo.sem, s_uf_lo.nth((l, g)))
                for i in range(5):
                    x_ = q1[:, i, 0:SEQ] if i < 4 else k1[:, 0:SEQ]
                    dve.wait_ge(s_rot.sem, s_rot.at((l, i)))
                    step(V.tensor_tensor(tmp_p[:, i % 2, 0:SEQ], ps[:, 6 + i % 2, :], sin1[:], ALU.mult))
                    step(V.tensor_tensor(x_, x_, cos1[:], ALU.mult))
                    V.tensor_tensor(x_, x_, tmp_p[:, i % 2, 0:SEQ], ALU.add).then_inc(s_roped.sem, s_roped.nth((l, i)))
                n_fm = 6 + 6
                for c in range(2):
                    for part in range(parts):
                        b, n, a = (n_fm % 4, SEQ, 0) if part == 0 else (4 + n_fm % 2, CTX, SEQ)
                        dve.wait_ge(s_mm.sem, s_mm.at((l, ("cc",), c, part)))
                        dve.wait_ge(s_proj.sem, s_proj.at((l, ("zc",), c, part)))
                        V.tensor_tensor(cz[:, c, a:a + n], ps[:, b, 0:n], cz[:, c, a:a + n], ALU.mult).then_inc(s_conv_t.sem, s_conv_t.nth((l, ("cc",), c, part)))
                    n_fm += 1
                for c in range(2):
                    dve.wait_ge(s_proj.sem, s_proj.at((l, ("gc",), c, parts - 1)))
                    V.tensor_tensor(cb[:, c, 0:nc_], cb[:, c, 0:nc_], tmp_p[:, c, 0:nc_], ALU.mult).then_inc(s_conv_gate.sem, s_conv_gate.nth((l, c)))
                dve.wait_ge(s_conv_gate.sem, s_conv_gate.at((l, 1)))
                dve.wait_ge(s_mm.sem, s_mm.at((l, ("ga", 1), 1, parts - 1)))
                cw, bias = VB[l]["conv_w"], VB[l]["conv_b"]
                for c in range(2):
                    tap = [vec_t[:, cw + 2 * j + c:cw + 2 * j + c + 1] for j in range(3)]
                    for part in range(parts):
                        a, n = (0, SEQ) if part == 0 else (SEQ, CTX)
                        z, o = cz[:, c, a:a + n], conv_y[:, c, a:a + n]
                        step(V.tensor_scalar(o, z, tap[1], vec_t[:, bias + c:bias + c + 1], ALU.mult, ALU.add))
                        step(V.scalar_tensor_tensor(o[:, 1:n], z[:, 0:n - 1], tap[0], o[:, 1:n], ALU.mult, ALU.add))
                        step(V.scalar_tensor_tensor(o[:, 0:n - 1], z[:, 1:n], tap[2], o[:, 0:n - 1], ALU.mult, ALU.add))
                    V.tensor_tensor(cb[:, c, 0:nc_], cb[:, c, 0:nc_], conv_y[:, c, 0:nc_], ALU.mult).then_inc(s_side.sem, s_side.nth((l, 2 + c)))
                dve.wait_ge(s_k_hi.sem, s_k_hi.at((l, KVH - 1)))
                for g in range(KVH):
                    k_ = k1[HD * g:HD * g + HD, :]
                    V.tensor_tensor(k1_lo[HD * g:HD * g + HD, :], k_, k_twice[HD * g:HD * g + HD, g, :].bitcast(F32),
                                    ALU.subtract).then_inc(s_k_lo.sem, s_k_lo.nth((l, g)))

                def q_lo(h):
                    b = HD * (h // 4)
                    dve.wait_ge(s_q_hi.sem, s_q_hi.at((l, h)))
                    V.tensor_tensor(q_parts[HD - b:2 * HD - b, h % 2, 0:nc_], q1[b:b + HD, h % 4, 0:nc_],
                                    q_parts[b:b + HD, h % 2, 0:nc_].bitcast(F32), ALU.subtract).then_inc(s_q_lo.sem, s_q_lo.nth((l, h)))

                q_lo(0)
                q_lo(1)
                for c in range(2):
                    for part in range(parts):
                        b, n, a = (6 + c, SEQ, 0) if part == 0 else (4 + c, CTX, SEQ)
                        dve.wait_ge(s_fmix.sem, s_fmix.at((l, c, part)))
                        V.tensor_tensor(gf[:, c, a:a + n], ps[:, b, 0:n], gf[:, c, a:a + n], ALU.mult).then_inc(s_side.sem, s_side.nth((l, c)))
                
                n_q = len(units1(l)) // HEADS

                def side_lo(st):
                    if st > 0 and st % n_q == 0 and st // n_q + 1 < HEADS:
                        q_lo(st // n_q + 1)
                    c = st - 1
                    if 0 <= c < 4:
                        src = gf[:, c, 0:nc_] if c < 2 else cb[:, c - 2, 0:nc_]
                        lo_part(h_lo[:, 4 + c, 0:nc_], src, h_hi[:, 4 + c, 0:nc_], (l, "s", c), (l, "s", c))

                attend(l, units1(l), side_lo)
                for t in range(nt + 1):
                    if t < nt:
                        dve.wait_ge(s_aot.sem, s_aot.at((l, t)))
                        if t >= 2:
                            dve.wait_ge(s_lo.sem, s_lo.at((l, "m", t - 2)))
                        V.tensor_tensor(tmp_m[:, t % 2, :].rearrange("p (c n) -> p c n", c=4),
                                              ps[:, 6, :].rearrange("p (c n) -> p c n", c=4), ga[:, :, P * t:P * t + P], ALU.mult).then_inc(s_gated.sem, s_gated.nth((l, t)))
                    if t > 0:
                        lo_part(h_lo[:, 0:4, P * (t - 1):P * t], tmp_m[:, (t - 1) % 2, :].rearrange("p (c n) -> p c n", c=4),
                                h_hi[:, 0:4, P * (t - 1):P * t], (l, "m", t - 1), (l, "m", t - 1))
                if l + 1 < DEPTH:
                    mods_out(l + 1, 0, 16, (l + 1, 0))
                    scale_and_shift(l + 1)
                mods_out(l, 16, 24, (l, 1))
                dve.wait_ge(s_lo.sem, s_lo.at((l, "m", nt - 1)))
                for s in range(parts):
                    step(V.tensor_tensor(mod_g[:, s, :], mod[:, s, 16:24], vec_t[:, VB[l]["g_post"]:VB[l]["g_post"] + KD], ALU.mult))
                    for c in range(KD):
                        m = V.tensor_scalar(diag[:, s, c, :], ident[:], mod_g[:, s, c:c + 1], None, ALU.mult).then_inc(s_diag.sem, s_diag.nth((l, s)))
                for st in range(nt + 3):
                    t = st
                    if t < nt:
                        dve.wait_ge(s_ssq.sem, s_ssq.at((l, "post", t)))
                        V.tensor_scalar(ssq[:, t:t + 1], ssq[:, t:t + 1], 1.0 / D, EPS, ALU.mult, ALU.add).then_inc(s_var.sem, s_var.nth((l, "post", t)))
                    t = st - 1
                    if not both and t == nt - 1:
                        lo_rows(DEPTH, "t", 0)
                    if 0 <= t < nt:
                        s = 0 if t < XT else 1
                        x_ = res[:, t, :] if t < XT else res_c[:, t - XT, :]
                        inverse((l, "post", t), t, 1)
                        dve.wait_ge(s_gate_b.sem, s_gate_b.at((l, s)))
                        V.scalar_tensor_tensor(y1[:, t, :], y1[:, t, :], rstd[:, t:t + 1], gate_b[:, s, :],
                                               ALU.mult, ALU.mult).then_inc(s_y_gated.sem, s_y_gated.nth((l, t)))
                        if not both or t == nt - 1:
                            dve.wait_ge(s_y_gated.sem, s_y_gated.at((l, t)))
                            if both:
                                dve.wait_ge(s_x_final.sem, s_x_final.at((l, t - 1)))
                            V.tensor_tensor(x_, x_, y1[:, t, :], ALU.add).then_inc(s_x_final.sem, s_x_final.nth((l, t)))
                    t = st - 2
                    if both and 0 <= t < NT:
                        pre_var(l + 1, t)
                    t = st - 3
                    if both and t >= 0:
                        pre_norm(l + 1, t)

            for l in range(DEPTH):
                y = DEPTH + l
                if y == DEPTH:
                    for t in range(1, XT):
                        lo_rows(y, "t", t)
                dve.wait_ge(s_layer_consts.sem, s_layer_consts.at(y))
                for i in range(2):
                    m = V.tensor_tensor_reduce(dlam[:, 64 * i:64 * i + 32], dlam[:, 64 * i:64 * i + 32], dlam[:, 64 * i + 32:64 * i + 64],
                                               1.0, 0.0, ALU.mult, ALU.add, lam[:, i:i + 1])
                    if i == 0:
                        step(m)
                m.then_inc(s_lam_sums.sem, s_lam_sums.nth(y))
                dve.wait_ge(s_lam_exp.sem, s_lam_exp.at(y))
                step(V.scalar_tensor_tensor(lam[:, 4:5], lam[:, 3:4], lam[:, 2:3], lam_c[:, 0:1], ALU.subtract, ALU.add))
                dve.wait_ge(s_ssq.sem, s_ssq.at((y, "c", 7)))
                step(V.tensor_scalar(ssq[:, 0:4], ssq[:, 0:4], 1.0 / 256, EPS, ALU.mult, ALU.add))
                V.tensor_scalar(ssq[:, 4:8], ssq[:, 4:8], 1.0 / 128, EPS, ALU.mult, ALU.add).then_inc(s_var.sem, s_var.nth((y, "c")))
                inverse((y, "c"), 0, 8)
                for t in range(XT):
                    step(V.tensor_scalar(c_in[:, t, 0:256], c_in[:, t, 0:256], rstd[:, t:t + 1], None, ALU.mult))
                    V.tensor_scalar(c_in[:, t, 256:384], c_in[:, t, 256:384], rstd[:, 4 + t:5 + t], None, ALU.mult).then_inc(s_latn.sem, s_latn.nth((y, t)))
                for i in range(3):
                    dve.wait_ge(s_lat_t.sem, s_lat_t.at((y, i)))
                    gain = LG + 2 * l + i if i < 2 else LG + 4 + l
                    V.tensor_scalar(tmp_c[:, i % 2, :], ps[:, i, :], vec_t[:, gain:gain + 1], None, ALU.mult).then_inc(s_lat.sem, s_lat.nth((y, i)))
                    dve.wait_ge(s_lat.sem, s_lat.at((y, i)))
                    hi, lo = (cq_hi[:, i, :], cq_lo[:, i, :]) if i < 2 else (ckv_hi[:], ckv_lo[:])
                    lo_part(lo, tmp_c[:, i % 2, :], hi, (y, "c", i), (y, "c", i))
                dve.wait_ge(s_lo.sem, s_lo.at((y, "c", 2)))
                R = slice(HD, QC)

                def rope(x_, bank, slot):
                    step(V.tensor_tensor(tmp_c[R, slot, :], ps[R, bank, :], sin2[R, :], ALU.mult))
                    step(V.tensor_tensor(x_, x_, cos2[R, :], ALU.mult))
                    return V.tensor_tensor(x_, x_, tmp_c[R, slot, :], ALU.add)

                dve.wait_ge(s_lat_t.sem, s_lat_t.at((y, 3)))
                V.tensor_copy(kc[R, 0, :], ps[R, 3, :]).then_inc(s_kr_raw.sem, s_kr_raw.nth(y))
                dve.wait_ge(s_kr_rot.sem, s_kr_rot.at(y))
                step(rope(kc[R, 0, :], 5, 0))
                for h in range(1, C_HEADS):
                    m = V.tensor_copy(kc[R, h, :], kc[R, 0, :]).then_inc(s_kr_all.sem, s_kr_all.nth(y))
                for h in range(C_HEADS):
                    dve.wait_ge(s_q_rot.sem, s_q_rot.at((y, h)))
                    rope(qc[R, h, :], 6 + h % 2, h % 2).then_inc(s_roped.sem, s_roped.nth((y, h)))
                dve.wait_ge(s_strips.sem, s_strips.at(y))

                def sub_norm(st):
                    o = ao_b[:].rearrange("p t (h d) -> p t h d", d=HD)
                    sq = sq_b[:].rearrange("p (t h) d -> p t h d", t=XT)
                    if st == LAST_PAIR + 7:
                        dve.wait_ge(s_o_out.sem, s_o_out.at((y, units2()[LAST_PAIR]["rank"])))
                        step(V.tensor_tensor(sq, o, o, ALU.mult))
                    if st == LAST_PAIR + 8:
                        step(V.tensor_reduce(ssq[:, 0:16], sq_b[:], AX_X, ALU.add))
                        V.tensor_scalar(ssq[:, 0:16], ssq[:, 0:16], 1.0 / HD, 1e-5, ALU.mult, ALU.add).then_inc(s_var.sem, s_var.nth((y, "sub")))
                    if st == LAST_PAIR + 11:
                        inverse((y, "sub"), 0, 16)
                        step(V.tensor_scalar(rstd[:, 0:16], rstd[:, 0:16], lam_c[:, 1:2], None, ALU.mult))
                        r = rstd[:, 0:16].rearrange("p (t h) -> p t h", t=XT).unsqueeze(3).broadcast_to((P, XT, B_HEADS, HD))
                        step(V.tensor_tensor(o, o, r, ALU.mult))
                    if st == LAST_PAIR + 12:
                        g = subln[:].unsqueeze(1).unsqueeze(1).broadcast_to((P, XT, B_HEADS, HD))
                        V.tensor_tensor(o, o, g, ALU.mult).then_inc(s_sub.sem, s_sub.nth(y))
                    if 0 <= st - LATENT_SPLIT - 1 < 3:
                        k = 5 + st - LATENT_SPLIT - 1
                        lo_part(g_lo[:, k, :], ao_fm[:, k - 2, :], g_hi[:, k, :], (y, "m", k), (y, "m", k))

                attend(y, units2(), sub_norm)
                for k in HEAD_CHUNKS:
                    src = ps[:, k - 3, :] if 3 <= k < 5 else ao_fm[:, k if k < 3 else k - 2, :]
                    lo_part(g_lo[:, k, :], src, g_hi[:, k, :], (y, "m", k), (y, "m", k))

                def residual(n, ch, t, key, bank):
                    dve.wait_ge(s_mm.sem, s_mm.at(key))
                    x_ = res[:, t, 512 * ch:512 * ch + 512]
                    V.scalar_tensor_tensor(x_, x_, ALPHA, ps[:, bank, :], ALU.mult, ALU.add).then_inc(s_resid.sem, s_resid.nth((y, n, ch, t)))
                    dve.wait_ge(s_resid.sem, s_resid.at((y, n, ch, t)))
                    step(V.bn_stats(bn[:, t, ch, :], x_))

                def statistics(n, t):
                    step(V.bn_aggr(mean_var[:, t, :], bn[:, t, :, :].rearrange("p c s -> p (c s)")))
                    V.tensor_scalar(ssq[:, t:t + 1], mean_var[:, t, 1:2], LN_EPS, None, ALU.add).then_inc(s_var.sem, s_var.nth((y, n, t)))

                def norm(n, w, done, t):
                    inverse((y, n, t), t, 1)
                    dve.wait_ge(s_ln.sem, s_ln.at((y, n)))
                    step(V.scalar_tensor_tensor(res[:, t, :], res[:, t, :], mean_var[:, t, 0:1], w[:, 0, :], ALU.subtract, ALU.mult))
                    V.scalar_tensor_tensor(res[:, t, :], res[:, t, :], rstd[:, t:t + 1], w[:, 1, :], ALU.mult, ALU.add).then_inc(done.sem, done.nth((y, t)))

                for t in range(XT):
                    residual(1, 0, t, (y, "o", 0, t), 4 + t)
                for t in range(XT):
                    residual(1, 1, t, (y, "o", 1, t), 4 + t)
                    statistics(1, t)
                    if t == XT - 1:
                        lo_rows(y, "h", 1)
                    norm(1, ln1, s_normed, t)
                    if t == 2:
                        lo_rows(y, "h", 0)
                for t in (2, 3):
                    lo_rows(y, "h", t)
                for j in range(FC):
                    dve.wait_ge(s_silu.sem, s_silu.at((y, j)))
                    dve.wait_ge(s_mm.sem, s_mm.at((y, "ffup", j)))
                    V.tensor_tensor(tmp_f[:, 2 + j % 2, :], ps[:, 2 * ((j + 2) % 4) + 1, :], tmp_f[:, j % 2, :], ALU.mult).then_inc(s_glu.sem, s_glu.nth((y, j)))
                    dve.wait_ge(s_glu.sem, s_glu.at((y, j)))
                    lo_part(hid_lo[:, j, :], tmp_f[:, 2 + j % 2, :], hid_hi[:, j, :], (y, "f", j), (y, "f", j))
                for t in range(XT):
                    for ch in range(2):
                        residual(2, ch, t, (y, "down", FC // 2 - 1, ch, t), 2 * t + ch)
                    statistics(2, t)
                    if t == XT - 1 and l + 1 < DEPTH:
                        lo_rows(y + 1, "t", 1)
                    norm(2, ln2, s_x_final, t)
                    if t == 2 and l + 1 < DEPTH:
                        lo_rows(y + 1, "t", 0)
                if l + 1 < DEPTH:
                    for t in (2, 3):
                        lo_rows(y + 1, "t", t)


_INS = ["x", "c", "ctx", "c_ctx", "w_mod", "b_mod", "g_pre", "g_post", "w_in", "w_out", "sink", "w_fourier",
        "conv_w", "conv_b", "rel_bias_2", "w_in_2", "q_norm_g_2", "kv_norm_g_2", "w_uq_2", "w_ukv_2",
        "diff_lambda_2", "subln_g_2", "w_o_2", "ln1_g_2", "ln1_b_2", "ln2_g_2", "ln2_b_2", "w_gate_2", "w_up_2", "w_down_2"]


def kernel(**inputs):
    import concourse.bacc as bacc
    from concourse.bass_utils import run_bass_kernel_spmd

    arrays = {f"in_{n}": np.ascontiguousarray(inputs[n]) for n in _INS}
    arrays.update({f"in_{n}": np.ascontiguousarray(a) for n, a in _constants().items()})
    seen = {}
    for _ in range(2):
        nc = bacc.Bacc("TRN2", target_bir_lowering=False, num_devices=1)
        aps = {n[3:]: nc.dram_tensor(n, a.shape, F32, kind="ExternalInput").ap() for n, a in arrays.items()}
        y = nc.dram_tensor("y", (1, SEQ, D), F32, kind="ExternalOutput").ap()
        _program(nc, aps, y, seen)
    return run_bass_kernel_spmd(nc, [arrays], core_ids=[0]).results[0]["y"]
```
